# Optimizing a Trainium2 kernel written in Bass

```python
import jax, jax.numpy as jnp
from jax import lax
import numpy as np

D_MODEL = 1024
BATCH = 1
SEQ = 512
DEPTH = 2

N_MEM = 256
EPS = 1e-6
D_MIX = D_MODEL
MLA_HEADS = 8
MLA_NOPE = 64
MLA_ROPE = 32
MLA_V = 64
Q_LORA = 256
KV_LORA = 128
ROPE_THETA = 10000.0
Q_BLOCK = 128
MLA_WIDTH = MLA_HEADS * MLA_V
SG_HEADS = 8
SG_WIDTH = D_MIX - MLA_WIDTH
SG_HEAD_DIM = SG_WIDTH // SG_HEADS
CHUNK = 128
MEM_HEADS = 4
MEM_HEAD_DIM = D_MODEL // MEM_HEADS
D_FF = 2816
CONV_W = 3
IN_COLS = Q_LORA + KV_LORA + MLA_ROPE + 2 * SG_WIDTH

kernel_name = "hybrid_mla_gmlp_memory_convffn_encoder"

def rmsnorm(x, g):
    xf = x.astype(jnp.float32)
    y = xf * lax.rsqrt(jnp.mean(xf * xf, axis=-1, keepdims=True) + EPS)
    return (y * g.astype(jnp.float32)).astype(x.dtype)

def layernorm(x, g, b):
    xf = x.astype(jnp.float32)
    mu = jnp.mean(xf, axis=-1, keepdims=True)
    xc = xf - mu
    var = jnp.mean(xc * xc, axis=-1, keepdims=True)
    y = xc * lax.rsqrt(var + EPS) * g.astype(jnp.float32) + b.astype(jnp.float32)
    return y.astype(x.dtype)

def rope_tables(positions):
    half = MLA_ROPE // 2
    inv_freq = ROPE_THETA ** (-jnp.arange(half, dtype=jnp.float32) / half)
    ang = positions.astype(jnp.float32)[..., None] * inv_freq
    return jnp.cos(ang), jnp.sin(ang)

def apply_rope(x, cos, sin):
    x1, x2 = jnp.split(x, 2, axis=-1)
    c = cos.astype(x.dtype)
    s = sin.astype(x.dtype)
    return jnp.concatenate([x1 * c - x2 * s, x2 * c + x1 * s], axis=-1)

def mla_mixer(h_q, h_kv, k_pe, cos, sin, q_norm_g, w_uq, kv_norm_g, w_ukv):
    B, S, _ = h_q.shape
    q = (rmsnorm(h_q, q_norm_g) @ w_uq).reshape(B, S, MLA_HEADS, MLA_NOPE + MLA_ROPE)
    q_nope = q[..., :MLA_NOPE]
    q_pe = apply_rope(q[..., MLA_NOPE:], cos[:, :, None, :], sin[:, :, None, :])
    kv = (rmsnorm(h_kv, kv_norm_g) @ w_ukv).reshape(B, S, MLA_HEADS, MLA_NOPE + MLA_V)
    k_nope = kv[..., :MLA_NOPE]
    v = kv[..., MLA_NOPE:]
    k_pe = apply_rope(k_pe, cos, sin)
    scale = (MLA_NOPE + MLA_ROPE) ** -0.5
    nb = S // Q_BLOCK
    qn_blk = q_nope.reshape(B, nb, Q_BLOCK, MLA_HEADS, MLA_NOPE).transpose(1, 0, 2, 3, 4)
    qp_blk = q_pe.reshape(B, nb, Q_BLOCK, MLA_HEADS, MLA_ROPE).transpose(1, 0, 2, 3, 4)

    def attend(blk):
        qn, qp = blk
        s = (jnp.einsum('bqhd,bkhd->bhqk', qn, k_nope)
             + jnp.einsum('bqhr,bkr->bhqk', qp, k_pe))
        p = jax.nn.softmax(s.astype(jnp.float32) * scale, axis=-1).astype(v.dtype)
        return jnp.einsum('bhqk,bkhd->bqhd', p, v)

    o = lax.map(attend, (qn_blk, qp_blk))
    return o.transpose(1, 0, 2, 3, 4).reshape(B, S, MLA_WIDTH)

def spatial_gating_mixer(h_sg, ln_g, ln_b, w_s, b_s):
    B, S, _ = h_sg.shape
    z = jax.nn.gelu(h_sg)
    u, v = z[..., :SG_WIDTH], z[..., SG_WIDTH:]
    v = layernorm(v, ln_g, ln_b)
    nc = S // CHUNK
    v = v.reshape(B, nc, CHUNK, SG_HEADS, SG_HEAD_DIM)
    mixed = (jnp.einsum('hij,bcjhd->bcihd', w_s, v)
             + b_s.T[None, None, :, :, None])
    return u * mixed.reshape(B, S, SG_WIDTH)

def memory_attention(h, mem_h, w_mq, w_mkv, w_mo):
    B, S, _ = h.shape
    q = (h @ w_mq).reshape(B, S, MEM_HEADS, MEM_HEAD_DIM)
    kv = (mem_h @ w_mkv).reshape(B, -1, 2, MEM_HEADS, MEM_HEAD_DIM)
    k, v = kv[:, :, 0], kv[:, :, 1]
    s = jnp.einsum('bqhd,bmhd->bhqm', q, k).astype(jnp.float32) * (MEM_HEAD_DIM ** -0.5)
    p = jax.nn.softmax(s, axis=-1).astype(v.dtype)
    o = jnp.einsum('bhqm,bmhd->bqhd', p, v).reshape(B, S, D_MODEL)
    return o @ w_mo

def conv_ffn(h, w_up, conv_w, conv_b, w_down):
    S = h.shape[1]
    a = h @ w_up
    pad = CONV_W // 2
    ap = jnp.pad(a, ((0, 0), (pad, pad), (0, 0)))
    a = sum(ap[:, k:k + S] * conv_w[k] for k in range(CONV_W)) + conv_b
    g, up = jnp.split(a, 2, axis=-1)
    return (jax.nn.silu(g) * up) @ w_down

def setup_inputs(seed: int = 0) -> dict:
    key = jax.random.key(seed)
    ks = jax.random.split(key, 32)

    def nrm(k, shape, scale):
        return jax.random.normal(k, shape, jnp.float32) * scale

    def gain(k, shape):
        return 1.0 + 0.02 * jax.random.normal(k, shape, jnp.float32)

    L = DEPTH
    x = nrm(ks[0], (BATCH, SEQ, D_MODEL), 1.0)
    mem = nrm(ks[1], (BATCH, N_MEM, D_MODEL), 1.0)
    positions = (jnp.arange(SEQ, dtype=jnp.int32)[None, :]
                 + jax.random.randint(ks[2], (BATCH, 1), 0, 4096, dtype=jnp.int32))
    return {
        "x": x,
        "mem": mem,
        "positions": positions,
        "norm_mix_g": gain(ks[3], (L, D_MODEL)),
        "w_in": nrm(ks[4], (L, D_MODEL, IN_COLS), D_MODEL ** -0.5),
        "q_norm_g": gain(ks[5], (L, Q_LORA)),
        "w_uq": nrm(ks[6], (L, Q_LORA, MLA_HEADS * (MLA_NOPE + MLA_ROPE)), Q_LORA ** -0.5),
        "kv_norm_g": gain(ks[7], (L, KV_LORA)),
        "w_ukv": nrm(ks[8], (L, KV_LORA, MLA_HEADS * (MLA_NOPE + MLA_V)), KV_LORA ** -0.5),
        "sg_ln_g": gain(ks[9], (L, SG_WIDTH)),
        "sg_ln_b": nrm(ks[10], (L, SG_WIDTH), 0.02),
        "sg_w_s": nrm(ks[11], (L, SG_HEADS, CHUNK, CHUNK), 0.5 * CHUNK ** -0.5),
        "sg_b_s": gain(ks[12], (L, SG_HEADS, CHUNK)),
        "out_norm_mla_g": gain(ks[13], (L, MLA_WIDTH)),
        "out_norm_sg_g": gain(ks[14], (L, SG_WIDTH)),
        "w_out": nrm(ks[15], (L, D_MIX, D_MODEL), D_MIX ** -0.5),
        "norm_mem_g": gain(ks[16], (L, D_MODEL)),
        "mem_norm_g": gain(ks[17], (L, D_MODEL)),
        "w_mq": nrm(ks[18], (L, D_MODEL, D_MODEL), D_MODEL ** -0.5),
        "w_mkv": nrm(ks[19], (L, D_MODEL, 2 * D_MODEL), D_MODEL ** -0.5),
        "w_mo": nrm(ks[20], (L, D_MODEL, D_MODEL), D_MODEL ** -0.5),
        "norm_ffn_g": gain(ks[21], (L, D_MODEL)),
        "w_up": nrm(ks[22], (L, D_MODEL, 2 * D_FF), D_MODEL ** -0.5),
        "conv_w": nrm(ks[23], (L, CONV_W, 2 * D_FF), CONV_W ** -0.5),
        "conv_b": nrm(ks[24], (L, 2 * D_FF), 0.02),
        "w_down": nrm(ks[25], (L, D_FF, D_MODEL), D_FF ** -0.5),
        "final_norm_g": gain(ks[26], (D_MODEL,)),
    }

def reference(x, mem, positions, norm_mix_g, w_in, q_norm_g, w_uq, kv_norm_g, w_ukv,
              sg_ln_g, sg_ln_b, sg_w_s, sg_b_s, out_norm_mla_g, out_norm_sg_g, w_out,
              norm_mem_g, mem_norm_g, w_mq, w_mkv, w_mo, norm_ffn_g, w_up, conv_w,
              conv_b, w_down, final_norm_g):
    cos, sin = rope_tables(positions)
    c1 = Q_LORA
    c2 = c1 + KV_LORA
    c3 = c2 + MLA_ROPE
    for l in range(DEPTH):
        h = rmsnorm(x, norm_mix_g[l])
        proj = h @ w_in[l]
        h_q, h_kv, k_pe, h_sg = proj[..., :c1], proj[..., c1:c2], proj[..., c2:c3], proj[..., c3:]
        o_mla = mla_mixer(h_q, h_kv, k_pe, cos, sin, q_norm_g[l], w_uq[l], kv_norm_g[l], w_ukv[l])
        o_sg = spatial_gating_mixer(h_sg, sg_ln_g[l], sg_ln_b[l], sg_w_s[l], sg_b_s[l])
        o = jnp.concatenate([rmsnorm(o_mla, out_norm_mla_g[l]),
                             rmsnorm(o_sg, out_norm_sg_g[l])], axis=-1)
        x = x + o @ w_out[l]
        h = rmsnorm(x, norm_mem_g[l])
        m = rmsnorm(mem, mem_norm_g[l])
        x = x + memory_attention(h, m, w_mq[l], w_mkv[l], w_mo[l])
        h = rmsnorm(x, norm_ffn_g[l])
        x = x + conv_ffn(h, w_up[l], conv_w[l], conv_b[l], w_down[l])
    return rmsnorm(x, final_norm_g)


_drawn_inputs = setup_inputs


def setup_inputs(seed=0):
    import zlib

    import numpy as np

    out = dict(_drawn_inputs(seed))
    spreads = {}
    factors = {'q_norm_g': 5.062,
     'sg_ln_g': 8.0,
     'sg_ln_b': 8.0,
     'sg_b_s': 4.974,
     'out_norm_mla_g': 3.748,
     'out_norm_sg_g': 3.893,
     'norm_mem_g': 8.0,
     'mem_norm_g': 8.0,
     'norm_ffn_g': 3.752,
     'conv_b': 3.656,
     'final_norm_g': 2.814}
    for name, (base, spread) in spreads.items():
        noise = np.random.default_rng([zlib.crc32(name.encode()), seed]).standard_normal(out[name].shape)
        drawn = base * np.exp(spread * noise) if base else spread * noise
        out[name] = __import__('jax').numpy.asarray(drawn.astype(out[name].dtype))
    for name, factor in factors.items():
        out[name] = (out[name] * factor).astype(out[name].dtype)
    return out
```

```python
import numpy as np
from contextlib import ExitStack

import concourse.bass as bass
from concourse import mybir

F32 = mybir.dt.float32
F32R = mybir.dt.float32r
I32 = mybir.dt.int32
ALU = mybir.AluOpType
ACT = mybir.ActivationFunctionType
AXX = mybir.AxisListType.X

P = 128
DEPTH, SEQ, D, N_MEM = 2, 512, 1024, 256
KD = D // P
TT = SEQ // P
EPS = 1e-6
HEADS, NOPE, ROPE, VD = 8, 64, 32, 64
QK = NOPE + ROPE
Q_LORA, KV_LORA = 256, 128
SG, SG_HEADS, SG_HD = 512, 8, 64
MEM_HEADS, MEM_HD = 4, 256
MT = N_MEM // P
D_FF = 2816
FT = D_FF // P
SCALE = float(QK) ** -0.5
MEM_SCALE = float(MEM_HD) ** -0.5

BLK = 1024
RAW, SPLIT = 2, 4
AHEAD = 3
B_LAT = 0
B_U = B_LAT + 4
B_V = B_U + 4
B_WV = B_V + 4
B_HEAD = B_WV + 1
B_WS = B_HEAD + HEADS // 2
B_OUT = B_WS + 1
B_MK = B_OUT + 8
B_MV = B_MK + 8
B_MQ = B_MV + 8
B_MO = B_MQ + 8
B_UP = (B_MO + 8, B_MO + 8 + 24 + 12)
B_DN = (B_UP[0] + 24, B_UP[1] + 20)
GROUPS = (6, 5)
BLOCKS = B_DN[1] + 10
assert BLOCKS % SPLIT == 0

MIX, NQ, NKV, MLA, MTOK, MEM, FFN = range(7)
NORM_TILES = (8, 2, 1, 4, 8, 8, 8)
NORM_DIM = (D, Q_LORA, KV_LORA, HEADS * VD, D, D, D)
NORM_COLS = (SEQ, SEQ, SEQ, SEQ, N_MEM, SEQ, SEQ)
N_NORMS = len(NORM_TILES)
TILE0 = tuple(sum(NORM_TILES[:m]) for m in range(N_NORMS + 1))
ADD0 = tuple(sum(n - 1 for n in NORM_TILES[:m]) for m in range(N_NORMS + 1))

G_MIX, G_Q, G_KV, G_MLA, G_SG, G_MTOK, G_MEM, G_FFN = 0, 8, 10, 11, 15, 19, 27, 35
C_BS = 43
C_W0, C_W1, C_W2, C_B = 51, 95, 139, 183
NPAR = 227
GAIN = (G_MIX, G_Q, G_KV, G_MLA, G_MTOK, G_MEM, G_FFN)

TWO_PI = 2 * np.pi
PI_A = 6.28125
PI_B = float(np.float32(np.round((TWO_PI - PI_A) * 2 ** 20) / 2 ** 20))
PI_C = float(np.float32(TWO_PI - PI_A - PI_B))
ROUND = 1.5 * 2.0 ** 23
PI_IN = 3.1415925


class Signal:

    def __init__(self, ctx, nc, name, per_layer, start=0):
        self.sem = ctx.enter_context(nc.semaphore(name))
        self.per_layer, self.start = per_layer, start

    def at(self, layer, n):
        return layer * self.per_layer + (n + self.start)


def encoder_program(nc, blocks_d, xT_d, memT_d, pos_d, par_d, ln_d, fin_d, freq_d, out_d):
    with ExitStack() as ctx:
        def sb(name, shape, dt=F32):
            return ctx.enter_context(nc.sbuf_tensor(name, shape, dt))

        def sig(name, per_layer, start=0):
            return Signal(ctx, nc, name, per_layer, start)

        x = sb("x", [P, KD, SEQ])
        h_hi = sb("h_hi", [P, KD, SEQ], F32R)
        h_lo = sb("h_lo", [P, KD, SEQ], F32R)
        raw = sb("raw", [P, RAW, BLK])
        w_hi = sb("w_hi", [P, SPLIT, BLK], F32R)
        w_lo = sb("w_lo", [P, SPLIT, BLK], F32R)
        arena = sb("arena", [P, 40, SEQ], F32R)
        work = sb("work", [P, 14, SEQ])
        trig = sb("trig", [P, 2, SEQ])
        ln_gb = sb("ln_gb", [P, 2, SG])
        par = sb("par", [P, NPAR])
        fin_g = sb("fin_g", [P, KD])
        freq = sb("freq", [P, 2])
        ones = sb("ones", [P, P])
        ident = sb("ident", [P, P])
        small = sb("small", [P, 64])

        q_hi, q_lo, k_hi, k_lo = (arena[:, 2 * i:2 * i + 2, :] for i in range(4))
        v_hi, v_lo = arena[:, 8:12, :], arena[:, 12:16, :]
        pt_hi, pt_lo = arena[:, 16:20, :], arena[:, 20:24, :]
        sv_hi, sv_lo = arena[:, 24:28, :], arena[:, 28:32, :]
        cq_hi, cq_lo = arena[:, 32:34, :], arena[:, 34:36, :]
        ckv_hi, ckv_lo = arena[:, 36:37, :], arena[:, 37:38, :]
        km_hi = arena[:, 0:4, :].rearrange("p a (b n) -> p (a b) n", b=2)
        km_lo = arena[:, 4:8, :].rearrange("p a (b n) -> p (a b) n", b=2)
        vm_hi, vm_lo = arena[:, 8:12, :], arena[:, 12:16, :]
        qm_hi, qm_lo = arena[:, 16:24, :], arena[:, 24:32, :]
        mt_hi = arena[:, 32:36, :].rearrange("p a (b n) -> p (a b) n", b=2)
        mt_lo = arena[:, 36:40, :].rearrange("p a (b n) -> p (a b) n", b=2)
        pm_hi, pm_lo = arena[:, 32:34, :], arena[:, 34:36, :]
        hid_hi, hid_lo = arena[:, 0:12, :], arena[:, 12:24, :]
        u = work[:, 0:4, :]
        memT = work[:, 0:4, :].rearrange("p a (b n) -> p (a b) n", b=2)
        lat = work[:, 4:8, :]
        o_mla = work[:, 4:8, :]
        acc, sq, nv, r0, rs = work[:, 8, :], work[:, 9:11, :], work[:, 11, :], work[:, 12, :], work[:, 13, :]
        e = work[:, 8:10, :]
        rot = work[:, 10:13, :]
        vt = work[:, 10:14, :]
        conv = work[:, 0:8, :]
        bn = small[:, 0:24].rearrange("p (a b) -> p a b", a=4)
        mv = small[:, 24:32].rearrange("p (a b) -> p a b", a=4)
        sm_v, sm_r, sm_t = small[:, 32:36], small[:, 36:40], small[:, 40:44]
        mx, nmx, sums, rin = small[:, 44:48], small[:, 48:52], small[:, 52:56], small[:, 56:60]

        ps = [ctx.enter_context(nc.psum_tensor(f"ps{i}", [P, SEQ], F32)) for i in range(8)]
        BA, BB = (0, 1, 2, 3), (4, 5, 6, 7)

        raw_in = [sig(f"raw_in{i}", 16 * BLOCKS // RAW) for i in range(RAW)]
        hi_done = sig("hi_done", BLOCKS)
        lo_done = sig("lo_done", BLOCKS)
        used = sig("used", BLOCKS, SPLIT)
        x_in = ctx.enter_context(nc.semaphore("x_in"))
        const_in = ctx.enter_context(nc.semaphore("const_in"))
        const_done = ctx.enter_context(nc.semaphore("const_done"))
        trig_dve = ctx.enter_context(nc.semaphore("trig_dve"))
        trig_act = ctx.enter_context(nc.semaphore("trig_act"))
        stored = ctx.enter_context(nc.semaphore("stored"))
        par_in = sig("par_in", 32)
        mem_in = sig("mem_in", 16)
        x_ready = sig("x_ready", 32, 8)
        sq_done = sig("sq_done", TILE0[-1])
        add_done = sig("add_done", ADD0[-1])
        ssq_done = sig("ssq_done", N_NORMS)
        nv_done = sig("nv_done", N_NORMS)
        ln_done = sig("ln_done", N_NORMS)
        r0_done = sig("r0_done", N_NORMS)
        y_done = sig("y_done", TILE0[-1])
        nhi_done = sig("nhi_done", TILE0[-1])
        nlo_done = sig("nlo_done", TILE0[-1])
        s_v = sig("s_v", 2)
        s_ln = sig("s_ln", 2)
        s_r0 = sig("s_r0", 2)
        lat_done = sig("lat_done", 4)
        kpe_ready = sig("kpe_ready", 1)
        kpe_hi = sig("kpe_hi", 2)
        u_done = sig("u_done", 4)
        vg_done = sig("vg_done", 4)
        vn_done = sig("vn_done", 4)
        svh_done = sig("svh_done", 4)
        svl_done = sig("svl_done", 4)
        wv_mm = sig("wv_mm", TT - 1)
        vh_done = sig("vh_done", 4)
        vl_done = sig("vl_done", 4)
        qp_mm = sig("qp_mm", HEADS)
        kp_mm = sig("kp_mm", HEADS // 2)
        qh_done = sig("qh_done", HEADS)
        pe_copied = sig("pe_copied", HEADS)
        ql_done = sig("ql_done", HEADS)
        roped = sig("roped", HEADS)
        kh_done = sig("kh_done", HEADS)
        kl_done = sig("kl_done", HEADS)
        peh_done = sig("peh_done", HEADS)
        qk_ready = sig("qk_ready", HEADS)
        score_mm = sig("score_mm", HEADS * TT)
        nmax_done = sig("nmax_done", HEADS * TT)
        exp_done = sig("exp_done", HEADS * TT)
        prob_done = sig("prob_done", HEADS * TT)
        turned = sig("turned", HEADS * TT)
        pth_done = sig("pth_done", HEADS * 4)
        ptl_done = sig("ptl_done", HEADS * 4)
        pv_mm = sig("pv_mm", HEADS)
        o_done = sig("o_done", HEADS)
        mix_mm = sig("mix_mm", SG_HEADS // 2 - 1)
        gated = sig("gated", SG_HEADS)
        sg_normed = sig("sg_normed", 4)
        sg_turned = sig("sg_turned", 4)
        sgh_done = sig("sgh_done", 4)
        sgl_done = sig("sgl_done", 4)
        kmh_done = sig("kmh_done", 8)
        kml_done = sig("kml_done", 8)
        vmh_done = sig("vmh_done", 4)
        vml_done = sig("vml_done", 4)
        qmh_done = sig("qmh_done", 8)
        qml_done = sig("qml_done", 8)
        mscore_mm = sig("mscore_mm", MEM_HEADS * TT)
        mnmax_done = sig("mnmax_done", MEM_HEADS * TT)
        mexp_done = sig("mexp_done", MEM_HEADS * TT)
        mprob_done = sig("mprob_done", MEM_HEADS * TT)
        mturned = sig("mturned", MEM_HEADS * TT)
        pmh_done = sig("pmh_done", MEM_HEADS * MT)
        pml_done = sig("pml_done", MEM_HEADS * MT)
        mpv_mm = sig("mpv_mm", MEM_HEADS * 2)
        omh_done = sig("omh_done", 8)
        oml_done = sig("oml_done", 8)
        tap1 = sig("tap1", 2 * FT)
        taps = sig("taps", 4 * FT, 16)
        silu_done = sig("silu_done", FT)
        prod_done = sig("prod_done", FT)
        fh_done = sig("fh_done", FT)
        fl_done = sig("fl_done", FT)
        dve_passed = ctx.enter_context(nc.semaphore("dve_passed"))
        pe_passed = ctx.enter_context(nc.semaphore("pe_passed"))
        N_STEP = 175
        dve_step = sig("dve_step", N_STEP)

        block = ctx.enter_context(nc.Block())

        @block.sync
        def _(sp):
            sp.dma_start(x[:, :, :], xT_d).then_inc(x_in, 16)
            for n in range(RAW):
                sp.dma_start(raw[:, n, :], blocks_d[n]).then_inc(raw_in[n].sem, 16)
            with sp.Fori(0, DEPTH * BLOCKS // RAW - 1) as i:
                for r in range(RAW):
                    sp.wait_ge(lo_done.sem, i * RAW + (r + 1))
                    sp.dma_start(raw[:, r, :],
                                 blocks_d[bass.ds(i * RAW + (r + RAW), 1), :, :].rearrange("a p n -> (a p) n"))\
                        .then_inc(raw_in[r].sem, 16)
            for t in range(KD):
                sp.wait_ge(nhi_done.sem, nhi_done.at(DEPTH, t + 1))
                sp.dma_start(out_d[:, t, :], conv[:, t, :]).then_inc(stored, 16)
            sp.wait_ge(stored, 16 * KD)

        @block.gpsimd
        def _(gp):
            gp.memset(ones[:, :], 1.0).then_inc(const_done, 1)
            gp.memset(ident[:, :], 0.0).then_inc(const_done, 1)
            gp.wait_ge(const_done, 2)
            gp.affine_select(out=ident[:, :], in_=ident[:, :], compare_op=ALU.not_equal, fill=1.0, base=0,
                             pattern=[[-1, P]], channel_multiplier=1).then_inc(const_done, 1)
            with gp.Fori(0, DEPTH * BLOCKS // SPLIT) as i:
                for r in range(SPLIT):
                    gp.wait_ge(hi_done.sem, i * SPLIT + (r + 1))
                    gp.tensor_tensor(w_lo[:, r, :], raw[:, r % RAW, :], w_hi[:, r, :].bitcast(F32),
                                     ALU.subtract).then_inc(lo_done.sem, 1)

        @block.scalar
        def _(act):
            act.sem_inc(used.sem, SPLIT)
            act.dma_start(work[64:96, 2, :].bitcast(I32), pos_d.to_broadcast([ROPE, SEQ])).then_inc(const_in, 16)
            act.dma_start(freq[:, :], freq_d).then_inc(const_in, 16)
            act.dma_start(fin_g[:, :], fin_d).then_inc(const_in, 16)
            act.wait_ge(trig_dve, 1)
            act.activation(trig[64:96, 1, :], work[64:96, 0, :], ACT.Sin).then_inc(trig_act, 1)
            act.wait_ge(trig_dve, 2)
            act.activation(trig[64:96, 0, :], work[64:96, 1, :], ACT.Sin).then_inc(trig_act, 1)

            def layer(l):
                def need(s, n):
                    act.wait_ge(s.sem, s.at(l, n))

                def split(b, i=0, step=0):
                    r = b % RAW
                    act.wait_ge(raw_in[r].sem,
                                l * (16 * BLOCKS // RAW) + i * (16 * step // RAW) + 16 * (b // RAW + 1))
                    act.wait_ge(used.sem,
                                l * BLOCKS + i * step + (b + 1))
                    act.activation(w_hi[:, b % SPLIT, :], raw[:, r, :], ACT.Copy).then_inc(hi_done.sem, 1)

                def ahead(b, i=0, step=0):
                    if b + AHEAD < BLOCKS:
                        split(b + AHEAD, i, step)

                def block_used(b):
                    need(used, b + 1)

                def squares(m, src, ready, acc_t=acc):
                    n = NORM_COLS[m]
                    for t in range(NORM_TILES[m]):
                        ready(t)
                        if t == 1 and m > 0:
                            need(nlo_done, TILE0[m])
                        if t >= 3:
                            need(add_done, ADD0[m] + t - 2)
                        dst = acc_t if t == 0 else sq[:, (t - 1) % 2, :]
                        act.activation(dst[:, 0:n], src(t), ACT.Square).then_inc(sq_done.sem, 1)

                def root(m):
                    n = NORM_COLS[m]
                    act.preload_act_table_set("natural_log_exp_and_others")
                    need(nv_done, m + 1)
                    act.activation(r0[:, 0:n], nv[:, 0:n], ACT.Ln).then_inc(ln_done.sem, 1)
                    need(ln_done, m + 1)
                    act.activation(r0[:, 0:n], r0[:, 0:n], ACT.Exp, scale=-0.5).then_inc(r0_done.sem, 1)

                def his(m, dst):
                    n = NORM_COLS[m]
                    for t in range(NORM_TILES[m]):
                        need(y_done, TILE0[m] + t + 1)
                        act.activation(dst(t), sq[:, t % 2, 0:n], ACT.Copy,
                                       scale=par[:, GAIN[m] + t:GAIN[m] + t + 1]).then_inc(nhi_done.sem, 1)

                def small_root(i):
                    act.preload_act_table_set("natural_log_exp_and_others")
                    need(s_v, i + 1)
                    act.activation(sm_r, sm_v, ACT.Ln).then_inc(s_ln.sem, 1)
                    need(s_ln, i + 1)
                    act.activation(sm_r, sm_r, ACT.Exp, scale=-0.5).then_inc(s_r0.sem, 1)

                act.dma_start(par[:, :], par_d[bass.ds(l, 1), :, :].rearrange("a p n -> (a p) n"))\
                    .then_inc(par_in.sem, 16)
                act.dma_start(ln_gb[:, :, :].rearrange("p a n -> p (a n)"),
                              ln_d[bass.ds(l, 1), :].to_broadcast([P, 2 * SG])).then_inc(par_in.sem, 16)
                for b in range(AHEAD):
                    split(b)
                squares(MIX, lambda t: x[:, t, :], lambda t: act.wait_ge(x_ready.sem, x_ready.at(l, t + 1 - 8)))
                root(MIX)
                need(par_in, 32)
                his(MIX, lambda t: h_hi[:, t, :])
                for b in range(B_LAT, B_LAT + 4):
                    ahead(b)
                squares(NQ, lambda t: lat[:, t, :], lambda t: need(lat_done, t + 1))
                squares(NKV, lambda t: lat[:, 2, :], lambda t: need(lat_done, 3), acc_t=sq[:, 1, :])
                ahead(B_U)
                ahead(B_U + 1)
                need(kpe_ready, 1)
                for p in range(2):
                    act.activation(k_hi[64:96, p, :], rot[64:96, 2, :], ACT.Copy).then_inc(kpe_hi.sem, 1)
                root(NQ)
                his(NQ, lambda t: cq_hi[:, t, :])
                root(NKV)
                his(NKV, lambda t: ckv_hi[:, t, :])
                ahead(B_U + 2)
                ahead(B_U + 3)
                block_used(B_U + 3)
                for t in range(TT):
                    act.activation(u[:, t, :], ps[BB[t]][:, :], ACT.Gelu_apprx_tanh).then_inc(u_done.sem, 1)
                for b in range(B_V, B_V + 4):
                    ahead(b)
                block_used(B_V + 3)
                for t in range(TT):
                    act.activation(vt[:, t, :], ps[BA[t]][:, :], ACT.Gelu_apprx_tanh).then_inc(vg_done.sem, 1)
                small_root(0)
                ahead(B_WV)
                for t in range(TT):
                    if t < TT - 1:
                        need(wv_mm, t + 1)
                    else:
                        block_used(B_WV)
                    act.activation(v_hi[:, t, :], ps[BB[t]][:, :], ACT.Copy).then_inc(vh_done.sem, 1)
                for t in range(TT):
                    need(vn_done, t + 1)
                    act.activation(sv_hi[:, t, :], vt[:, t, :], ACT.Copy).then_inc(svh_done.sem, 1)

                def q_part(h):
                    need(qp_mm, h + 1)
                    act.activation(q_hi[0:64, h % 2, :], ps[0][0:64, :], ACT.Copy).then_inc(qh_done.sem, 1)
                    act.activation(rot[64:96, 0, :], ps[0][64:96, :], ACT.Copy).then_inc(pe_copied.sem, 1)

                def k_part(h):
                    if h % 2 == 0:
                        need(kp_mm, h // 2 + 1)
                    else:
                        block_used(B_HEAD + h // 2)
                    act.activation(k_hi[0:64, h % 2, :], ps[0][0:64, :], ACT.Copy).then_inc(kh_done.sem, 1)
                    need(roped, h + 1)
                    act.activation(q_hi[64:96, h % 2, :], rot[64:96, 2, :], ACT.Copy).then_inc(peh_done.sem, 1)

                def exps(h, t):
                    i = h * TT + t
                    need(nmax_done, i + 1)
                    if i >= 2:
                        need(turned, i - 1)
                    act.activation(e[:, t % 2, :], ps[2 + t % 2][:, :], ACT.Exp, bias=nmx[:, t:t + 1],
                                   scale=SCALE, accum_out=sums[:, t:t + 1]).then_inc(exp_done.sem, 1)

                act.preload_act_table_set("natural_log_exp_and_others")
                need(svl_done, 4)
                q_part(0)
                k_part(0)
                ahead(B_HEAD)
                q_part(1)
                exps(0, 0)
                exps(0, 1)
                k_part(1)
                for h in range(HEADS):
                    exps(h, 2)
                    exps(h, 3)
                    for t in range(TT):
                        need(turned, TT * h + TT)
                        act.activation(pt_hi[:, t, :], ps[4 + t][:, :], ACT.Copy).then_inc(pth_done.sem, 1)
                    if h + 1 < HEADS:
                        exps(h + 1, 0)
                        exps(h + 1, 1)
                    if h % 2 == 0:
                        ahead(B_HEAD + h // 2 + 1)
                    if h + 2 < HEADS:
                        q_part(h + 2)
                    need(pv_mm, h + 1)
                    act.activation(o_mla[64 * (h % 2):64 * (h % 2) + 64, h // 2, :], ps[1][0:64, :], ACT.Copy)\
                        .then_inc(o_done.sem, 1)
                    if h + 2 < HEADS:
                        k_part(h + 2)
                squares(MLA, lambda t: o_mla[:, t, :], lambda t: need(o_done, 2 * t + 2))
                root(MLA)
                his(MLA, lambda t: h_hi[:, t, :])
                small_root(1)
                for t in range(4):
                    need(sg_turned, 4)
                    act.activation(h_hi[:, 4 + t, :], ps[t][:, :], ACT.Copy,
                                   scale=par[:, G_SG + t:G_SG + t + 1]).then_inc(sgh_done.sem, 1)
                act.dma_start(memT, memT_d).then_inc(mem_in.sem, 16)
                for b in range(B_OUT, B_OUT + 4):
                    ahead(b)
                squares(MTOK, lambda t: memT[:, t, :], lambda t: need(mem_in, 16) if t == 0 else None)
                root(MTOK)
                his(MTOK, lambda t: mt_hi[:, t, :])
                for b in range(B_OUT + 4, B_OUT + 8):
                    ahead(b)
                squares(MEM, lambda t: x[:, t, :], lambda t: need(x_ready, t + 1))
                for b in range(B_MK, B_MK + 4):
                    ahead(b)
                root(MEM)
                his(MEM, lambda t: h_hi[:, t, :])

                def keys(g):
                    block_used(B_MK + 4 * g + 3)
                    for j in range(4):
                        act.activation(km_hi[:, 4 * g + j, :], ps[(BB, BA)[g][j]][:, 0:N_MEM], ACT.Copy)\
                            .then_inc(kmh_done.sem, 1)

                def values(g):
                    block_used(B_MV + 4 * g + 3)
                    for j in range(MT):
                        act.activation(vm_hi[:, 2 * j + g, :], ps[4 + 2 * g + j][:, :], ACT.Copy)\
                            .then_inc(vmh_done.sem, 1)

                def queries(g):
                    block_used(B_MQ + 4 * g + 3)
                    for j in range(4):
                        act.activation(qm_hi[:, 4 * g + j, :], ps[(BA, BB)[g][j]][:, :], ACT.Copy)\
                            .then_inc(qmh_done.sem, 1)

                keys(0)
                for b in range(B_MK + 4, B_MK + 8):
                    ahead(b)
                keys(1)
                for g in range(2):
                    for b in range(B_MV + 4 * g, B_MV + 4 * g + 4):
                        ahead(b)
                    values(g)
                for g in range(2):
                    for b in range(B_MQ + 4 * g, B_MQ + 4 * g + 4):
                        ahead(b)
                    queries(g)

                def mexps(h, t):
                    i = h * TT + t
                    need(mnmax_done, i + 1)
                    if i >= 2:
                        need(mturned, i - 1)
                    act.activation(e[:, t % 2, 0:N_MEM], ps[t % 2][:, 0:N_MEM], ACT.Exp, bias=nmx[:, t:t + 1],
                                   scale=MEM_SCALE, accum_out=sums[:, t:t + 1]).then_inc(mexp_done.sem, 1)

                def outputs(h):
                    for j in range(2):
                        need(mpv_mm, 2 * h + j + 1)
                        act.activation(h_hi[:, 2 * h + j, :], ps[4 + 2 * (h % 2) + j][:, :], ACT.Copy)\
                            .then_inc(omh_done.sem, 1)

                mexps(0, 0)
                mexps(0, 1)
                for h in range(MEM_HEADS):
                    mexps(h, 2)
                    mexps(h, 3)
                    need(mturned, TT * h + TT)
                    for t in range(MT):
                        act.activation(pm_hi[:, t, :], ps[2 + t][:, :], ACT.Copy).then_inc(pmh_done.sem, 1)
                    if h + 1 < MEM_HEADS:
                        mexps(h + 1, 0)
                        mexps(h + 1, 1)
                    outputs(h)
                for b in range(B_MO, B_MO + 8):
                    ahead(b)
                squares(FFN, lambda t: x[:, t, :], lambda t: need(x_ready, 8 + t + 1))
                root(FFN)
                his(FFN, lambda t: h_hi[:, t, :])

                def up_group(half, r, i, step):
                    g = sum(GROUPS[:half]) + r
                    for b in range(B_UP[half] + 4 * r, B_UP[half] + 4 * r + 4):
                        ahead(b, i, 4 * step)
                    act.wait_ge(used.sem, l * BLOCKS + i * (4 * step) + (B_UP[half] + 4 * r + 4 + SPLIT))
                    bank = 4 * (r % 2)
                    for j in range(2):
                        for s in range(2):
                            c = s * FT + 2 * g + j
                            cb = par[:, bass.ds(i * (2 * step) + (C_B + c), 1)] if step else par[:, C_B + c:C_B + c + 1]
                            cw = par[:, bass.ds(i * (2 * step) + (C_W1 + c), 1)] if step else par[:, C_W1 + c:C_W1 + c + 1]
                            act.activation(conv[:, bank + 2 * j + s, :], ps[bank + 2 * s + j][:, :], ACT.Identity,
                                           bias=cb, scale=cw).then_inc(tap1.sem, 1)
                    for j in range(2):
                        act.wait_ge(taps.sem, l * (4 * FT) + i * (8 * step) + (8 * g + 4 * j + 2 + taps.start))
                        cg = conv[:, bank + 2 * j, :]
                        act.activation(cg, cg, ACT.Silu).then_inc(silu_done.sem, 1)
                    for j in range(2):
                        act.wait_ge(prod_done.sem, l * FT + i * (2 * step) + (2 * g + j + 1))
                        dst = hid_hi[:, bass.ds(i * (2 * step) + (2 * r + j), 1), :] if step \
                            else hid_hi[:, 2 * r + j:2 * r + j + 1, :]
                        act.activation(dst, conv[:, bank + 2 * j:bank + 2 * j + 1, :], ACT.Copy).then_inc(fh_done.sem, 1)

                for half in range(2):
                    with act.Fori(0, GROUPS[half] // 2) as i:
                        for r in range(2):
                            up_group(half, r, i, 2)
                    if GROUPS[half] % 2:
                        up_group(half, GROUPS[half] - 1, 0, 0)
                    for b in range(B_DN[half], B_DN[half] + 2 * GROUPS[half]):
                        ahead(b)
                return squares, root, need

            with act.Fori(0, DEPTH) as l:
                layer(l)

            for t in range(KD):
                act.wait_ge(x_ready.sem, x_ready.at(DEPTH, t + 1 - 8))
                if t >= 3:
                    act.wait_ge(add_done.sem, add_done.at(DEPTH, t - 2))
                dst = acc if t == 0 else sq[:, (t - 1) % 2, :]
                act.activation(dst, x[:, t, :], ACT.Square).then_inc(sq_done.sem, 1)
            act.preload_act_table_set("natural_log_exp_and_others")
            act.wait_ge(nv_done.sem, nv_done.at(DEPTH, 1))
            act.activation(r0, nv, ACT.Ln).then_inc(ln_done.sem, 1)
            act.wait_ge(ln_done.sem, ln_done.at(DEPTH, 1))
            act.activation(r0, r0, ACT.Exp, scale=-0.5).then_inc(r0_done.sem, 1)
            act.wait_ge(const_in, 48)
            for t in range(KD):
                act.wait_ge(y_done.sem, y_done.at(DEPTH, t + 1))
                act.activation(conv[:, t, :], sq[:, t % 2, :], ACT.Copy, scale=fin_g[:, t:t + 1])\
                    .then_inc(nhi_done.sem, 1)

        @block.vector
        def _(dve):
            pos_i = work[64:96, 2, :].bitcast(I32)
            pos, ang, kt = work[64:96, 3, :], work[64:96, 4, :], work[64:96, 5, :]
            steps = [0]

            def prep(ins):
                steps[0] += 1
                ins.then_inc(const_done, 1)
                dve.wait_ge(const_done, 3 + steps[0])

            dve.wait_ge(const_in, 48)
            dve.wait_ge(const_done, 3)
            prep(dve.tensor_copy(pos, pos_i))
            prep(dve.tensor_scalar(ang, pos, freq[64:96, 0:1], None, ALU.mult))
            for which, (quarter, out_t) in enumerate(((0.0, work[64:96, 0, :]), (0.25, work[64:96, 1, :]))):
                prep(dve.tensor_scalar(kt, ang, float(1 / TWO_PI), quarter, ALU.mult, ALU.add))
                prep(dve.tensor_scalar(kt, kt, ROUND, None, ALU.add))
                prep(dve.tensor_scalar(kt, kt, ROUND, None, ALU.subtract))
                prep(dve.scalar_tensor_tensor(out=out_t, in0=kt, scalar=-PI_A, in1=ang, op0=ALU.mult, op1=ALU.add))
                prep(dve.scalar_tensor_tensor(out=out_t, in0=kt, scalar=-PI_B, in1=out_t, op0=ALU.mult, op1=ALU.add))
                prep(dve.scalar_tensor_tensor(out=out_t, in0=kt, scalar=-PI_C, in1=out_t, op0=ALU.mult, op1=ALU.add))
                if quarter:
                    prep(dve.tensor_scalar(out_t, out_t, float(np.pi / 2), None, ALU.add))
                prep(dve.tensor_scalar(out_t, out_t, -PI_IN, PI_IN, ALU.max, ALU.min))
                dve.sem_inc(trig_dve, 1)
            dve.wait_ge(trig_act, 2)
            prep(dve.tensor_scalar(trig[64:96, 1, :], trig[64:96, 1, :], freq[64:96, 1:2], None, ALU.mult))
            dve.wait_ge(x_in, 16)
            dve.sem_inc(x_ready.sem, 8)
            dve.sem_inc(taps.sem, taps.start)

            def adds(l, m):
                n = NORM_COLS[m]
                for t in range(1, NORM_TILES[m]):
                    dve.wait_ge(sq_done.sem, sq_done.at(l, TILE0[m] + t + 1))
                    if t >= 2:
                        dve.wait_ge(add_done.sem, add_done.at(l, ADD0[m] + t - 1))
                    dve.tensor_tensor(acc[:, 0:n], acc[:, 0:n], sq[:, (t - 1) % 2, 0:n], ALU.add)\
                        .then_inc(add_done.sem, 1)

            def layer_tools(l):
                count = [0]

                def need(s, n):
                    dve.wait_ge(s.sem, s.at(l, n))

                def link(ins):
                    count[0] += 1
                    ins.then_inc(dve_step.sem, 1)
                    dve.wait_ge(dve_step.sem, dve_step.at(l, count[0]))

                def mean_square(m, bank, also=0):
                    n = NORM_COLS[m]
                    need(ssq_done, m + 1 + also)
                    dve.tensor_scalar(nv[:, 0:n], ps[bank][:, 0:n], 1.0 / NORM_DIM[m], EPS, ALU.mult, ALU.add)\
                        .then_inc(nv_done.sem, 1)

                def newton(m):
                    n = NORM_COLS[m]
                    a, v, r = rs[:, 0:n], nv[:, 0:n], r0[:, 0:n]
                    need(r0_done, m + 1)
                    link(dve.tensor_tensor(a, r, r, ALU.mult))
                    link(dve.scalar_tensor_tensor(out=a, in0=a, scalar=-0.5, in1=v, op0=ALU.mult, op1=ALU.mult))
                    link(dve.scalar_tensor_tensor(out=a, in0=a, scalar=1.5, in1=r, op0=ALU.add, op1=ALU.mult))

                def apply(m, src, hi, lo):
                    n = NORM_COLS[m]

                    def y(t):
                        if t >= 2:
                            need(nlo_done, TILE0[m] + t - 1)
                        dve.tensor_tensor(sq[:, t % 2, 0:n], src(t), rs[:, 0:n], ALU.mult).then_inc(y_done.sem, 1)

                    y(0)
                    for t in range(NORM_TILES[m]):
                        if t + 1 < NORM_TILES[m]:
                            y(t + 1)
                        need(nhi_done, TILE0[m] + t + 1)
                        dve.scalar_tensor_tensor(out=lo(t), in0=sq[:, t % 2, 0:n],
                                                 scalar=par[:, GAIN[m] + t:GAIN[m] + t + 1], in1=hi(t).bitcast(F32),
                                                 op0=ALU.mult, op1=ALU.subtract).then_inc(nlo_done.sem, 1)

                def small_root(i):
                    need(s_r0, i + 1)
                    link(dve.tensor_tensor(sm_t, sm_r, sm_r, ALU.mult))
                    link(dve.scalar_tensor_tensor(out=sm_t, in0=sm_t, scalar=-0.5, in1=sm_v, op0=ALU.mult, op1=ALU.mult))
                    link(dve.scalar_tensor_tensor(out=sm_t, in0=sm_t, scalar=1.5, in1=sm_r, op0=ALU.add, op1=ALU.mult))

                return need, link, mean_square, newton, apply, small_root, count

            half_turn = [(i + 16) % 32 for i in range(32)]

            def layer(l):
                need, link, mean_square, newton, apply, small_root, count = layer_tools(l)

                def rope(src, done):
                    dve.sem_inc(dve_passed, 1)
                    link(dve.stream_shuffle(rot[64:96, 1, :], src, half_turn))
                    link(dve.tensor_tensor(rot[64:96, 1, :], rot[64:96, 1, :], trig[64:96, 1, :], ALU.mult))
                    link(dve.tensor_tensor(rot[64:96, 2, :], src, trig[64:96, 0, :], ALU.mult))
                    dve.tensor_tensor(rot[64:96, 2, :], rot[64:96, 2, :], rot[64:96, 1, :], ALU.add)\
                        .then_inc(done.sem, 1)

                adds(l, MIX)
                mean_square(MIX, 4)
                newton(MIX)
                apply(MIX, lambda t: x[:, t, :], lambda t: h_hi[:, t, :], lambda t: h_lo[:, t, :])
                need(used, B_LAT + 4)
                for j in range(3):
                    dve.tensor_copy(lat[:, j, :], ps[j][:, :]).then_inc(lat_done.sem, 1)
                dve.tensor_copy(lat[64:96, 3, :], ps[3][64:96, :]).then_inc(lat_done.sem, 1)
                need(lat_done, 4)
                rope(lat[64:96, 3, :], kpe_ready)
                for p in range(2):
                    need(kpe_hi, p + 1)
                    dve.tensor_tensor(k_lo[64:96, p, :], rot[64:96, 2, :], k_hi[64:96, p, :].bitcast(F32), ALU.subtract)
                adds(l, NQ)
                mean_square(NQ, 0, also=1)
                newton(NQ)
                apply(NQ, lambda t: lat[:, t, :], lambda t: cq_hi[:, t, :], lambda t: cq_lo[:, t, :])
                mean_square(NKV, 1)
                newton(NKV)
                apply(NKV, lambda t: lat[:, 2, :], lambda t: ckv_hi[:, t, :], lambda t: ckv_lo[:, t, :])
                for t in range(TT):
                    need(vg_done, t + 1)
                    link(dve.bn_stats(bn[:, t, :], vt[:, t, :]))
                    dve.sem_inc(dve_passed, 1)
                    link(dve.bn_aggr(mv[:, t, :], bn[:, t, :]))
                dve.tensor_scalar(sm_v, mv[:, :, 1], EPS, None, ALU.add).then_inc(s_v.sem, 1)
                small_root(0)
                for t in range(TT):
                    link(dve.tensor_scalar(vt[:, t, :], vt[:, t, :], mv[:, t, 0:1], sm_t[:, t:t + 1],
                                           ALU.subtract, ALU.mult))
                    link(dve.tensor_tensor(vt[:, t, :], vt[:, t, :], ln_gb[:, 0, :], ALU.mult))
                    dve.tensor_tensor(vt[:, t, :], vt[:, t, :], ln_gb[:, 1, :], ALU.add).then_inc(vn_done.sem, 1)
                for t in range(TT):
                    need(vh_done, t + 1)
                    dve.tensor_tensor(v_lo[:, t, :], ps[BB[t]][:, :], v_hi[:, t, :].bitcast(F32), ALU.subtract)\
                        .then_inc(vl_done.sem, 1)
                for t in range(TT):
                    need(svh_done, t + 1)
                    dve.tensor_tensor(sv_lo[:, t, :], vt[:, t, :], sv_hi[:, t, :].bitcast(F32), ALU.subtract)\
                        .then_inc(svl_done.sem, 1)

                def q_part(h):
                    need(qh_done, h + 1)
                    need(pe_copied, h + 1)
                    dve.tensor_tensor(q_lo[0:64, h % 2, :], ps[0][0:64, :], q_hi[0:64, h % 2, :].bitcast(F32),
                                      ALU.subtract).then_inc(ql_done.sem, 1)
                    rope(rot[64:96, 0, :], roped)

                def k_part(h):
                    need(kh_done, h + 1)
                    dve.tensor_tensor(k_lo[0:64, h % 2, :], ps[0][0:64, :], k_hi[0:64, h % 2, :].bitcast(F32),
                                      ALU.subtract).then_inc(kl_done.sem, 1)
                    need(peh_done, h + 1)
                    dve.tensor_tensor(q_lo[64:96, h % 2, :], rot[64:96, 2, :], q_hi[64:96, h % 2, :].bitcast(F32),
                                      ALU.subtract).then_inc(qk_ready.sem, 1)

                def maximum(mm, done, bank, n, scale, h, t):
                    need(mm, h * TT + t + 1)
                    link(dve.reduce_max(mx[:, t:t + 1], ps[bank][:, 0:n], AXX))
                    dve.tensor_scalar(nmx[:, t:t + 1], mx[:, t:t + 1], -scale, None, ALU.mult).then_inc(done.sem, 1)

                def probs(exps, done, n, h, t):
                    need(exps, h * TT + t + 1)
                    link(dve.reciprocal(rin[:, t:t + 1], sums[:, t:t + 1]))
                    dve.tensor_scalar(e[:, t % 2, 0:n], e[:, t % 2, 0:n], rin[:, t:t + 1], None, ALU.mult)\
                        .then_inc(done.sem, 1)

                def amax(h, t):
                    maximum(score_mm, nmax_done, 2 + t % 2, SEQ, SCALE, h, t)

                def aprob(h, t):
                    probs(exp_done, prob_done, SEQ, h, t)

                q_part(0)
                k_part(0)
                q_part(1)
                amax(0, 0)
                amax(0, 1)
                aprob(0, 0)
                aprob(0, 1)
                k_part(1)
                for h in range(HEADS):
                    for t in (2, 3):
                        amax(h, t)
                        aprob(h, t)
                    if h + 1 < HEADS:
                        amax(h + 1, 0)
                        amax(h + 1, 1)
                    for t in range(TT):
                        need(pth_done, 4 * h + t + 1)
                        dve.tensor_tensor(pt_lo[:, t, :], ps[4 + t][:, :], pt_hi[:, t, :].bitcast(F32), ALU.subtract)\
                            .then_inc(ptl_done.sem, 1)
                    if h + 1 < HEADS:
                        aprob(h + 1, 0)
                        aprob(h + 1, 1)
                    if h + 2 < HEADS:
                        q_part(h + 2)
                        k_part(h + 2)
                adds(l, MLA)
                for s in range(SG_HEADS):
                    if s < SG_HEADS - 2:
                        need(mix_mm, s // 2 + 1)
                    else:
                        need(used, B_WS + 1)
                    us = u[:, :, SG_HD * s:SG_HD * s + SG_HD]
                    dve.scalar_tensor_tensor(out=us, in0=ps[4 + s // 2][:, (s % 2) * 256:(s % 2) * 256 + 256]
                                             .rearrange("p (c d) -> p c d", c=TT),
                                             scalar=par[:, C_BS + s:C_BS + s + 1], in1=us,
                                             op0=ALU.add, op1=ALU.mult).then_inc(gated.sem, 1)
                mean_square(MLA, 2)
                need(gated, SG_HEADS)
                for t in range(TT):
                    link(dve.bn_stats(bn[:, t, :], u[:, t, :]))
                    dve.sem_inc(dve_passed, 1)
                    link(dve.bn_aggr(mv[:, t, :], bn[:, t, :]))
                link(dve.tensor_tensor(sm_t, mv[:, :, 0], mv[:, :, 0], ALU.mult))
                dve.scalar_tensor_tensor(out=sm_v, in0=sm_t, scalar=EPS, in1=mv[:, :, 1], op0=ALU.add, op1=ALU.add)\
                    .then_inc(s_v.sem, 1)
                newton(MLA)
                apply(MLA, lambda t: o_mla[:, t, :], lambda t: h_hi[:, t, :], lambda t: h_lo[:, t, :])
                small_root(1)
                for t in range(TT):
                    dve.tensor_scalar(u[:, t, :], u[:, t, :], sm_t[:, t:t + 1], None, ALU.mult).then_inc(sg_normed.sem, 1)
                for t in range(4):
                    need(sgh_done, t + 1)
                    dve.scalar_tensor_tensor(out=h_lo[:, 4 + t, :], in0=ps[t][:, :],
                                             scalar=par[:, G_SG + t:G_SG + t + 1], in1=h_hi[:, 4 + t, :].bitcast(F32),
                                             op0=ALU.mult, op1=ALU.subtract).then_inc(sgl_done.sem, 1)
                adds(l, MTOK)
                need(used, B_OUT + 4)
                def residual(b_last, banks, t0):
                    need(used, b_last + 1)
                    for j in range(4):
                        dve.tensor_tensor(x[:, t0 + j, :], x[:, t0 + j, :], ps[banks[j]][:, :], ALU.add)\
                            .then_inc(x_ready.sem, 1)

                residual(B_OUT + 3, BB, 0)
                mean_square(MTOK, 0)
                newton(MTOK)
                apply(MTOK, lambda t: memT[:, t, :], lambda t: mt_hi[:, t, :], lambda t: mt_lo[:, t, :])
                residual(B_OUT + 7, BA, 4)
                adds(l, MEM)
                mean_square(MEM, 0)
                newton(MEM)
                apply(MEM, lambda t: x[:, t, :], lambda t: h_hi[:, t, :], lambda t: h_lo[:, t, :])
                for g in range(2):
                    for j in range(4):
                        need(kmh_done, 4 * g + j + 1)
                        dve.tensor_tensor(km_lo[:, 4 * g + j, :], ps[(BB, BA)[g][j]][:, 0:N_MEM],
                                          km_hi[:, 4 * g + j, :].bitcast(F32), ALU.subtract).then_inc(kml_done.sem, 1)
                for g in range(2):
                    for j in range(MT):
                        need(vmh_done, MT * g + j + 1)
                        dve.tensor_tensor(vm_lo[:, 2 * j + g, :], ps[4 + 2 * g + j][:, :],
                                          vm_hi[:, 2 * j + g, :].bitcast(F32), ALU.subtract).then_inc(vml_done.sem, 1)
                for g in range(2):
                    for j in range(4):
                        need(qmh_done, 4 * g + j + 1)
                        dve.tensor_tensor(qm_lo[:, 4 * g + j, :], ps[(BA, BB)[g][j]][:, :],
                                          qm_hi[:, 4 * g + j, :].bitcast(F32), ALU.subtract).then_inc(qml_done.sem, 1)

                def mmax(h, t):
                    maximum(mscore_mm, mnmax_done, t % 2, N_MEM, MEM_SCALE, h, t)

                def mprob(h, t):
                    probs(mexp_done, mprob_done, N_MEM, h, t)

                mmax(0, 0)
                mmax(0, 1)
                mprob(0, 0)
                mprob(0, 1)
                for h in range(MEM_HEADS):
                    for t in (2, 3):
                        mmax(h, t)
                        mprob(h, t)
                    if h + 1 < MEM_HEADS:
                        mmax(h + 1, 0)
                        mmax(h + 1, 1)
                    for t in range(MT):
                        need(pmh_done, MT * h + t + 1)
                        dve.tensor_tensor(pm_lo[:, t, :], ps[2 + t][:, :], pm_hi[:, t, :].bitcast(F32), ALU.subtract)\
                            .then_inc(pml_done.sem, 1)
                    if h + 1 < MEM_HEADS:
                        mprob(h + 1, 0)
                        mprob(h + 1, 1)
                    for j in range(2):
                        need(omh_done, 2 * h + j + 1)
                        dve.tensor_tensor(h_lo[:, 2 * h + j, :], ps[4 + 2 * (h % 2) + j][:, :],
                                          h_hi[:, 2 * h + j, :].bitcast(F32), ALU.subtract).then_inc(oml_done.sem, 1)
                residual(B_MO + 3, BA, 0)
                residual(B_MO + 7, BB, 4)
                adds(l, FFN)
                mean_square(FFN, 0)
                newton(FFN)
                apply(FFN, lambda t: x[:, t, :], lambda t: h_hi[:, t, :], lambda t: h_lo[:, t, :])

                def up_group(half, r, i, step):
                    g = sum(GROUPS[:half]) + r
                    bank = 4 * (r % 2)

                    def col(base):
                        return par[:, bass.ds(i * (2 * step) + base, 1)] if step else par[:, base:base + 1]

                    def outer(j, s):
                        n = 4 * g + 2 * j + s
                        dve.wait_ge(tap1.sem, l * (2 * FT) + i * (4 * step) + (n + 1))
                        c, a = conv[:, bank + 2 * j + s, :], ps[bank + 2 * s + j]
                        at = s * FT + 2 * g + j
                        dve.scalar_tensor_tensor(out=c[:, 1:SEQ], in0=a[:, 0:SEQ - 1], scalar=col(C_W0 + at),
                                                 in1=c[:, 1:SEQ], op0=ALU.mult, op1=ALU.add).then_inc(taps.sem, 1)
                        dve.wait_ge(taps.sem, l * (4 * FT) + i * (8 * step) + (2 * n + 1 + taps.start))
                        dve.scalar_tensor_tensor(out=c[:, 0:SEQ - 1], in0=a[:, 1:SEQ], scalar=col(C_W2 + at),
                                                 in1=c[:, 0:SEQ - 1], op0=ALU.mult, op1=ALU.add).then_inc(taps.sem, 1)

                    def product(j):
                        n = 2 * g + j
                        dve.wait_ge(silu_done.sem, l * FT + i * (2 * step) + (n + 1))
                        dve.wait_ge(taps.sem, l * (4 * FT) + i * (8 * step) + (4 * n + 4 + taps.start))
                        c = conv[:, bank + 2 * j, :]
                        dve.tensor_tensor(c, c, conv[:, bank + 2 * j + 1, :], ALU.mult).then_inc(prod_done.sem, 1)

                    def low(j):
                        dve.wait_ge(fh_done.sem, l * FT + i * (2 * step) + (2 * g + j + 1))
                        at = bass.ds(i * (2 * step) + (2 * r + j), 1) if step else slice(2 * r + j, 2 * r + j + 1)
                        dve.tensor_tensor(hid_lo[:, at, :], conv[:, bank + 2 * j:bank + 2 * j + 1, :],
                                          hid_hi[:, at, :].bitcast(F32), ALU.subtract).then_inc(fl_done.sem, 1)

                    outer(0, 0)
                    outer(0, 1)
                    outer(1, 0)
                    product(0)
                    outer(1, 1)
                    product(1)
                    low(0)
                    low(1)

                for half in range(2):
                    with dve.Fori(0, GROUPS[half] // 2) as i:
                        for r in range(2):
                            up_group(half, r, i, 2)
                    if GROUPS[half] % 2:
                        up_group(half, GROUPS[half] - 1, 0, 0)
                    for hf in range(2):
                        residual(B_DN[half] + GROUPS[half] * (hf + 1) - 1, ((BA, BB), (BB, BA))[half][hf], 4 * hf)
                assert count[0] == N_STEP, count[0]

            with dve.Fori(0, DEPTH) as l:
                layer(l)

            need, link, mean_square, newton, apply, small_root, count = layer_tools(DEPTH)
            adds(DEPTH, MIX)
            mean_square(MIX, 4)
            newton(MIX)
            for t in range(KD):
                if t >= 2:
                    need(nhi_done, t - 1)
                dve.tensor_tensor(sq[:, t % 2, :], x[:, t, :], rs, ALU.mult).then_inc(y_done.sem, 1)

        @block.tensor
        def _(pe):
            pe.wait_ge(const_done, 3)

            def layer(l):
                def need(s, n):
                    pe.wait_ge(s.sem, s.at(l, n))

                def block_ready(b, i=0, step=0):
                    pe.wait_ge(lo_done.sem, l * BLOCKS + i * step + (b + 1))

                def product3(out, a_hi, a_lo, b_hi, b_lo, first, last):
                    pe.matmul(out, a_hi, b_hi, start=first, stop=False)
                    pe.matmul(out, a_hi, b_lo, start=False, stop=False)
                    return pe.matmul(out, a_lo, b_hi, start=False, stop=last)

                def sum_squares(m, bank, acc_t=acc):
                    n = NORM_COLS[m]
                    if NORM_TILES[m] > 1:
                        need(add_done, ADD0[m + 1])
                    else:
                        need(sq_done, TILE0[m] + 1)
                    pe.matmul(ps[bank][:, 0:n], ones[:, :], acc_t[:, 0:n], start=True, stop=True)\
                        .then_inc(ssq_done.sem, 1)

                def halves(b, width):
                    s = b % SPLIT
                    return (w_hi[:, s, :].rearrange("p (k c) -> p k c", c=width),
                            w_lo[:, s, :].rearrange("p (k c) -> p k c", c=width))

                def project(b0, banks, x_hi, x_lo, ready, n=SEQ, cols=None, blocks=4, k0=0, i=0, step=0):
                    for kp in range(blocks):
                        block_ready(b0 + kp, i, step)
                        wh, wl = halves(b0 + kp, 512)
                        for jk in range(2):
                            k = 2 * kp + jk
                            ready(k)
                            for j in range(len(banks)):
                                c = cols[j] if cols else slice(P * j, P * j + P)
                                last = product3(ps[banks[j]][0:c.stop - c.start, 0:n], wh[:, jk, c], wl[:, jk, c],
                                                x_hi[:, k, 0:n], x_lo[:, k, 0:n],
                                                k == 0, k == 2 * blocks - 1)
                        last.then_inc(used.sem, 1)

                def project_tokens(b0, banks, x_hi, x_lo, ready):
                    for kp in range(4):
                        block_ready(b0 + kp)
                        wh, wl = halves(b0 + kp, 512)
                        for jk in range(2):
                            k = 2 * kp + jk
                            ready(k)
                            for j in range(len(banks)):
                                c = slice(P * j, P * j + P)
                                last = product3(ps[banks[j]][:, :], x_hi[:, k, c], x_lo[:, k, c],
                                                wh[:, jk, :], wl[:, jk, :], k == 0, k == 7)
                        last.then_inc(used.sem, 1)

                def normed(m):
                    return lambda k: need(nlo_done, TILE0[m] + k + 1)

                sum_squares(MIX, 4)
                project(B_LAT, BA, h_hi, h_lo, normed(MIX),
                        cols=[slice(0, 128), slice(128, 256), slice(256, 384), slice(320, 416)])
                need(nv_done, MIX + 1)
                project_tokens(B_U, BB, h_hi, h_lo, lambda k: None)
                need(lat_done, 4)
                sum_squares(NQ, 0)
                sum_squares(NKV, 1, acc_t=sq[:, 1, :])
                need(nv_done, NKV + 1)
                project_tokens(B_V, BA, h_hi, h_lo, lambda k: None)
                block_ready(B_WV)
                wh, wl = halves(B_WV, 512)
                need(nlo_done, TILE0[NKV] + 1)
                need(u_done, 4)
                for t in range(TT):
                    c = slice(P * t, P * t + P)
                    last = product3(ps[BB[t]][:, :], ckv_hi[:, 0, c], ckv_lo[:, 0, c], wh[:, 0, :], wl[:, 0, :],
                                    True, True)
                    if t < TT - 1:
                        last.then_inc(wv_mm.sem, 1)
                last.then_inc(used.sem, 1)

                def q_proj(h):
                    b = B_HEAD + h // 2
                    if h % 2 == 0:
                        block_ready(b)
                    wh, wl = halves(b, BLK)
                    if h == 0:
                        need(vg_done, 4)
                    else:
                        need(kl_done, h)
                    for k in range(2):
                        c = slice(k * 2 * QK + (h % 2) * QK, k * 2 * QK + (h % 2) * QK + QK)
                        last = product3(ps[0][0:QK, :], wh[:, 0, c], wl[:, 0, c], cq_hi[:, k, :], cq_lo[:, k, :],
                                        k == 0, k == 1)
                    last.then_inc(qp_mm.sem, 1)

                def k_proj(h):
                    b = B_HEAD + h // 2
                    wh, wl = halves(b, BLK)
                    c = slice(4 * QK + (h % 2) * NOPE, 4 * QK + (h % 2) * NOPE + NOPE)
                    need(ql_done, h + 1)
                    pe.matmul(ps[0][0:NOPE, :], wh[:, 0, c], ckv_hi[:, 0, :], start=True, stop=False)
                    pe.matmul(ps[0][0:NOPE, :], wl[:, 0, c], ckv_hi[:, 0, :], start=False, stop=False)
                    pe.matmul(ps[0][0:NOPE, :], wh[:, 0, c], ckv_lo[:, 0, :], start=False, stop=True)\
                        .then_inc((used if h % 2 else kp_mm).sem, 1)

                def scores(h, t):
                    i = h * TT + t
                    if t == 0:
                        need(qk_ready, h + 1)
                    if i >= 2:
                        need(exp_done, i - 1)
                    c = slice(P * t, P * t + P)
                    product3(ps[2 + t % 2][:, :], q_hi[0:QK, h % 2, c], q_lo[0:QK, h % 2, c],
                             k_hi[0:QK, h % 2, :], k_lo[0:QK, h % 2, :], True, True).then_inc(score_mm.sem, 1)

                def turn(h, t):
                    need(prob_done, h * TT + t + 1)
                    if t == 0 and h > 0:
                        need(ptl_done, 4 * h)
                    for k in range(TT):
                        last = pe.transpose(ps[4 + k][:, P * t:P * t + P], e[:, t % 2, P * k:P * k + P], ident[:, :])
                    last.then_inc(turned.sem, 1)

                def attend(h):
                    if h > 0:
                        need(o_done, h)
                    c = slice(VD * h, VD * h + VD)
                    for k in range(TT):
                        need(ptl_done, 4 * h + k + 1)
                        last = product3(ps[1][0:VD, :], v_hi[:, k, c], v_lo[:, k, c], pt_hi[:, k, :], pt_lo[:, k, :],
                                        k == 0, k == TT - 1)
                    last.then_inc(pv_mm.sem, 1)

                need(nlo_done, TILE0[NQ] + 2)
                q_proj(0)
                k_proj(0)
                q_proj(1)
                scores(0, 0)
                scores(0, 1)
                k_proj(1)
                need(vl_done, 4)
                for h in range(HEADS):
                    turn(h, 0)
                    scores(h, 2)
                    turn(h, 1)
                    scores(h, 3)
                    turn(h, 2)
                    turn(h, 3)
                    if h + 1 < HEADS:
                        scores(h + 1, 0)
                        scores(h + 1, 1)
                    if h + 2 < HEADS:
                        q_proj(h + 2)
                    attend(h)
                    if h + 2 < HEADS:
                        k_proj(h + 2)

                block_ready(B_WS)
                wh, wl = halves(B_WS, P)
                need(svl_done, 4)
                for s in range(SG_HEADS):
                    c = slice(SG_HD * s, SG_HD * s + SG_HD)
                    out = ps[4 + s // 2][:, (s % 2) * 256:(s % 2) * 256 + 256].rearrange("p (c d) -> p c d", c=TT)
                    last = product3(out, wh[:, s, :], wl[:, s, :], sv_hi[:, :, c], sv_lo[:, :, c], True, True)
                    if s % 2:
                        last.then_inc((mix_mm if s < SG_HEADS - 1 else used).sem, 1)
                sum_squares(MLA, 2)
                need(nv_done, MLA + 1)
                for t in range(TT):
                    need(sg_normed, t + 1)
                    for f in range(4):
                        last = pe.transpose(ps[f][:, P * t:P * t + P], u[:, t, P * f:P * f + P], ident[:, :])
                    last.then_inc(sg_turned.sem, 1)

                def mixed(k):
                    if k < 4:
                        need(nlo_done, TILE0[MLA] + k + 1)
                    else:
                        need(sgl_done, k - 3)

                project(B_OUT, BB, h_hi, h_lo, mixed)
                need(sgl_done, 4)
                sum_squares(MTOK, 0)
                need(nv_done, MTOK + 1)
                project(B_OUT + 4, BA, h_hi, h_lo, lambda k: None)
                need(x_ready, 4)
                project(B_MK, BB, mt_hi, mt_lo, normed(MTOK), n=N_MEM)
                need(x_ready, 8)
                sum_squares(MEM, 0)
                need(nv_done, MEM + 1)
                project(B_MK + 4, BA, mt_hi, mt_lo, lambda k: None, n=N_MEM)
                need(kml_done, 4)
                project_tokens(B_MV, (4, 5), mt_hi, mt_lo, lambda k: None)
                project_tokens(B_MV + 4, (6, 7), mt_hi, mt_lo, lambda k: None)
                need(kml_done, 8)
                project(B_MQ, BA, h_hi, h_lo, normed(MEM))
                need(vml_done, 4)
                project(B_MQ + 4, BB, h_hi, h_lo, lambda k: None)

                def mscores(h, t):
                    i = h * TT + t
                    if i >= 2:
                        need(mexp_done, i - 1)
                    if t == 0:
                        need(qml_done, 2 * h + 2)
                    c = slice(P * t, P * t + P)
                    for k in range(2):
                        f = 2 * h + k
                        last = product3(ps[t % 2][:, 0:N_MEM], qm_hi[:, f, c], qm_lo[:, f, c],
                                        km_hi[:, f, :], km_lo[:, f, :], k == 0, k == 1)
                    last.then_inc(mscore_mm.sem, 1)

                def mturn(h, t):
                    need(mprob_done, h * TT + t + 1)
                    if t == 0 and h > 0:
                        need(pml_done, MT * h)
                    for k in range(MT):
                        last = pe.transpose(ps[2 + k][:, P * t:P * t + P], e[:, t % 2, P * k:P * k + P], ident[:, :])
                    last.then_inc(mturned.sem, 1)

                def mattend(h):
                    if h >= 2:
                        need(oml_done, 2 * h - 2)
                    for j in range(2):
                        f = 2 * h + j
                        c = slice((f % 4) * P, (f % 4) * P + P)
                        for k in range(MT):
                            need(pml_done, MT * h + k + 1)
                            at = 2 * k + f // 4
                            last = product3(ps[4 + 2 * (h % 2) + j][:, :], vm_hi[:, at, c], vm_lo[:, at, c],
                                            pm_hi[:, k, :], pm_lo[:, k, :], k == 0, k == MT - 1)
                        last.then_inc(mpv_mm.sem, 1)

                need(qml_done, 8)
                mscores(0, 0)
                mscores(0, 1)
                for h in range(MEM_HEADS):
                    mturn(h, 0)
                    mscores(h, 2)
                    mturn(h, 1)
                    mscores(h, 3)
                    mturn(h, 2)
                    mturn(h, 3)
                    if h + 1 < MEM_HEADS:
                        mscores(h + 1, 0)
                        mscores(h + 1, 1)
                    mattend(h)
                project(B_MO, BA, h_hi, h_lo, lambda k: need(oml_done, k + 1))
                project(B_MO + 4, BB, h_hi, h_lo, lambda k: None)

                need(x_ready, 12)
                sum_squares(FFN, 0)
                need(nv_done, FFN + 1)
                need(nlo_done, TILE0[FFN] + 1)

                def up_group(half, r, i, step):
                    g = sum(GROUPS[:half]) + r
                    bank = 4 * (r % 2)
                    pe.wait_ge(taps.sem, l * (4 * FT) + i * (8 * step) + (8 * (g - 1) + taps.start))
                    project(B_UP[half] + 4 * r, tuple(range(bank, bank + 4)), h_hi, h_lo,
                            normed(FFN) if g == 0 else (lambda k: None), i=i, step=4 * step)

                for half in range(2):
                    pe.sem_inc(pe_passed, 1)
                    with pe.Fori(0, GROUPS[half] // 2) as i:
                        for r in range(2):
                            up_group(half, r, i, 2)
                    if GROUPS[half] % 2:
                        up_group(half, GROUPS[half] - 1, 0, 0)
                    g0 = sum(GROUPS[:half])
                    for hf in range(2):
                        need(taps, 8 * (g0 + GROUPS[half] - 1 + hf))
                        project(B_DN[half] + GROUPS[half] * hf, ((BA, BB), (BB, BA))[half][hf], hid_hi, hid_lo,
                                (lambda k: need(fl_done, 2 * g0 + k + 1)) if hf == 0 else (lambda k: None),
                                blocks=GROUPS[half])
                    if half == 0:
                        need(x_ready, 24)

            with pe.Fori(0, DEPTH) as l:
                layer(l)
            pe.wait_ge(add_done.sem, add_done.at(DEPTH, KD - 1))
            pe.matmul(ps[4][:, :], ones[:, :], acc, start=True, stop=True).then_inc(ssq_done.sem, 1)


def _pack(w, c0, width):
    k = w.shape[0] // (2 * P)
    return w[:, c0:c0 + width].reshape(k, 2, P, width).transpose(0, 2, 1, 3).reshape(k, P, 2 * width)


def _weight_blocks(w_in, w_uq, w_ukv, w_s, w_out, w_mkv, w_mq, w_mo, w_up, w_down):
    out = np.zeros((BLOCKS, P, BLK), np.float32)
    c3 = Q_LORA + KV_LORA + ROPE
    for k in range(2):
        out[B_LAT:B_LAT + 4, :, 512 * k:512 * k + c3] = \
            w_in[:, 0:c3].reshape(4, 2, P, c3)[:, k]
    out[B_U:B_U + 4] = _pack(w_in, c3, SG)
    out[B_V:B_V + 4] = _pack(w_in, c3 + SG, SG)
    ukv = w_ukv.reshape(KV_LORA, HEADS, NOPE + VD)
    out[B_WV, :, 0:HEADS * VD] = ukv[:, :, NOPE:].reshape(KV_LORA, HEADS * VD)
    uq = w_uq.reshape(2, P, HEADS, QK)
    for p in range(HEADS // 2):
        for k in range(2):
            out[B_HEAD + p, :, 2 * QK * k:2 * QK * (k + 1)] = uq[k, :, 2 * p:2 * p + 2, :].reshape(P, 2 * QK)
        out[B_HEAD + p, :, 4 * QK:4 * QK + 2 * NOPE] = ukv[:, 2 * p:2 * p + 2, 0:NOPE].reshape(P, 2 * NOPE)
    out[B_WS] = w_s.transpose(2, 0, 1).reshape(P, SG_HEADS * P)
    for base, w, c in ((B_OUT, w_out, 0), (B_MK, w_mkv, 0), (B_MV, w_mkv, D), (B_MQ, w_mq, 0), (B_MO, w_mo, 0)):
        for g in range(2):
            out[base + 4 * g:base + 4 * g + 4] = _pack(w, c + 512 * g, 512)
    g = 0
    for half in range(2):
        for r in range(GROUPS[half]):
            cols = np.concatenate([w_up[:, 256 * g:256 * g + 256], w_up[:, D_FF + 256 * g:D_FF + 256 * g + 256]], 1)
            out[B_UP[half] + 4 * r:B_UP[half] + 4 * r + 4] = _pack(cols, 0, 512)
            g += 1
        rows = w_down[256 * sum(GROUPS[:half]):256 * sum(GROUPS[:half + 1])]
        for hf in range(2):
            n = GROUPS[half]
            out[B_DN[half] + n * hf:B_DN[half] + n * (hf + 1)] = _pack(rows, 512 * hf, 512)
    return out


def _columns(v):
    return v.reshape(-1, P).T


def kernel(**inputs):
    import concourse.bacc as bacc
    from concourse.bass_utils import run_bass_kernel_spmd

    a = {k: np.asarray(v) for k, v in inputs.items()}
    blocks = np.concatenate([
        _weight_blocks(*(a[n][l] for n in ("w_in", "w_uq", "w_ukv", "sg_w_s", "w_out", "w_mkv", "w_mq", "w_mo",
                                           "w_up", "w_down"))) for l in range(DEPTH)])
    par = np.stack([np.concatenate(
        [_columns(a[n][l]) for n in ("norm_mix_g", "q_norm_g", "kv_norm_g", "out_norm_mla_g", "out_norm_sg_g",
                                     "mem_norm_g", "norm_mem_g", "norm_ffn_g")]
        + [a["sg_b_s"][l].T] + [_columns(a["conv_w"][l, k]) for k in range(3)] + [_columns(a["conv_b"][l])], 1)
        for l in range(DEPTH)])
    half = ROPE // 2
    inv = np.float32(10000.0) ** (-np.arange(half, dtype=np.float32) / np.float32(half))
    freq = np.zeros((P, 2), np.float32)
    freq[64:80, 0] = freq[80:96, 0] = inv
    freq[64:80, 1], freq[80:96, 1] = -1.0, 1.0
    arrays = {
        "blocks": blocks,
        "xT": np.ascontiguousarray(a["x"][0].T.reshape(KD, P, SEQ).transpose(1, 0, 2)),
        "memT": np.ascontiguousarray(a["mem"][0].T.reshape(KD, P, N_MEM).transpose(1, 0, 2)),
        "pos": np.ascontiguousarray(a["positions"]),
        "par": np.ascontiguousarray(par),
        "ln": np.ascontiguousarray(np.concatenate([a["sg_ln_g"], a["sg_ln_b"]], 1)),
        "fin": np.ascontiguousarray(_columns(a["final_norm_g"])),
        "freq": freq,
    }
    nc = bacc.Bacc("TRN2", target_bir_lowering=False, num_devices=1)
    args = [nc.dram_tensor(f"{n}_d", v.shape, mybir.dt.from_np(v.dtype), kind="ExternalInput").ap()
            for n, v in arrays.items()]
    out = nc.dram_tensor("outT_d", (P, KD, SEQ), F32, kind="ExternalOutput").ap()
    encoder_program(nc, *args, out)
    r = run_bass_kernel_spmd(nc, [{f"{n}_d": v for n, v in arrays.items()}], core_ids=[0])
    outT = r.results[0]["outT_d"]
    return np.ascontiguousarray(outT.transpose(1, 0, 2).reshape(D, SEQ).T)[None]
```

```python
import numpy as np
from contextlib import ExitStack

import concourse.bass as bass
from concourse import mybir

F32 = mybir.dt.float32
F32R = mybir.dt.float32r
I32 = mybir.dt.int32
ALU = mybir.AluOpType
ACT = mybir.ActivationFunctionType
AXX = mybir.AxisListType.X

P = 128
DEPTH, SEQ, D, N_MEM = 2, 512, 1024, 256
KD = D // P
TT = SEQ // P
EPS = 1e-6
HEADS, NOPE, ROPE, VD = 8, 64, 32, 64
QK = NOPE + ROPE
Q_LORA, KV_LORA = 256, 128
SG, SG_HEADS, SG_HD = 512, 8, 64
MEM_HEADS, MEM_HD = 4, 256
MT = N_MEM // P
D_FF = 2816
FT = D_FF // P
SCALE = float(QK) ** -0.5
MEM_SCALE = float(MEM_HD) ** -0.5

BLK = 1024
RAW, SPLIT = 2, 4
AHEAD = 3
B_LAT = 0
B_U = B_LAT + 4
B_V = B_U + 4
B_WV = B_V + 4
B_HEAD = B_WV + 1
B_WS = B_HEAD + HEADS // 2
B_OUT = B_WS + 1
B_MK = B_OUT + 8
B_MV = B_MK + 8
B_MQ = B_MV + 8
B_MO = B_MQ + 8
B_UP = (B_MO + 8, B_MO + 8 + 24 + 12)
B_DN = (B_UP[0] + 24, B_UP[1] + 20)
GROUPS = (6, 5)
BLOCKS = B_DN[1] + 10
assert BLOCKS % SPLIT == 0

MIX, NQ, NKV, MLA, MTOK, MEM, FFN = range(7)
NORM_TILES = (8, 2, 1, 4, 8, 8, 8)
NORM_DIM = (D, Q_LORA, KV_LORA, HEADS * VD, D, D, D)
NORM_COLS = (SEQ, SEQ, SEQ, SEQ, N_MEM, SEQ, SEQ)
N_NORMS = len(NORM_TILES)
TILE0 = tuple(sum(NORM_TILES[:m]) for m in range(N_NORMS + 1))
ADD0 = tuple(sum(n - 1 for n in NORM_TILES[:m]) for m in range(N_NORMS + 1))

Y_TILES = tuple(0 if m in (MIX, FFN) else n for m, n in enumerate(NORM_TILES))
Y0 = tuple(sum(Y_TILES[:m]) for m in range(N_NORMS + 1))

G_MIX, G_Q, G_KV, G_MLA, G_SG, G_MTOK, G_MEM, G_FFN = 0, 8, 10, 11, 15, 19, 27, 35
C_BS = 43
C_W0, C_W1, C_W2, C_B = 51, 95, 139, 183
NPAR = 227
GAIN = (G_MIX, G_Q, G_KV, G_MLA, G_MTOK, G_MEM, G_FFN)

TWO_PI = 2 * np.pi
PI_A = 6.28125
PI_B = float(np.float32(np.round((TWO_PI - PI_A) * 2 ** 20) / 2 ** 20))
PI_C = float(np.float32(TWO_PI - PI_A - PI_B))
ROUND = 1.5 * 2.0 ** 23
PI_IN = 3.1415925


class Signal:

    def __init__(self, ctx, nc, name, per_layer, start=0):
        self.sem = ctx.enter_context(nc.semaphore(name))
        self.per_layer, self.start = per_layer, start

    def at(self, layer, n):
        return layer * self.per_layer + (n + self.start)


def encoder_program(nc, blocks_d, xT_d, memT_d, pos_d, par_d, ln_d, fin_d, freq_d, out_d):
    with ExitStack() as ctx:
        def sb(name, shape, dt=F32):
            return ctx.enter_context(nc.sbuf_tensor(name, shape, dt))

        def sig(name, per_layer, start=0):
            return Signal(ctx, nc, name, per_layer, start)

        x = sb("x", [P, KD, SEQ])
        h_hi = sb("h_hi", [P, KD, SEQ], F32R)
        h_lo = sb("h_lo", [P, KD, SEQ], F32R)
        raw = sb("raw", [P, RAW, BLK])
        w_hi = sb("w_hi", [P, SPLIT, BLK], F32R)
        w_lo = sb("w_lo", [P, SPLIT, BLK], F32R)
        arena = sb("arena", [P, 36, SEQ], F32R)
        work = sb("work", [P, 18, SEQ])
        trig = sb("trig", [P, 2, SEQ])
        ln_gb = sb("ln_gb", [P, 2, SG])
        par = sb("par", [P, NPAR])
        fin_g = sb("fin_g", [P, KD])
        freq = sb("freq", [P, 2])
        ones = sb("ones", [P, P])
        ident = sb("ident", [P, P])
        small = sb("small", [P, 64])

        q_hi, q_lo, k_hi, k_lo = (arena[:, 2 * i:2 * i + 2, :] for i in range(4))
        v_hi, v_lo = arena[:, 8:12, :], arena[:, 12:16, :]
        pt_hi = (arena[:, 16:20, :], h_hi[:, 0:4, :])
        pt_lo = (arena[:, 20:24, :], h_lo[:, 0:4, :])
        sv_hi, sv_lo = h_hi[:, 4:8, :], h_lo[:, 4:8, :]
        cq_hi, cq_lo = arena[:, 24:26, :], arena[:, 26:28, :]
        ckv_hi, ckv_lo = arena[:, 28:29, :], arena[:, 29:30, :]
        km_hi = arena[:, 0:4, :].rearrange("p a (b n) -> p (a b) n", b=2)
        km_lo = arena[:, 4:8, :].rearrange("p a (b n) -> p (a b) n", b=2)
        vm_hi, vm_lo = arena[:, 8:12, :], arena[:, 12:16, :]
        mt_hi = arena[:, 16:20, :].rearrange("p a (b n) -> p (a b) n", b=2)
        mt_lo = arena[:, 20:24, :].rearrange("p a (b n) -> p (a b) n", b=2)
        qm_hi, qm_lo = arena[:, 16:24, :], arena[:, 24:32, :]
        pm_hi, pm_lo = arena[:, 32:34, :], arena[:, 34:36, :]
        hid_hi, hid_lo = arena[:, 0:12, :], arena[:, 12:24, :]
        u = work[:, 0:4, :]
        memT = work[:, 0:4, :].rearrange("p a (b n) -> p (a b) n", b=2)
        lat = work[:, 4:8, :]
        o_mla = work[:, 4:8, :]
        acc, sq, nv, r0, rs = work[:, 8, :], work[:, 9:11, :], work[:, 11, :], work[:, 12, :], work[:, 13, :]
        nv_kv = work[:, 14, :]
        e = work[:, 8:11, :]
        rot = work[:, 11:14, :]
        vt = work[:, 14:18, :]
        conv = work[:, 0:8, :]
        lin = work[:, 14:18, :]
        bn = small[:, 0:24].rearrange("p (a b) -> p a b", a=4)
        mv = small[:, 24:32].rearrange("p (a b) -> p a b", a=4)
        sm_v, sm_r, sm_t = small[:, 32:36], small[:, 36:40], small[:, 40:44]
        mx, nmx, sums, rin = small[:, 44:48], small[:, 48:52], small[:, 52:56], small[:, 56:60]
        rs_tok = small[:, 60:64]

        ps = [ctx.enter_context(nc.psum_tensor(f"ps{i}", [P, SEQ], F32)) for i in range(8)]
        BA, BB = (0, 1, 2, 3), (4, 5, 6, 7)

        raw_in = [sig(f"raw_in{i}", 16 * BLOCKS // RAW) for i in range(RAW)]
        hi_done = sig("hi_done", BLOCKS)
        lo_done = sig("lo_done", BLOCKS)
        used = sig("used", BLOCKS, SPLIT)
        x_in = ctx.enter_context(nc.semaphore("x_in"))
        const_in = ctx.enter_context(nc.semaphore("const_in"))
        const_done = ctx.enter_context(nc.semaphore("const_done"))
        trig_dve = ctx.enter_context(nc.semaphore("trig_dve"))
        trig_act = ctx.enter_context(nc.semaphore("trig_act"))
        stored = ctx.enter_context(nc.semaphore("stored"))
        par_in = sig("par_in", 32)
        mem_in = sig("mem_in", 16)
        x_ready = sig("x_ready", 32, 8)
        sq_done = sig("sq_done", TILE0[-1])
        add_done = sig("add_done", ADD0[-1])
        ssq_done = sig("ssq_done", N_NORMS)
        nv_done = sig("nv_done", N_NORMS)
        ln_done = sig("ln_done", N_NORMS)
        r0_done = sig("r0_done", N_NORMS)
        y_done = sig("y_done", Y0[-1])
        nhi_done = sig("nhi_done", TILE0[-1])
        nlo_done = sig("nlo_done", TILE0[-1])
        ssq_tok = sig("ssq_tok", 1)
        s_v = sig("s_v", 3)
        s_ln = sig("s_ln", 3)
        s_r0 = sig("s_r0", 3)
        lat_done = sig("lat_done", 4)
        kpe_ready = sig("kpe_ready", 1)
        kpe_hi = sig("kpe_hi", 2)
        u_done = sig("u_done", 4)
        vg_done = sig("vg_done", 4)
        vn_done = sig("vn_done", 4)
        svh_done = sig("svh_done", 4)
        svl_done = sig("svl_done", 4)
        wv_mm = sig("wv_mm", TT - 1)
        vh_done = sig("vh_done", 4)
        vl_done = sig("vl_done", 4)
        qp_mm = sig("qp_mm", HEADS)
        kp_mm = sig("kp_mm", HEADS // 2)
        qh_done = sig("qh_done", HEADS)
        pe_copied = sig("pe_copied", HEADS)
        ql_done = sig("ql_done", HEADS)
        roped = sig("roped", HEADS)
        kh_done = sig("kh_done", HEADS)
        kl_done = sig("kl_done", HEADS)
        shuffled = sig("shuffled", HEADS)
        peh_done = sig("peh_done", HEADS)
        pel_done = sig("pel_done", HEADS)
        pool_step = sig("pool_step", 2 * HEADS)
        recip_done = sig("recip_done", HEADS * TT)
        mrecip_done = sig("mrecip_done", MEM_HEADS * TT)
        score_mm = sig("score_mm", HEADS * TT)
        nmax_done = sig("nmax_done", HEADS * TT)
        exp_done = sig("exp_done", HEADS * TT)
        prob_done = sig("prob_done", HEADS * TT)
        turned = sig("turned", HEADS * TT)
        pth_done = sig("pth_done", HEADS * TT)
        ptl_done = sig("ptl_done", HEADS * TT)
        pv_mm = sig("pv_mm", HEADS)
        o_done = sig("o_done", HEADS)
        mix_mm = sig("mix_mm", SG_HEADS // 2 - 1)
        gated = sig("gated", SG_HEADS)
        sg_normed = sig("sg_normed", 4)
        sg_turned = sig("sg_turned", 2)
        sgh_done = sig("sgh_done", 4)
        sgl_done = sig("sgl_done", 4)
        kmh_done = sig("kmh_done", 8)
        kml_done = sig("kml_done", 8)
        vmh_done = sig("vmh_done", 4)
        vml_done = sig("vml_done", 4)
        qmh_done = sig("qmh_done", 8)
        qml_done = sig("qml_done", 8)
        mscore_mm = sig("mscore_mm", MEM_HEADS * TT)
        mnmax_done = sig("mnmax_done", MEM_HEADS * TT)
        mexp_done = sig("mexp_done", MEM_HEADS * TT)
        mprob_done = sig("mprob_done", MEM_HEADS * TT)
        mturned = sig("mturned", MEM_HEADS * TT)
        pmh_done = sig("pmh_done", MEM_HEADS * TT)
        pml_done = sig("pml_done", MEM_HEADS * TT)
        mpv_mm = sig("mpv_mm", MEM_HEADS * 2)
        omh_done = sig("omh_done", 8)
        oml_done = sig("oml_done", 8)
        tap1 = sig("tap1", 2 * FT)
        taps = sig("taps", 4 * FT)
        scaled = sig("scaled", 2 * FT, 8)
        silu_done = sig("silu_done", FT)
        prod_done = sig("prod_done", FT)
        fh_done = sig("fh_done", FT)
        fl_done = sig("fl_done", FT)
        dve_passed = ctx.enter_context(nc.semaphore("dve_passed"))
        pe_passed = ctx.enter_context(nc.semaphore("pe_passed"))
        N_STEP = 108
        dve_step = sig("dve_step", N_STEP)

        block = ctx.enter_context(nc.Block())

        @block.sync
        def _(sp):
            sp.dma_start(x[:, :, :], xT_d).then_inc(x_in, 16)
            for n in range(RAW):
                sp.dma_start(raw[:, n, :], blocks_d[n]).then_inc(raw_in[n].sem, 16)
            with sp.Fori(0, DEPTH * BLOCKS // RAW - 1) as i:
                for r in range(RAW):
                    sp.wait_ge(lo_done.sem, i * RAW + (r + 1))
                    sp.dma_start(raw[:, r, :],
                                 blocks_d[bass.ds(i * RAW + (r + RAW), 1), :, :].rearrange("a p n -> (a p) n"))\
                        .then_inc(raw_in[r].sem, 16)
            for t in range(KD):
                sp.wait_ge(nhi_done.sem, nhi_done.at(DEPTH, t + 1))
                sp.dma_start(out_d[:, t, :], conv[:, t, :]).then_inc(stored, 16)
            sp.wait_ge(stored, 16 * KD)

        @block.gpsimd
        def _(gp):
            gp.memset(ones[:, :], 1.0).then_inc(const_done, 1)
            gp.memset(ident[:, :], 0.0).then_inc(const_done, 1)
            gp.wait_ge(const_done, 2)
            gp.affine_select(out=ident[:, :], in_=ident[:, :], compare_op=ALU.not_equal, fill=1.0, base=0,
                             pattern=[[-1, P]], channel_multiplier=1).then_inc(const_done, 1)

            def layer(l):
                def need(s, n):
                    gp.wait_ge(s.sem, s.at(l, n))

                steps = [0]

                def link(ins):
                    steps[0] += 1
                    ins.then_inc(pool_step.sem, 1)
                    need(pool_step, steps[0])

                def low(b, i=0, step=0):
                    gp.wait_ge(hi_done.sem, l * BLOCKS + i * step + (b + 1))
                    gp.tensor_tensor(w_lo[:, b % SPLIT, :], raw[:, b % RAW, :], w_hi[:, b % SPLIT, :].bitcast(F32),
                                     ALU.subtract).then_inc(lo_done.sem, 1)

                def lows(b0, n):
                    with gp.Fori(0, n // SPLIT) as i:
                        for r in range(SPLIT):
                            low(b0 + r, i, SPLIT)
                    for r in range(n // SPLIT * SPLIT, n):
                        low(b0 + r)

                def rotate(h):
                    need(shuffled, h + 1)
                    link(gp.tensor_tensor(rot[64:96, 1, :], rot[64:96, 1, :], trig[64:96, 1, :], ALU.mult))
                    link(gp.tensor_tensor(rot[64:96, 2, :], rot[64:96, 0, :], trig[64:96, 0, :], ALU.mult))
                    gp.tensor_tensor(rot[64:96, 2, :], rot[64:96, 2, :], rot[64:96, 1, :], ALU.add)\
                        .then_inc(roped.sem, 1)

                def rotated_low(h):
                    need(peh_done, h + 1)
                    gp.tensor_tensor(q_lo[64:96, h % 2, :], rot[64:96, 2, :], q_hi[64:96, h % 2, :].bitcast(F32),
                                     ALU.subtract).then_inc(pel_done.sem, 1)

                def gate_low(t):
                    need(svh_done, t + 1)
                    gp.tensor_tensor(sv_lo[:, t, :], vt[:, t, :], sv_hi[:, t, :].bitcast(F32), ALU.subtract)\
                        .then_inc(svl_done.sem, 1)

                lows(0, B_HEAD + AHEAD)
                need(lo_done, B_HEAD + AHEAD)
                rotate(0)
                rotated_low(0)
                rotate(1)
                rotated_low(1)
                for h in range(HEADS):
                    if h in (1, 2, 3, 5, 7):
                        need(pel_done, min(h + 2, HEADS))
                    if h % 2 == 1:
                        low(B_HEAD + AHEAD + h // 2)
                        if h + 2 < HEADS:
                            need(lo_done, B_HEAD + AHEAD + h // 2 + 1)
                    if h in (1, 2):
                        gate_low(2 * h - 2)
                        gate_low(2 * h - 1)
                        need(svl_done, 2 * h)
                    if h + 2 < HEADS:
                        rotate(h + 2)
                        rotated_low(h + 2)
                lows(B_WS + AHEAD, BLOCKS - (B_WS + AHEAD))

            with gp.Fori(0, DEPTH) as l:
                layer(l)

        @block.scalar
        def _(act):
            act.sem_inc(used.sem, SPLIT)
            act.dma_start(work[64:96, 2, :].bitcast(I32), pos_d.to_broadcast([ROPE, SEQ])).then_inc(const_in, 16)
            act.dma_start(freq[:, :], freq_d).then_inc(const_in, 16)
            act.dma_start(fin_g[:, :], fin_d).then_inc(const_in, 16)
            act.wait_ge(trig_dve, 1)
            act.activation(trig[64:96, 1, :], work[64:96, 0, :], ACT.Sin).then_inc(trig_act, 1)
            act.wait_ge(trig_dve, 2)
            act.activation(trig[64:96, 0, :], work[64:96, 1, :], ACT.Sin).then_inc(trig_act, 1)

            def layer(l):
                def need(s, n):
                    act.wait_ge(s.sem, s.at(l, n))

                def split(b, i=0, step=0):
                    r = b % RAW
                    act.wait_ge(raw_in[r].sem,
                                l * (16 * BLOCKS // RAW) + i * (16 * step // RAW) + 16 * (b // RAW + 1))
                    act.wait_ge(used.sem,
                                l * BLOCKS + i * step + (b + 1))
                    act.activation(w_hi[:, b % SPLIT, :], raw[:, r, :], ACT.Copy).then_inc(hi_done.sem, 1)

                def ahead(b, i=0, step=0):
                    if b + AHEAD < BLOCKS:
                        split(b + AHEAD, i, step)

                def block_used(b):
                    need(used, b + 1)

                def squares(m, src, ready, acc_t=acc):
                    n = NORM_COLS[m]
                    for t in range(NORM_TILES[m]):
                        ready(t)
                        if t == 1 and m > 0:
                            need(nlo_done, TILE0[m])
                        if t >= 3:
                            need(add_done, ADD0[m] + t - 2)
                        dst = acc_t if t == 0 else sq[:, (t - 1) % 2, :]
                        act.activation(dst[:, 0:n], src(t), ACT.Square).then_inc(sq_done.sem, 1)

                def root(m, v=nv):
                    n = NORM_COLS[m]
                    act.preload_act_table_set("natural_log_exp_and_others")
                    need(nv_done, m + 1)
                    act.activation(r0[:, 0:n], v[:, 0:n], ACT.Ln).then_inc(ln_done.sem, 1)
                    need(ln_done, m + 1)
                    act.activation(r0[:, 0:n], r0[:, 0:n], ACT.Exp, scale=-0.5).then_inc(r0_done.sem, 1)

                def his(m, dst):
                    n = NORM_COLS[m]
                    for t in range(NORM_TILES[m]):
                        need(y_done, Y0[m] + t + 1)
                        act.activation(dst(t), sq[:, t % 2, 0:n], ACT.Copy,
                                       scale=par[:, GAIN[m] + t:GAIN[m] + t + 1]).then_inc(nhi_done.sem, 1)

                def his_and_squares(m, x0):
                    for t in range(KD):
                        need(x_ready, x0 + t + 1)
                        act.activation(h_hi[:, t, :], x[:, t, :], ACT.Copy,
                                       scale=par[:, GAIN[m] + t:GAIN[m] + t + 1]).then_inc(nhi_done.sem, 1)
                        if t == 1 and m > 0:
                            need(nlo_done, TILE0[m])
                        if t >= 3:
                            need(add_done, ADD0[m] + t - 2)
                        act.activation(acc if t == 0 else sq[:, (t - 1) % 2, :], x[:, t, :], ACT.Square)\
                            .then_inc(sq_done.sem, 1)

                def small_root(i):
                    act.preload_act_table_set("natural_log_exp_and_others")
                    need(s_v, i + 1)
                    act.activation(sm_r, sm_v, ACT.Ln).then_inc(s_ln.sem, 1)
                    need(s_ln, i + 1)
                    act.activation(sm_r, sm_r, ACT.Exp, scale=-0.5).then_inc(s_r0.sem, 1)

                act.dma_start(par[:, :], par_d[bass.ds(l, 1), :, :].rearrange("a p n -> (a p) n"))\
                    .then_inc(par_in.sem, 16)
                act.dma_start(ln_gb[:, :, :].rearrange("p a n -> p (a n)"),
                              ln_d[bass.ds(l, 1), :].to_broadcast([P, 2 * SG])).then_inc(par_in.sem, 16)
                for b in range(AHEAD):
                    split(b)
                need(par_in, 32)
                his_and_squares(MIX, -8)
                for b in range(B_LAT, B_LAT + 4):
                    ahead(b)
                root(MIX)
                small_root(0)
                squares(NQ, lambda t: lat[:, t, :], lambda t: need(lat_done, t + 1))
                squares(NKV, lambda t: lat[:, 2, :], lambda t: need(lat_done, 3), acc_t=sq[:, 1, :])
                ahead(B_U)
                ahead(B_U + 1)
                need(kpe_ready, 1)
                for p in range(2):
                    act.activation(k_hi[64:96, p, :], rot[64:96, 2, :], ACT.Copy).then_inc(kpe_hi.sem, 1)
                ahead(B_U + 2)
                root(NQ)
                his(NQ, lambda t: cq_hi[:, t, :])
                root(NKV, nv_kv)
                his(NKV, lambda t: ckv_hi[:, t, :])
                ahead(B_U + 3)
                block_used(B_U + 3)
                for t in range(TT):
                    act.activation(u[:, t, :], ps[BB[t]][:, :], ACT.Gelu_apprx_tanh, scale=rs_tok[:, t:t + 1])\
                        .then_inc(u_done.sem, 1)
                for b in range(B_V, B_V + 4):
                    ahead(b)
                block_used(B_V + 3)
                for t in range(TT):
                    act.activation(vt[:, t, :], ps[BA[t]][:, :], ACT.Gelu_apprx_tanh, scale=rs_tok[:, t:t + 1])\
                        .then_inc(vg_done.sem, 1)
                ahead(B_WV)
                for t in range(TT):
                    if t < TT - 1:
                        need(wv_mm, t + 1)
                    else:
                        block_used(B_WV)
                    act.activation(v_hi[:, t, :], ps[BB[t]][:, :], ACT.Copy).then_inc(vh_done.sem, 1)

                def q_part(h):
                    need(qp_mm, h + 1)
                    act.activation(q_hi[0:64, h % 2, :], ps[0][0:64, :], ACT.Copy).then_inc(qh_done.sem, 1)
                    if h > 0:
                        need(pel_done, h)
                    act.activation(rot[64:96, 0, :], ps[0][64:96, :], ACT.Copy).then_inc(pe_copied.sem, 1)

                def k_part(h):
                    if h % 2 == 0:
                        need(kp_mm, h // 2 + 1)
                    else:
                        block_used(B_HEAD + h // 2)
                    act.activation(k_hi[0:64, h % 2, :], ps[0][0:64, :], ACT.Copy).then_inc(kh_done.sem, 1)

                def rotated(h):
                    need(roped, h + 1)
                    act.activation(q_hi[64:96, h % 2, :], rot[64:96, 2, :], ACT.Copy).then_inc(peh_done.sem, 1)

                def exps(i):
                    need(nmax_done, i + 1)
                    if i >= 3:
                        need(turned, i - 2)
                    act.activation(e[:, i % 3, :], ps[2 + i % 2][:, :], ACT.Exp, bias=nmx[:, i % 4:i % 4 + 1],
                                   scale=SCALE, accum_out=sums[:, i % 4:i % 4 + 1]).then_inc(exp_done.sem, 1)

                def probs(i):
                    need(recip_done, i + 1)
                    act.activation(e[:, i % 3, :], e[:, i % 3, :], ACT.Copy, scale=rin[:, i % 4:i % 4 + 1])\
                        .then_inc(prob_done.sem, 1)

                def turned_hi(i):
                    need(turned, i + 1)
                    h, t = divmod(i, TT)
                    if t == 0 and h >= 2:
                        need(pv_mm, h - 1)
                    act.activation(pt_hi[h % 2][:, :, P * t:P * t + P],
                                   ps[4 + i % 2][:, :].rearrange("p (k q) -> p k q", k=TT), ACT.Copy)\
                        .then_inc(pth_done.sem, 1)

                def attended(h):
                    need(pv_mm, h + 1)
                    act.activation(o_mla[64 * (h % 2):64 * (h % 2) + 64, h // 2, :], ps[1][0:64, :], ACT.Copy)\
                        .then_inc(o_done.sem, 1)

                def gate_turned(n):
                    need(sg_turned, n + 1)
                    for f in (2 * n, 2 * n + 1):
                        act.activation(h_hi[:, 4 + f, :], ps[6 + f % 2][:, :], ACT.Copy,
                                       scale=par[:, G_SG + f:G_SG + f + 1]).then_inc(sgh_done.sem, 1)

                act.preload_act_table_set("natural_log_exp_and_others")
                q_part(0)
                k_part(0)
                ahead(B_HEAD)
                rotated(0)
                q_part(1)
                k_part(1)
                exps(0)
                exps(1)
                rotated(1)
                for i in range(HEADS * TT):
                    h, t = divmod(i, TT)
                    probs(i)
                    if i >= 1:
                        turned_hi(i - 1)
                    if i + 2 < HEADS * TT:
                        exps(i + 2)
                    if t == 0 and 1 <= h and h + 1 < HEADS:
                        k_part(h + 1)
                    if t == 1:
                        if 1 <= h and h + 1 < HEADS:
                            rotated(h + 1)
                    if t == 2:
                        if h >= 1:
                            attended(h - 1)
                        if h + 2 < HEADS:
                            q_part(h + 2)
                    if t == 3:
                        if h % 2 == 0:
                            ahead(B_HEAD + h // 2 + 1)
                        if h == 0:
                            small_root(1)
                        if h == 6:
                            small_root(2)
                        if h == 7:
                            gate_turned(0)
                    if h in (1, 2) and t in (1, 3):
                        g = 2 * h - 2 + t // 2
                        need(vn_done, g + 1)
                        act.activation(sv_hi[:, g, :], vt[:, g, :], ACT.Copy).then_inc(svh_done.sem, 1)
                turned_hi(HEADS * TT - 1)
                gate_turned(1)
                attended(HEADS - 1)
                squares(MLA, lambda t: o_mla[:, t, :], lambda t: need(o_done, 2 * t + 2))
                root(MLA)
                his(MLA, lambda t: h_hi[:, t, :])
                act.dma_start(memT, memT_d).then_inc(mem_in.sem, 16)
                for b in range(B_OUT, B_OUT + 4):
                    ahead(b)
                squares(MTOK, lambda t: memT[:, t, :], lambda t: need(mem_in, 16) if t == 0 else None)
                root(MTOK)
                his(MTOK, lambda t: mt_hi[:, t, :])
                for b in range(B_OUT + 4, B_OUT + 8):
                    ahead(b)
                squares(MEM, lambda t: x[:, t, :], lambda t: need(x_ready, t + 1))
                for b in range(B_MK, B_MK + 4):
                    ahead(b)

                def keys(g):
                    block_used(B_MK + 4 * g + 3)
                    for j in range(4):
                        act.activation(km_hi[:, 4 * g + j, :], ps[(BB, BA)[g][j]][:, 0:N_MEM], ACT.Copy)\
                            .then_inc(kmh_done.sem, 1)

                def values(g):
                    block_used(B_MV + 4 * g + 3)
                    for j in range(MT):
                        act.activation(vm_hi[:, 2 * j + g, :], ps[4 + 2 * g + j][:, :], ACT.Copy)\
                            .then_inc(vmh_done.sem, 1)

                def queries(g):
                    block_used(B_MQ + 4 * g + 3)
                    for j in range(4):
                        act.activation(qm_hi[:, 4 * g + j, :], ps[(BA, BB)[g][j]][:, :], ACT.Copy)\
                            .then_inc(qmh_done.sem, 1)

                keys(0)
                for b in range(B_MK + 4, B_MK + 8):
                    ahead(b)
                keys(1)
                for b in range(B_MV, B_MV + 4):
                    ahead(b)
                values(0)
                root(MEM)
                his(MEM, lambda t: h_hi[:, t, :])
                for b in range(B_MV + 4, B_MV + 8):
                    ahead(b)
                values(1)
                for g in range(2):
                    for b in range(B_MQ + 4 * g, B_MQ + 4 * g + 4):
                        ahead(b)
                    queries(g)

                def mexps(i):
                    need(mnmax_done, i + 1)
                    if i >= 3:
                        need(mturned, i - 2)
                    act.activation(e[:, i % 3, 0:N_MEM], ps[i % 2][:, 0:N_MEM], ACT.Exp, bias=nmx[:, i % 4:i % 4 + 1],
                                   scale=MEM_SCALE, accum_out=sums[:, i % 4:i % 4 + 1]).then_inc(mexp_done.sem, 1)

                def mprobs(i):
                    need(mrecip_done, i + 1)
                    act.activation(e[:, i % 3, 0:N_MEM], e[:, i % 3, 0:N_MEM], ACT.Copy, scale=rin[:, i % 4:i % 4 + 1])\
                        .then_inc(mprob_done.sem, 1)

                def mturned_hi(i):
                    need(mturned, i + 1)
                    h, t = divmod(i, TT)
                    if t == 0 and h >= 1:
                        need(mpv_mm, 2 * h)
                    act.activation(pm_hi[:, :, P * t:P * t + P],
                                   ps[2 + i % 2][:, 0:MT * P].rearrange("p (k q) -> p k q", k=MT), ACT.Copy)\
                        .then_inc(pmh_done.sem, 1)

                def outputs(h):
                    for j in range(2):
                        need(mpv_mm, 2 * h + j + 1)
                        act.activation(h_hi[:, 2 * h + j, :], ps[4 + 2 * (h % 2) + j][:, :], ACT.Copy)\
                            .then_inc(omh_done.sem, 1)

                act.preload_act_table_set("natural_log_exp_and_others")
                mexps(0)
                mexps(1)
                for i in range(MEM_HEADS * TT):
                    h, t = divmod(i, TT)
                    mprobs(i)
                    if i >= 1:
                        mturned_hi(i - 1)
                    if i + 2 < MEM_HEADS * TT:
                        mexps(i + 2)
                    if t == 1 and h >= 1:
                        outputs(h - 1)
                mturned_hi(MEM_HEADS * TT - 1)
                outputs(MEM_HEADS - 1)
                for b in range(B_MO, B_MO + 8):
                    ahead(b)
                his_and_squares(FFN, 8)

                def up_group(half, r, i, step):
                    g = sum(GROUPS[:half]) + r
                    for b in range(B_UP[half] + 4 * r, B_UP[half] + 4 * r + 4):
                        ahead(b, i, 4 * step)
                        if g == 0 and b == B_UP[0] and not step:
                            root(FFN)
                    bank = 4 * (r % 2)
                    for j in range(2):
                        for s in range(2):
                            act.wait_ge(scaled.sem, l * (2 * FT) + i * (4 * step) + (4 * g + 2 * j + s + 1 + scaled.start))
                            c = s * FT + 2 * g + j
                            cb = par[:, bass.ds(i * (2 * step) + (C_B + c), 1)] if step else par[:, C_B + c:C_B + c + 1]
                            cw = par[:, bass.ds(i * (2 * step) + (C_W1 + c), 1)] if step else par[:, C_W1 + c:C_W1 + c + 1]
                            act.activation(conv[:, bank + 2 * j + s, :], lin[:, 2 * j + s, :], ACT.Identity,
                                           bias=cb, scale=cw).then_inc(tap1.sem, 1)
                    for j in range(2):
                        act.wait_ge(taps.sem, l * (4 * FT) + i * (8 * step) + (8 * g + 4 * j + 2 + taps.start))
                        cg = conv[:, bank + 2 * j, :]
                        act.activation(cg, cg, ACT.Silu).then_inc(silu_done.sem, 1)
                    for j in range(2):
                        act.wait_ge(prod_done.sem, l * FT + i * (2 * step) + (2 * g + j + 1))
                        dst = hid_hi[:, bass.ds(i * (2 * step) + (2 * r + j), 1), :] if step \
                            else hid_hi[:, 2 * r + j:2 * r + j + 1, :]
                        act.activation(dst, conv[:, bank + 2 * j:bank + 2 * j + 1, :], ACT.Copy).then_inc(fh_done.sem, 1)

                for half in range(2):
                    peeled = 0
                    if half == 0:
                        up_group(0, 0, 0, 0)
                        up_group(0, 1, 0, 0)
                        peeled = 2
                    with act.Fori(0, (GROUPS[half] - peeled) // 2) as i:
                        for r in range(peeled, peeled + 2):
                            up_group(half, r, i, 2)
                    if GROUPS[half] % 2:
                        up_group(half, GROUPS[half] - 1, 0, 0)
                    for b in range(B_DN[half], B_DN[half] + 2 * GROUPS[half]):
                        ahead(b)

            with act.Fori(0, DEPTH) as l:
                layer(l)

            for t in range(KD):
                act.wait_ge(x_ready.sem, x_ready.at(DEPTH, t + 1 - 8))
                if t >= 3:
                    act.wait_ge(add_done.sem, add_done.at(DEPTH, t - 2))
                dst = acc if t == 0 else sq[:, (t - 1) % 2, :]
                act.activation(dst, x[:, t, :], ACT.Square).then_inc(sq_done.sem, 1)
            act.preload_act_table_set("natural_log_exp_and_others")
            act.wait_ge(nv_done.sem, nv_done.at(DEPTH, 1))
            act.activation(r0, nv, ACT.Ln).then_inc(ln_done.sem, 1)
            act.wait_ge(ln_done.sem, ln_done.at(DEPTH, 1))
            act.activation(r0, r0, ACT.Exp, scale=-0.5).then_inc(r0_done.sem, 1)
            act.wait_ge(const_in, 48)
            for t in range(KD):
                act.wait_ge(y_done.sem, y_done.at(DEPTH, t + 1))
                act.activation(conv[:, t, :], sq[:, t % 2, :], ACT.Copy, scale=fin_g[:, t:t + 1])\
                    .then_inc(nhi_done.sem, 1)

        @block.vector
        def _(dve):
            pos_i = work[64:96, 2, :].bitcast(I32)
            pos, ang, kt = work[64:96, 3, :], work[64:96, 4, :], work[64:96, 5, :]
            steps = [0]

            def prep(ins):
                steps[0] += 1
                ins.then_inc(const_done, 1)
                dve.wait_ge(const_done, 3 + steps[0])

            dve.wait_ge(const_in, 48)
            dve.wait_ge(const_done, 3)
            prep(dve.tensor_copy(pos, pos_i))
            prep(dve.tensor_scalar(ang, pos, freq[64:96, 0:1], None, ALU.mult))
            for which, (quarter, out_t) in enumerate(((0.0, work[64:96, 0, :]), (0.25, work[64:96, 1, :]))):
                prep(dve.tensor_scalar(kt, ang, float(1 / TWO_PI), quarter, ALU.mult, ALU.add))
                prep(dve.tensor_scalar(kt, kt, ROUND, None, ALU.add))
                prep(dve.tensor_scalar(kt, kt, ROUND, None, ALU.subtract))
                prep(dve.scalar_tensor_tensor(out=out_t, in0=kt, scalar=-PI_A, in1=ang, op0=ALU.mult, op1=ALU.add))
                prep(dve.scalar_tensor_tensor(out=out_t, in0=kt, scalar=-PI_B, in1=out_t, op0=ALU.mult, op1=ALU.add))
                prep(dve.scalar_tensor_tensor(out=out_t, in0=kt, scalar=-PI_C, in1=out_t, op0=ALU.mult, op1=ALU.add))
                if quarter:
                    prep(dve.tensor_scalar(out_t, out_t, float(np.pi / 2), None, ALU.add))
                prep(dve.tensor_scalar(out_t, out_t, -PI_IN, PI_IN, ALU.max, ALU.min))
                dve.sem_inc(trig_dve, 1)
            dve.wait_ge(trig_act, 2)
            prep(dve.tensor_scalar(trig[64:96, 1, :], trig[64:96, 1, :], freq[64:96, 1:2], None, ALU.mult))
            dve.wait_ge(x_in, 16)
            dve.sem_inc(x_ready.sem, 8)
            dve.sem_inc(scaled.sem, scaled.start)

            def adds(l, m):
                n = NORM_COLS[m]
                for t in range(1, NORM_TILES[m]):
                    dve.wait_ge(sq_done.sem, sq_done.at(l, TILE0[m] + t + 1))
                    if t >= 2:
                        dve.wait_ge(add_done.sem, add_done.at(l, ADD0[m] + t - 1))
                    dve.tensor_tensor(acc[:, 0:n], acc[:, 0:n], sq[:, (t - 1) % 2, 0:n], ALU.add)\
                        .then_inc(add_done.sem, 1)

            def layer_tools(l):
                count = [0]

                def need(s, n):
                    dve.wait_ge(s.sem, s.at(l, n))

                def link(ins):
                    count[0] += 1
                    ins.then_inc(dve_step.sem, 1)
                    dve.wait_ge(dve_step.sem, dve_step.at(l, count[0]))

                def mean_square(m, bank, v=nv):
                    n = NORM_COLS[m]
                    need(ssq_done, m + 1)
                    dve.tensor_scalar(v[:, 0:n], ps[bank][:, 0:n], 1.0 / NORM_DIM[m], EPS, ALU.mult, ALU.add)\
                        .then_inc(nv_done.sem, 1)

                def newton(m, nv=nv):
                    n = NORM_COLS[m]
                    a, v, r = rs[:, 0:n], nv[:, 0:n], r0[:, 0:n]
                    need(r0_done, m + 1)
                    link(dve.tensor_tensor(a, r, r, ALU.mult))
                    link(dve.scalar_tensor_tensor(out=a, in0=a, scalar=-0.5, in1=v, op0=ALU.mult, op1=ALU.mult))
                    link(dve.scalar_tensor_tensor(out=a, in0=a, scalar=1.5, in1=r, op0=ALU.add, op1=ALU.mult))

                def apply(m, src, hi, lo):
                    n = NORM_COLS[m]

                    def y(t):
                        if t >= 2:
                            need(nlo_done, TILE0[m] + t - 1)
                        dve.tensor_tensor(sq[:, t % 2, 0:n], src(t), rs[:, 0:n], ALU.mult).then_inc(y_done.sem, 1)

                    y(0)
                    for t in range(NORM_TILES[m]):
                        if t + 1 < NORM_TILES[m]:
                            y(t + 1)
                        need(nhi_done, TILE0[m] + t + 1)
                        dve.scalar_tensor_tensor(out=lo(t), in0=sq[:, t % 2, 0:n],
                                                 scalar=par[:, GAIN[m] + t:GAIN[m] + t + 1], in1=hi(t).bitcast(F32),
                                                 op0=ALU.mult, op1=ALU.subtract).then_inc(nlo_done.sem, 1)

                def small_root(i, out=sm_t):
                    need(s_r0, i + 1)
                    link(dve.tensor_tensor(sm_t, sm_r, sm_r, ALU.mult))
                    link(dve.scalar_tensor_tensor(out=sm_t, in0=sm_t, scalar=-0.5, in1=sm_v, op0=ALU.mult, op1=ALU.mult))
                    link(dve.scalar_tensor_tensor(out=out, in0=sm_t, scalar=1.5, in1=sm_r, op0=ALU.add, op1=ALU.mult))

                return need, link, mean_square, newton, apply, small_root, count

            half_turn = [(i + 16) % 32 for i in range(32)]

            def layer(l):
                need, link, mean_square, newton, apply, small_root, count = layer_tools(l)

                def lows_and_adds(m):
                    for t in range(KD):
                        need(nhi_done, TILE0[m] + t + 1)
                        dve.scalar_tensor_tensor(out=h_lo[:, t, :], in0=x[:, t, :],
                                                 scalar=par[:, GAIN[m] + t:GAIN[m] + t + 1],
                                                 in1=h_hi[:, t, :].bitcast(F32), op0=ALU.mult, op1=ALU.subtract)\
                            .then_inc(nlo_done.sem, 1)
                        if t >= 1:
                            need(sq_done, TILE0[m] + t + 1)
                            if t >= 2:
                                need(add_done, ADD0[m] + t - 1)
                            dve.tensor_tensor(acc, acc, sq[:, (t - 1) % 2, :], ALU.add).then_inc(add_done.sem, 1)

                lows_and_adds(MIX)
                mean_square(MIX, 4)
                need(ssq_tok, 1)
                dve.tensor_scalar(sm_v, ps[5][:, 0:TT], 1.0 / D, EPS, ALU.mult, ALU.add).then_inc(s_v.sem, 1)
                newton(MIX)
                small_root(0, rs_tok)
                need(used, B_LAT + 4)
                for j in range(3):
                    dve.tensor_tensor(lat[:, j, :], ps[j][:, :], rs, ALU.mult).then_inc(lat_done.sem, 1)
                dve.tensor_tensor(lat[64:96, 3, :], ps[3][64:96, :], rs[64:96, :], ALU.mult).then_inc(lat_done.sem, 1)
                need(lat_done, 4)
                dve.sem_inc(dve_passed, 1)
                key = lat[64:96, 3, :]
                link(dve.stream_shuffle(rot[64:96, 1, :], key, half_turn))
                link(dve.tensor_tensor(rot[64:96, 1, :], rot[64:96, 1, :], trig[64:96, 1, :], ALU.mult))
                link(dve.tensor_tensor(rot[64:96, 2, :], key, trig[64:96, 0, :], ALU.mult))
                dve.tensor_tensor(rot[64:96, 2, :], rot[64:96, 2, :], rot[64:96, 1, :], ALU.add)\
                    .then_inc(kpe_ready.sem, 1)
                adds(l, NQ)
                for p in range(2):
                    need(kpe_hi, p + 1)
                    link(dve.tensor_tensor(k_lo[64:96, p, :], rot[64:96, 2, :], k_hi[64:96, p, :].bitcast(F32),
                                           ALU.subtract))
                mean_square(NQ, 0)
                mean_square(NKV, 1, nv_kv)
                newton(NQ)
                apply(NQ, lambda t: lat[:, t, :], lambda t: cq_hi[:, t, :], lambda t: cq_lo[:, t, :])
                newton(NKV, nv_kv)
                apply(NKV, lambda t: lat[:, 2, :], lambda t: ckv_hi[:, t, :], lambda t: ckv_lo[:, t, :])
                for t in range(TT):
                    need(vh_done, t + 1)
                    dve.tensor_tensor(v_lo[:, t, :], ps[BB[t]][:, :], v_hi[:, t, :].bitcast(F32), ALU.subtract)\
                        .then_inc(vl_done.sem, 1)

                def q_part(h):
                    need(qh_done, h + 1)
                    need(pe_copied, h + 1)
                    dve.tensor_tensor(q_lo[0:64, h % 2, :], ps[0][0:64, :], q_hi[0:64, h % 2, :].bitcast(F32),
                                      ALU.subtract).then_inc(ql_done.sem, 1)
                    dve.stream_shuffle(rot[64:96, 1, :], rot[64:96, 0, :], half_turn).then_inc(shuffled.sem, 1)

                def k_part(h):
                    need(kh_done, h + 1)
                    dve.tensor_tensor(k_lo[0:64, h % 2, :], ps[0][0:64, :], k_hi[0:64, h % 2, :].bitcast(F32),
                                      ALU.subtract).then_inc(kl_done.sem, 1)

                def maximum(i, mm, exps, done, bank, n, scale):
                    c = slice(i % 4, i % 4 + 1)
                    need(mm, i + 1)
                    link(dve.reduce_max(mx[:, c], ps[bank + i % 2][:, 0:n], AXX))
                    dve.tensor_scalar(nmx[:, c], mx[:, c], -scale, None, ALU.mult).then_inc(done.sem, 1)

                def recip(i, exps, done):
                    c = slice(i % 4, i % 4 + 1)
                    need(exps, i + 1)
                    dve.reciprocal(rin[:, c], sums[:, c]).then_inc(done.sem, 1)

                def amax(i):
                    maximum(i, score_mm, exp_done, nmax_done, 2, SEQ, SCALE)

                def turned_lo(i):
                    need(pth_done, i + 1)
                    h, t = divmod(i, TT)
                    c = slice(P * t, P * t + P)
                    dve.tensor_tensor(pt_lo[h % 2][:, :, c], ps[4 + i % 2][:, :].rearrange("p (k q) -> p k q", k=TT),
                                      pt_hi[h % 2][:, :, c].bitcast(F32), ALU.subtract).then_inc(ptl_done.sem, 1)

                def statistics(src, t):
                    link(dve.bn_stats(bn[:, t, :], src[:, t, :]))
                    dve.sem_inc(dve_passed, 1)
                    link(dve.bn_aggr(mv[:, t, :], bn[:, t, :]))

                def gated_heads(n):
                    for s in range(4 * n, 4 * n + 4):
                        if s < SG_HEADS - 2:
                            need(mix_mm, s // 2 + 1)
                        else:
                            need(used, B_WS + 1)
                        us = u[:, :, SG_HD * s:SG_HD * s + SG_HD]
                        dve.scalar_tensor_tensor(out=us, in0=ps[6 + (s // 2) % 2][:, (s % 2) * 256:(s % 2) * 256 + 256]
                                                 .rearrange("p (c d) -> p c d", c=TT),
                                                 scalar=par[:, C_BS + s:C_BS + s + 1], in1=us,
                                                 op0=ALU.add, op1=ALU.mult).then_inc(gated.sem, 1)

                def gate_turned(n):
                    for f in (2 * n, 2 * n + 1):
                        need(sgh_done, f + 1)
                        dve.scalar_tensor_tensor(out=h_lo[:, 4 + f, :], in0=ps[6 + f % 2][:, :],
                                                 scalar=par[:, G_SG + f:G_SG + f + 1], in1=h_hi[:, 4 + f, :].bitcast(F32),
                                                 op0=ALU.mult, op1=ALU.subtract).then_inc(sgl_done.sem, 1)

                q_part(0)
                k_part(0)
                q_part(1)
                k_part(1)
                amax(0)
                amax(1)
                recip(0, exp_done, recip_done)
                for i in range(HEADS * TT):
                    h, t = divmod(i, TT)
                    if i + 1 < HEADS * TT:
                        recip(i + 1, exp_done, recip_done)
                    if i + 2 < HEADS * TT:
                        amax(i + 2)
                    if i >= 1:
                        turned_lo(i - 1)
                    if t == 1 and 1 <= h and h + 1 < HEADS:
                        k_part(h + 1)
                    if t == 3 and h + 2 < HEADS:
                        q_part(h + 2)
                    if h == 0 and t < 2:
                        need(vg_done, 4)
                        statistics(vt, 2 * t)
                        statistics(vt, 2 * t + 1)
                        if t == 1:
                            dve.tensor_scalar(sm_v, mv[:, :, 1], EPS, None, ALU.add).then_inc(s_v.sem, 1)
                    if h == 1 and t == 0:
                        small_root(1)
                    if h in (1, 2) and t in (0, 2):
                        g = 2 * h - 2 + t // 2
                        link(dve.tensor_scalar(vt[:, g, :], vt[:, g, :], mv[:, g, 0:1], sm_t[:, g:g + 1],
                                               ALU.subtract, ALU.mult))
                        link(dve.tensor_tensor(vt[:, g, :], vt[:, g, :], ln_gb[:, 0, :], ALU.mult))
                        dve.tensor_tensor(vt[:, g, :], vt[:, g, :], ln_gb[:, 1, :], ALU.add).then_inc(vn_done.sem, 1)
                    if h in (5, 6) and t == 2:
                        gated_heads(h - 5)
                    if h == 6 and t == 3:
                        need(gated, SG_HEADS)
                        for c in range(TT):
                            statistics(u, c)
                        link(dve.tensor_tensor(sm_t, mv[:, :, 0], mv[:, :, 0], ALU.mult))
                        dve.scalar_tensor_tensor(out=sm_v, in0=sm_t, scalar=EPS, in1=mv[:, :, 1], op0=ALU.add,
                                                 op1=ALU.add).then_inc(s_v.sem, 1)
                    if h == 7 and t == 0:
                        small_root(2)
                        for c in range(TT):
                            dve.tensor_scalar(u[:, c, :], u[:, c, :], sm_t[:, c:c + 1], None, ALU.mult)\
                                .then_inc(sg_normed.sem, 1)
                    if h == 7 and t == 3:
                        gate_turned(0)
                turned_lo(HEADS * TT - 1)
                gate_turned(1)
                adds(l, MLA)
                mean_square(MLA, 2)
                newton(MLA)
                apply(MLA, lambda t: o_mla[:, t, :], lambda t: h_hi[:, t, :], lambda t: h_lo[:, t, :])
                adds(l, MTOK)
                need(used, B_OUT + 4)
                def residual(b_last, banks, t0):
                    need(used, b_last + 1)
                    for j in range(4):
                        dve.tensor_tensor(x[:, t0 + j, :], x[:, t0 + j, :], ps[banks[j]][:, :], ALU.add)\
                            .then_inc(x_ready.sem, 1)

                residual(B_OUT + 3, BB, 0)
                mean_square(MTOK, 0)
                newton(MTOK)
                apply(MTOK, lambda t: memT[:, t, :], lambda t: mt_hi[:, t, :], lambda t: mt_lo[:, t, :])
                residual(B_OUT + 7, BA, 4)
                adds(l, MEM)
                def values_lo(g):
                    for j in range(MT):
                        need(vmh_done, MT * g + j + 1)
                        dve.tensor_tensor(vm_lo[:, 2 * j + g, :], ps[4 + 2 * g + j][:, :],
                                          vm_hi[:, 2 * j + g, :].bitcast(F32), ALU.subtract).then_inc(vml_done.sem, 1)

                for g in range(2):
                    for j in range(4):
                        need(kmh_done, 4 * g + j + 1)
                        dve.tensor_tensor(km_lo[:, 4 * g + j, :], ps[(BB, BA)[g][j]][:, 0:N_MEM],
                                          km_hi[:, 4 * g + j, :].bitcast(F32), ALU.subtract).then_inc(kml_done.sem, 1)
                values_lo(0)
                mean_square(MEM, 0)
                newton(MEM)
                apply(MEM, lambda t: x[:, t, :], lambda t: h_hi[:, t, :], lambda t: h_lo[:, t, :])
                values_lo(1)
                for g in range(2):
                    for j in range(4):
                        need(qmh_done, 4 * g + j + 1)
                        dve.tensor_tensor(qm_lo[:, 4 * g + j, :], ps[(BA, BB)[g][j]][:, :],
                                          qm_hi[:, 4 * g + j, :].bitcast(F32), ALU.subtract).then_inc(qml_done.sem, 1)

                def mmax(i):
                    maximum(i, mscore_mm, mexp_done, mnmax_done, 0, N_MEM, MEM_SCALE)

                def mturned_lo(i):
                    need(pmh_done, i + 1)
                    c = slice(P * (i % TT), P * (i % TT) + P)
                    dve.tensor_tensor(pm_lo[:, :, c], ps[2 + i % 2][:, 0:MT * P].rearrange("p (k q) -> p k q", k=MT),
                                      pm_hi[:, :, c].bitcast(F32), ALU.subtract).then_inc(pml_done.sem, 1)

                def outputs(h):
                    for j in range(2):
                        need(omh_done, 2 * h + j + 1)
                        dve.tensor_tensor(h_lo[:, 2 * h + j, :], ps[4 + 2 * (h % 2) + j][:, :],
                                          h_hi[:, 2 * h + j, :].bitcast(F32), ALU.subtract).then_inc(oml_done.sem, 1)

                mmax(0)
                mmax(1)
                recip(0, mexp_done, mrecip_done)
                for i in range(MEM_HEADS * TT):
                    h, t = divmod(i, TT)
                    if i + 1 < MEM_HEADS * TT:
                        recip(i + 1, mexp_done, mrecip_done)
                    if i + 2 < MEM_HEADS * TT:
                        mmax(i + 2)
                    if i >= 1:
                        mturned_lo(i - 1)
                    if t == 2 and h >= 1:
                        outputs(h - 1)
                mturned_lo(MEM_HEADS * TT - 1)
                outputs(MEM_HEADS - 1)
                residual(B_MO + 3, BA, 0)
                residual(B_MO + 7, BB, 4)
                lows_and_adds(FFN)
                mean_square(FFN, 4)
                newton(FFN)

                def up_group(half, r, i, step):
                    g = sum(GROUPS[:half]) + r
                    bank = 4 * (r % 2)

                    def col(base):
                        return par[:, bass.ds(i * (2 * step) + base, 1)] if step else par[:, base:base + 1]

                    def scale(j, s):
                        dve.tensor_tensor(lin[:, 2 * j + s, :], ps[bank + 2 * s + j][:, :], rs, ALU.mult)\
                            .then_inc(scaled.sem, 1)

                    def outer(j, s):
                        n = 4 * g + 2 * j + s
                        dve.wait_ge(tap1.sem, l * (2 * FT) + i * (4 * step) + (n + 1))
                        c, a = conv[:, bank + 2 * j + s, :], lin[:, 2 * j + s, :]
                        at = s * FT + 2 * g + j
                        dve.scalar_tensor_tensor(out=c[:, 1:SEQ], in0=a[:, 0:SEQ - 1], scalar=col(C_W0 + at),
                                                 in1=c[:, 1:SEQ], op0=ALU.mult, op1=ALU.add).then_inc(taps.sem, 1)
                        dve.wait_ge(taps.sem, l * (4 * FT) + i * (8 * step) + (2 * n + 1 + taps.start))
                        dve.scalar_tensor_tensor(out=c[:, 0:SEQ - 1], in0=a[:, 1:SEQ], scalar=col(C_W2 + at),
                                                 in1=c[:, 0:SEQ - 1], op0=ALU.mult, op1=ALU.add).then_inc(taps.sem, 1)

                    def product(j):
                        n = 2 * g + j
                        dve.wait_ge(silu_done.sem, l * FT + i * (2 * step) + (n + 1))
                        dve.wait_ge(taps.sem, l * (4 * FT) + i * (8 * step) + (4 * n + 4 + taps.start))
                        c = conv[:, bank + 2 * j, :]
                        dve.tensor_tensor(c, c, conv[:, bank + 2 * j + 1, :], ALU.mult).then_inc(prod_done.sem, 1)

                    def low(j):
                        dve.wait_ge(fh_done.sem, l * FT + i * (2 * step) + (2 * g + j + 1))
                        at = bass.ds(i * (2 * step) + (2 * r + j), 1) if step else slice(2 * r + j, 2 * r + j + 1)
                        dve.tensor_tensor(hid_lo[:, at, :], conv[:, bank + 2 * j:bank + 2 * j + 1, :],
                                          hid_hi[:, at, :].bitcast(F32), ALU.subtract).then_inc(fl_done.sem, 1)

                    dve.wait_ge(used.sem, l * BLOCKS + i * (4 * step) + (B_UP[half] + 4 * r + 4 + SPLIT))
                    if g:
                        dve.wait_ge(taps.sem, l * (4 * FT) + i * (8 * step) + 8 * g)
                    for j in range(2):
                        for s in range(2):
                            scale(j, s)
                    outer(0, 0)
                    outer(0, 1)
                    outer(1, 0)
                    product(0)
                    outer(1, 1)
                    product(1)
                    low(0)
                    low(1)

                dve.sem_inc(dve_passed, 1)
                for half in range(2):
                    with dve.Fori(0, GROUPS[half] // 2) as i:
                        for r in range(2):
                            up_group(half, r, i, 2)
                    if GROUPS[half] % 2:
                        up_group(half, GROUPS[half] - 1, 0, 0)
                    for hf in range(2):
                        residual(B_DN[half] + GROUPS[half] * (hf + 1) - 1, ((BA, BB), (BB, BA))[half][hf], 4 * hf)
                assert count[0] == N_STEP, count[0]

            with dve.Fori(0, DEPTH) as l:
                layer(l)

            need, link, mean_square, newton, apply, small_root, count = layer_tools(DEPTH)
            adds(DEPTH, MIX)
            mean_square(MIX, 4)
            newton(MIX)
            for t in range(KD):
                if t >= 2:
                    need(nhi_done, t - 1)
                dve.tensor_tensor(sq[:, t % 2, :], x[:, t, :], rs, ALU.mult).then_inc(y_done.sem, 1)

        @block.tensor
        def _(pe):
            pe.wait_ge(const_done, 3)

            def layer(l):
                def need(s, n):
                    pe.wait_ge(s.sem, s.at(l, n))

                def block_ready(b, i=0, step=0):
                    pe.wait_ge(lo_done.sem, l * BLOCKS + i * step + (b + 1))

                def product3(out, a_hi, a_lo, b_hi, b_lo, first, last):
                    pe.matmul(out, a_hi, b_hi, start=first, stop=False)
                    pe.matmul(out, a_hi, b_lo, start=False, stop=False)
                    return pe.matmul(out, a_lo, b_hi, start=False, stop=last)

                def sum_squares(m, bank, acc_t=acc):
                    n = NORM_COLS[m]
                    if NORM_TILES[m] > 1:
                        need(add_done, ADD0[m + 1])
                    else:
                        need(sq_done, TILE0[m] + 1)
                    pe.matmul(ps[bank][:, 0:n], ones[:, :], acc_t[:, 0:n], start=True, stop=True)\
                        .then_inc(ssq_done.sem, 1)

                def halves(b, width):
                    s = b % SPLIT
                    return (w_hi[:, s, :].rearrange("p (k c) -> p k c", c=width),
                            w_lo[:, s, :].rearrange("p (k c) -> p k c", c=width))

                def project(b0, banks, x_hi, x_lo, ready, n=SEQ, cols=None, blocks=4, i=0, step=0,
                            between=None, norm_after=None, order=None):
                    order = order or list(range(blocks))
                    for n_kp, kp in enumerate(order):
                        block_ready(b0 + n_kp, i, step)
                        wh, wl = halves(b0 + n_kp, 512)
                        if between and n_kp == (blocks - 1 if norm_after is None else norm_after):
                            between()
                        for jk in range(2):
                            k = 2 * kp + jk
                            ready(k)
                            for j in range(len(banks)):
                                c = cols[j] if cols else slice(P * j, P * j + P)
                                last = product3(ps[banks[j]][0:c.stop - c.start, 0:n], wh[:, jk, c], wl[:, jk, c],
                                                x_hi[:, k, 0:n], x_lo[:, k, 0:n],
                                                n_kp == 0 and jk == 0, n_kp == blocks - 1 and jk == 1)
                        last.then_inc(used.sem, 1)

                def project_tokens(b0, banks, x_hi, x_lo, ready):
                    for kp in range(4):
                        block_ready(b0 + kp)
                        wh, wl = halves(b0 + kp, 512)
                        for jk in range(2):
                            k = 2 * kp + jk
                            ready(k)
                            for j in range(len(banks)):
                                c = slice(P * j, P * j + P)
                                last = product3(ps[banks[j]][:, :], x_hi[:, k, c], x_lo[:, k, c],
                                                wh[:, jk, :], wl[:, jk, :], k == 0, k == 7)
                        last.then_inc(used.sem, 1)

                def normed(m):
                    return lambda k: need(nlo_done, TILE0[m] + k + 1)

                def mixers_norm():
                    sum_squares(MIX, 4)
                    for t in range(TT):
                        last = pe.matmul(ps[5][:, t:t + 1], acc[:, P * t:P * t + P], ones[:, 0:1], start=True, stop=True)
                    last.then_inc(ssq_tok.sem, 1)

                project(B_LAT, BA, h_hi, h_lo, normed(MIX),
                        cols=[slice(0, 128), slice(128, 256), slice(256, 384), slice(320, 416)],
                        between=mixers_norm)
                need(s_v, 1)
                project_tokens(B_U, BB, h_hi, h_lo, lambda k: None)
                need(lat_done, 4)
                sum_squares(NQ, 0)
                sum_squares(NKV, 1, acc_t=sq[:, 1, :])
                need(nv_done, NKV + 1)
                project_tokens(B_V, BA, h_hi, h_lo, lambda k: None)
                block_ready(B_WV)
                wh, wl = halves(B_WV, 512)
                need(nlo_done, TILE0[NKV] + 1)
                need(u_done, 4)
                for t in range(TT):
                    c = slice(P * t, P * t + P)
                    last = product3(ps[BB[t]][:, :], ckv_hi[:, 0, c], ckv_lo[:, 0, c], wh[:, 0, :], wl[:, 0, :],
                                    True, True)
                    if t < TT - 1:
                        last.then_inc(wv_mm.sem, 1)
                last.then_inc(used.sem, 1)

                def q_proj(h):
                    b = B_HEAD + h // 2
                    if h % 2 == 0:
                        block_ready(b)
                    wh, wl = halves(b, BLK)
                    if h == 0:
                        need(vg_done, 4)
                    else:
                        need(kl_done, h)
                    for k in range(2):
                        c = slice(k * 2 * QK + (h % 2) * QK, k * 2 * QK + (h % 2) * QK + QK)
                        last = product3(ps[0][0:QK, :], wh[:, 0, c], wl[:, 0, c], cq_hi[:, k, :], cq_lo[:, k, :],
                                        k == 0, k == 1)
                    last.then_inc(qp_mm.sem, 1)

                def k_proj(h):
                    b = B_HEAD + h // 2
                    wh, wl = halves(b, BLK)
                    c = slice(4 * QK + (h % 2) * NOPE, 4 * QK + (h % 2) * NOPE + NOPE)
                    need(ql_done, h + 1)
                    pe.matmul(ps[0][0:NOPE, :], wh[:, 0, c], ckv_hi[:, 0, :], start=True, stop=False)
                    pe.matmul(ps[0][0:NOPE, :], wl[:, 0, c], ckv_hi[:, 0, :], start=False, stop=False)
                    pe.matmul(ps[0][0:NOPE, :], wh[:, 0, c], ckv_lo[:, 0, :], start=False, stop=True)\
                        .then_inc((used if h % 2 else kp_mm).sem, 1)

                def scores(i):
                    h, t = divmod(i, TT)
                    if t == 0:
                        need(kl_done, h + 1)
                        need(pel_done, h + 1)
                    if i >= 2:
                        need(exp_done, i - 1)
                    c = slice(P * t, P * t + P)
                    product3(ps[2 + i % 2][:, :], q_hi[0:QK, h % 2, c], q_lo[0:QK, h % 2, c],
                             k_hi[0:QK, h % 2, :], k_lo[0:QK, h % 2, :], True, True).then_inc(score_mm.sem, 1)

                def turn(i):
                    need(prob_done, i + 1)
                    if i >= 2:
                        need(ptl_done, i - 1)
                    for k in range(TT):
                        last = pe.transpose(ps[4 + i % 2][:, P * k:P * k + P], e[:, i % 3, P * k:P * k + P], ident[:, :])
                    last.then_inc(turned.sem, 1)

                def attend(h):
                    need(ptl_done, TT * h + TT)
                    if h > 0:
                        need(o_done, h)
                    c = slice(VD * h, VD * h + VD)
                    for k in range(TT):
                        last = product3(ps[1][0:VD, :], v_hi[:, k, c], v_lo[:, k, c],
                                        pt_hi[h % 2][:, k, :], pt_lo[h % 2][:, k, :], k == 0, k == TT - 1)
                    last.then_inc(pv_mm.sem, 1)

                def mix(n):
                    if n == 0:
                        block_ready(B_WS)
                        need(svl_done, 4)
                        need(vl_done, 4)
                    else:
                        need(gated, 4)
                    wh, wl = halves(B_WS, P)
                    for s in range(4 * n, 4 * n + 4):
                        c = slice(SG_HD * s, SG_HD * s + SG_HD)
                        out = ps[6 + (s // 2) % 2][:, (s % 2) * 256:(s % 2) * 256 + 256]\
                            .rearrange("p (c d) -> p c d", c=TT)
                        last = product3(out, wh[:, s, :], wl[:, s, :], sv_hi[:, :, c], sv_lo[:, :, c], True, True)
                        if s % 2:
                            last.then_inc((mix_mm if s < SG_HEADS - 1 else used).sem, 1)

                def turn_gated(n):
                    if n == 0:
                        need(sg_normed, 4)
                    else:
                        need(sgl_done, 2)
                    for f in (2 * n, 2 * n + 1):
                        for t in range(TT):
                            last = pe.transpose(ps[6 + f % 2][:, P * t:P * t + P], u[:, t, P * f:P * f + P], ident[:, :])
                    last.then_inc(sg_turned.sem, 1)

                need(nlo_done, TILE0[NQ] + 2)
                q_proj(0)
                k_proj(0)
                q_proj(1)
                k_proj(1)
                scores(0)
                scores(1)
                need(vl_done, 4)
                for i in range(HEADS * TT):
                    h, t = divmod(i, TT)
                    if i + 2 < HEADS * TT:
                        scores(i + 2)
                    turn(i)
                    if t == 0 and 1 <= h and h + 1 < HEADS:
                        k_proj(h + 1)
                    if t == 1 and h >= 1:
                        attend(h - 1)
                    if t == 1 and h in (5, 6):
                        mix(h - 5)
                    if t == 2 and h + 2 < HEADS:
                        q_proj(h + 2)
                    if t == 2 and h == HEADS - 1:
                        turn_gated(0)
                attend(HEADS - 1)
                turn_gated(1)

                def mixed(k):
                    if k < 4:
                        need(nlo_done, TILE0[MLA] + k + 1)
                    else:
                        need(sgl_done, k - 3)

                need(sgl_done, 4)
                project(B_OUT, BB, h_hi, h_lo, mixed, order=[2, 3, 0, 1], norm_after=1,
                        between=lambda: sum_squares(MLA, 2))
                sum_squares(MTOK, 0)
                need(nv_done, MTOK + 1)
                project(B_OUT + 4, BA, h_hi, h_lo, lambda k: None, order=[2, 3, 0, 1])
                need(x_ready, 4)
                project(B_MK, BB, mt_hi, mt_lo, normed(MTOK), n=N_MEM)
                need(x_ready, 8)
                project(B_MK + 4, BA, mt_hi, mt_lo, lambda k: None, n=N_MEM)
                need(kml_done, 4)
                project_tokens(B_MV, (4, 5), mt_hi, mt_lo, lambda k: None)
                need(kml_done, 8)
                sum_squares(MEM, 0)
                project_tokens(B_MV + 4, (6, 7), mt_hi, mt_lo, lambda k: None)
                project(B_MQ, BA, h_hi, h_lo, normed(MEM))
                need(vml_done, 4)
                project(B_MQ + 4, BB, h_hi, h_lo, lambda k: None)

                def mscores(i):
                    h, t = divmod(i, TT)
                    if i >= 2:
                        need(mexp_done, i - 1)
                    c = slice(P * t, P * t + P)
                    for k in range(2):
                        f = 2 * h + k
                        last = product3(ps[i % 2][:, 0:N_MEM], qm_hi[:, f, c], qm_lo[:, f, c],
                                        km_hi[:, f, :], km_lo[:, f, :], k == 0, k == 1)
                    last.then_inc(mscore_mm.sem, 1)

                def mturn(i):
                    need(mprob_done, i + 1)
                    if i >= 2:
                        need(pml_done, i - 1)
                    for k in range(MT):
                        last = pe.transpose(ps[2 + i % 2][:, P * k:P * k + P], e[:, i % 3, P * k:P * k + P], ident[:, :])
                    last.then_inc(mturned.sem, 1)

                def mattend(h):
                    need(pml_done, TT * h + TT)
                    if h >= 2:
                        need(oml_done, 2 * h - 2)
                    for j in range(2):
                        f = 2 * h + j
                        c = slice((f % 4) * P, (f % 4) * P + P)
                        for k in range(MT):
                            at = 2 * k + f // 4
                            last = product3(ps[4 + 2 * (h % 2) + j][:, :], vm_hi[:, at, c], vm_lo[:, at, c],
                                            pm_hi[:, k, :], pm_lo[:, k, :], k == 0, k == MT - 1)
                        last.then_inc(mpv_mm.sem, 1)

                need(qml_done, 8)
                mscores(0)
                mscores(1)
                for i in range(MEM_HEADS * TT):
                    h, t = divmod(i, TT)
                    if i + 2 < MEM_HEADS * TT:
                        mscores(i + 2)
                    mturn(i)
                    if t == 0 and h >= 1:
                        mattend(h - 1)
                mattend(MEM_HEADS - 1)
                project(B_MO, BA, h_hi, h_lo, lambda k: need(oml_done, k + 1))
                project(B_MO + 4, BB, h_hi, h_lo, lambda k: None)

                def ffn_norm():
                    need(x_ready, 16)
                    sum_squares(FFN, 4)

                need(x_ready, 12)

                def up_group(half, r, i, step, **first):
                    g = sum(GROUPS[:half]) + r
                    bank = 4 * (r % 2)
                    pe.wait_ge(scaled.sem, l * (2 * FT) + i * (4 * step) + (4 * (g - 1) + scaled.start))
                    project(B_UP[half] + 4 * r, tuple(range(bank, bank + 4)), h_hi, h_lo,
                            normed(FFN) if first else lambda k: None, i=i, step=4 * step, **first)

                for half in range(2):
                    peeled = 0
                    if half == 0:
                        up_group(0, 0, 0, 0, between=ffn_norm)
                        need(nv_done, FFN + 1)
                        up_group(0, 1, 0, 0)
                        peeled = 2
                    else:
                        pe.sem_inc(pe_passed, 1)
                    with pe.Fori(0, (GROUPS[half] - peeled) // 2) as i:
                        for r in range(peeled, peeled + 2):
                            up_group(half, r, i, 2)
                    if GROUPS[half] % 2:
                        up_group(half, GROUPS[half] - 1, 0, 0)
                    g0 = sum(GROUPS[:half])
                    for hf in range(2):
                        need(scaled, 4 * (g0 + GROUPS[half] - 1 + hf))
                        project(B_DN[half] + GROUPS[half] * hf, ((BA, BB), (BB, BA))[half][hf], hid_hi, hid_lo,
                                (lambda k: need(fl_done, 2 * g0 + k + 1)) if hf == 0 else (lambda k: None),
                                blocks=GROUPS[half])
                    if half == 0:
                        need(x_ready, 24)

            with pe.Fori(0, DEPTH) as l:
                layer(l)
            pe.wait_ge(add_done.sem, add_done.at(DEPTH, KD - 1))
            pe.matmul(ps[4][:, :], ones[:, :], acc, start=True, stop=True).then_inc(ssq_done.sem, 1)


def _pack(w, c0, width):
    k = w.shape[0] // (2 * P)
    return w[:, c0:c0 + width].reshape(k, 2, P, width).transpose(0, 2, 1, 3).reshape(k, P, 2 * width)


def _weight_blocks(w_in, w_uq, w_ukv, w_s, w_out, w_mkv, w_mq, w_mo, w_up, w_down):
    out = np.zeros((BLOCKS, P, BLK), np.float32)
    c3 = Q_LORA + KV_LORA + ROPE
    for k in range(2):
        out[B_LAT:B_LAT + 4, :, 512 * k:512 * k + c3] = \
            w_in[:, 0:c3].reshape(4, 2, P, c3)[:, k]
    out[B_U:B_U + 4] = _pack(w_in, c3, SG)
    out[B_V:B_V + 4] = _pack(w_in, c3 + SG, SG)
    ukv = w_ukv.reshape(KV_LORA, HEADS, NOPE + VD)
    out[B_WV, :, 0:HEADS * VD] = ukv[:, :, NOPE:].reshape(KV_LORA, HEADS * VD)
    uq = w_uq.reshape(2, P, HEADS, QK)
    for p in range(HEADS // 2):
        for k in range(2):
            out[B_HEAD + p, :, 2 * QK * k:2 * QK * (k + 1)] = uq[k, :, 2 * p:2 * p + 2, :].reshape(P, 2 * QK)
        out[B_HEAD + p, :, 4 * QK:4 * QK + 2 * NOPE] = ukv[:, 2 * p:2 * p + 2, 0:NOPE].reshape(P, 2 * NOPE)
    out[B_WS] = w_s.transpose(2, 0, 1).reshape(P, SG_HEADS * P)
    for base, w, c in ((B_MK, w_mkv, 0), (B_MV, w_mkv, D), (B_MQ, w_mq, 0), (B_MO, w_mo, 0)):
        for g in range(2):
            out[base + 4 * g:base + 4 * g + 4] = _pack(w, c + 512 * g, 512)
    for g in range(2):
        out[B_OUT + 4 * g:B_OUT + 4 * g + 4] = _pack(w_out, 512 * g, 512)[[2, 3, 0, 1]]
    g = 0
    for half in range(2):
        for r in range(GROUPS[half]):
            cols = np.concatenate([w_up[:, 256 * g:256 * g + 256], w_up[:, D_FF + 256 * g:D_FF + 256 * g + 256]], 1)
            out[B_UP[half] + 4 * r:B_UP[half] + 4 * r + 4] = _pack(cols, 0, 512)
            g += 1
        rows = w_down[256 * sum(GROUPS[:half]):256 * sum(GROUPS[:half + 1])]
        for hf in range(2):
            n = GROUPS[half]
            out[B_DN[half] + n * hf:B_DN[half] + n * (hf + 1)] = _pack(rows, 512 * hf, 512)
    return out


def _columns(v):
    return v.reshape(-1, P).T


def kernel(**inputs):
    import concourse.bacc as bacc
    from concourse.bass_utils import run_bass_kernel_spmd

    a = {k: np.asarray(v) for k, v in inputs.items()}
    blocks = np.concatenate([
        _weight_blocks(*(a[n][l] for n in ("w_in", "w_uq", "w_ukv", "sg_w_s", "w_out", "w_mkv", "w_mq", "w_mo",
                                           "w_up", "w_down"))) for l in range(DEPTH)])
    par = np.stack([np.concatenate(
        [_columns(a[n][l]) for n in ("norm_mix_g", "q_norm_g", "kv_norm_g", "out_norm_mla_g", "out_norm_sg_g",
                                     "mem_norm_g", "norm_mem_g", "norm_ffn_g")]
        + [a["sg_b_s"][l].T] + [_columns(a["conv_w"][l, k]) for k in range(3)] + [_columns(a["conv_b"][l])], 1)
        for l in range(DEPTH)])
    half = ROPE // 2
    inv = np.float32(10000.0) ** (-np.arange(half, dtype=np.float32) / np.float32(half))
    freq = np.zeros((P, 2), np.float32)
    freq[64:80, 0] = freq[80:96, 0] = inv
    freq[64:80, 1], freq[80:96, 1] = -1.0, 1.0
    arrays = {
        "blocks": blocks,
        "xT": np.ascontiguousarray(a["x"][0].T.reshape(KD, P, SEQ).transpose(1, 0, 2)),
        "memT": np.ascontiguousarray(a["mem"][0].T.reshape(KD, P, N_MEM).transpose(1, 0, 2)),
        "pos": np.ascontiguousarray(a["positions"]),
        "par": np.ascontiguousarray(par),
        "ln": np.ascontiguousarray(np.concatenate([a["sg_ln_g"], a["sg_ln_b"]], 1)),
        "fin": np.ascontiguousarray(_columns(a["final_norm_g"])),
        "freq": freq,
    }
    nc = bacc.Bacc("TRN2", target_bir_lowering=False, num_devices=1)
    args = [nc.dram_tensor(f"{n}_d", v.shape, mybir.dt.from_np(v.dtype), kind="ExternalInput").ap()
            for n, v in arrays.items()]
    out = nc.dram_tensor("outT_d", (P, KD, SEQ), F32, kind="ExternalOutput").ap()
    encoder_program(nc, *args, out)
    r = run_bass_kernel_spmd(nc, [{f"{n}_d": v for n, v in arrays.items()}], core_ids=[0])
    outT = r.results[0]["outT_d"]
    return np.ascontiguousarray(outT.transpose(1, 0, 2).reshape(D, SEQ).T)[None]
```

```python
import numpy as np
from contextlib import ExitStack

import concourse.bass as bass
from concourse import mybir

F32 = mybir.dt.float32
F32R = mybir.dt.float32r
I32 = mybir.dt.int32
ALU = mybir.AluOpType
ACT = mybir.ActivationFunctionType
AXX = mybir.AxisListType.X

P = 128
DEPTH, SEQ, D, N_MEM = 2, 512, 1024, 256
KD = D // P
TT = SEQ // P
EPS = 1e-6
HEADS, NOPE, ROPE, VD = 8, 64, 32, 64
QK = NOPE + ROPE
Q_LORA, KV_LORA = 256, 128
SG, SG_HEADS, SG_HD = 512, 8, 64
MEM_HEADS, MEM_HD = 4, 256
MT = N_MEM // P
D_FF = 2816
FT = D_FF // P
SCALE = float(QK) ** -0.5
MEM_SCALE = float(MEM_HD) ** -0.5

BLK = 1024
RAW, SPLIT = 4, 4
AHEAD = 3
B_LAT = 0
B_U = B_LAT + 4
B_WV = B_U + 4
B_V = B_WV + 2
B_HEAD = (B_WV + 1, B_V + 4, B_V + 5, B_V + 7)
B_WS = B_V + 6
B_OUT = B_V + 8
B_MK = B_OUT + 8
B_MV = B_MK + 8
B_MQ = B_MV + 8
B_MO = B_MQ + 8
B_UP = (B_MO + 8, B_MO + 8 + 24 + 12)
B_DN = (B_UP[0] + 24, B_UP[1] + 20)
GROUPS = (6, 5)
EARLY = 2
BLOCKS = B_DN[1] + 10
assert BLOCKS % SPLIT == 0 and BLOCKS % RAW == 0

MIX, NQ, NKV, MLA, MTOK, MEM, FFN = range(7)
NORM_TILES = (8, 2, 1, 4, 8, 8, 8)
NORM_DIM = (D, Q_LORA, KV_LORA, HEADS * VD, D, D, D)
NORM_COLS = (SEQ, SEQ, SEQ, SEQ, N_MEM, SEQ, SEQ)
N_NORMS = len(NORM_TILES)
WIDE = {m: i for i, m in enumerate((MIX, NKV, MLA, MTOK, FFN))}
TOK = {m: i for i, m in enumerate((MIX, NQ, MEM))}
TILE0 = tuple(sum(NORM_TILES[:m]) for m in range(N_NORMS + 1))
ADD0 = tuple(sum(n - 1 for n in NORM_TILES[:m]) for m in range(N_NORMS + 1))

Y_TILES = tuple(0 if m in (MIX, NQ, MEM, FFN) else n for m, n in enumerate(NORM_TILES))
Y0 = tuple(sum(Y_TILES[:m]) for m in range(N_NORMS + 1))

G_MIX, G_Q, G_KV, G_MLA, G_SG, G_MTOK, G_MEM, G_FFN = 0, 8, 10, 11, 15, 19, 27, 35
C_BS = 43
C_W0, C_W1, C_W2, C_B = 51, 95, 139, 183
NPAR = 227
GAIN = (G_MIX, G_Q, G_KV, G_MLA, G_MTOK, G_MEM, G_FFN)

TWO_PI = 2 * np.pi
PI_A = 6.28125
PI_B = float(np.float32(np.round((TWO_PI - PI_A) * 2 ** 20) / 2 ** 20))
PI_C = float(np.float32(TWO_PI - PI_A - PI_B))
ROUND = 1.5 * 2.0 ** 23
PI_IN = 3.1415925


MIX_STEPS = ((4, 1), (4, 3), (5, 0), (5, 2))
GATED_STEPS = ((6, 0), (6, 1), (6, 2), (6, 3))
SQUARE_STEPS = ((4, 3), (5, 3), (7, 2))
ADD_STEPS = ((6, 1), (7, 3))
STAT_STEPS = ((0, 1), (0, 2), (0, 3), (1, 0))
NORM_STEPS = ((1, 1), (1, 3), (2, 1), (3, 1))
SPLIT_STEPS = ((1, 2), (2, 0), (2, 2), (3, 2))


class Signal:

    def __init__(self, ctx, nc, name, per_layer, start=0):
        self.sem = ctx.enter_context(nc.semaphore(name))
        self.per_layer, self.start = per_layer, start

    def at(self, layer, n, later=0):
        return layer * self.per_layer + (n + self.start + later * self.per_layer)


def encoder_program(nc, blocks_d, xT_d, memT_d, pos_d, par_d, ln_d, fin_d, freq_d, out_d):
    with ExitStack() as ctx:
        def sb(name, shape, dt=F32):
            return ctx.enter_context(nc.sbuf_tensor(name, shape, dt))

        def sig(name, per_layer, start=0):
            return Signal(ctx, nc, name, per_layer, start)

        x = sb("x", [P, KD, SEQ])
        h_hi = sb("h_hi", [P, KD, SEQ], F32R)
        h_lo = sb("h_lo", [P, KD, SEQ], F32R)
        raw = sb("raw", [P, RAW, BLK])
        w_hi = sb("w_hi", [P, SPLIT, BLK], F32R)
        w_lo = sb("w_lo", [P, SPLIT, BLK], F32R)
        arena = sb("arena", [P, 32, SEQ], F32R)
        work = sb("work", [P, 18, SEQ])
        trig = sb("trig", [P, 2, SEQ])
        par = sb("par", [P, NPAR])
        mix_g = sb("mix_g", [P, (DEPTH + 1) * KD])
        freq = sb("freq", [P, 4])
        ones = sb("ones", [P, P])
        ident = sb("ident", [P, P])
        small = sb("small", [P, 96])

        q_hi, q_lo, k_hi, k_lo = (arena[:, 2 * i:2 * i + 2, :] for i in range(4))
        v_hi, v_lo = arena[:, 8:12, :], arena[:, 12:16, :]
        pt_hi = (arena[:, 16:20, :], h_hi[:, 0:4, :])
        pt_lo = (arena[:, 20:24, :], h_lo[:, 0:4, :])
        sv_hi, sv_lo = h_hi[:, 4:8, :], h_lo[:, 4:8, :]
        cq_hi, cq_lo = arena[:, 24:26, :], arena[:, 26:28, :]
        ckv_hi, ckv_lo = arena[:, 28:29, :], arena[:, 29:30, :]
        km_hi = arena[:, 0:4, :].rearrange("p a (b n) -> p (a b) n", b=2)
        km_lo = arena[:, 4:8, :].rearrange("p a (b n) -> p (a b) n", b=2)
        vm_hi, vm_lo = arena[:, 8:12, :], arena[:, 12:16, :]
        mt_hi = arena[:, 16:20, :].rearrange("p a (b n) -> p (a b) n", b=2)
        mt_lo = arena[:, 20:24, :].rearrange("p a (b n) -> p (a b) n", b=2)
        qm_hi, qm_lo = arena[:, 16:24, :], arena[:, 24:32, :]
        pm_hi = (h_hi[:, 0:2, :], h_hi[:, 2:4, :])
        pm_lo = (h_lo[:, 0:2, :], h_lo[:, 2:4, :])
        hid_hi, hid_lo = arena[:, 0:12, :], arena[:, 12:24, :]
        u = work[:, 0:4, :]
        memT = work[:, 0:4, :].rearrange("p a (b n) -> p (a b) n", b=2)
        lat_kv, key = work[:, 6, :], work[64:96, 7, :]
        o_mla = work[:, 4:8, :]
        ln_gb = work[:, 6:8, :]
        acc, sq, nv, r0, rs = work[:, 8, :], work[:, 9:11, :], work[:, 11, :], work[:, 12, :], work[:, 13, :]
        nv_kv = work[:, 14, :]
        e = work[:, 8:11, :]
        em = e.rearrange("p a (b n) -> p (a b) n", b=2)
        rot = work[:, 11:14, :]
        vt = work[:, 14:18, :]
        acc_o, sq_o = work[:, 14, :], work[:, 15:17, :]
        conv = work[:, 0:8, :]
        lin = work[:, 14:18, :]
        bn = small[:, 0:24].rearrange("p (a b) -> p a b", a=4)
        mv = small[:, 24:32].rearrange("p (a b) -> p a b", a=4)
        sm_v, sm_r, sm_t = small[:, 32:36], small[:, 36:40], small[:, 40:44]
        mx, nmx, sums, rin = small[:, 44:48], small[:, 48:52], small[:, 52:56], small[:, 56:60]
        rs_tok = small[:, 60:64]
        qs, nqs = small[:, 64:68], small[:, 68:72]
        rsum = work[0:64, 11, :]
        hsum, hrec = small[:, 80:88], small[:, 88:96]
        ms, nms = small[:, 72:76], small[:, 76:80]

        ps = [ctx.enter_context(nc.psum_tensor(f"ps{i}", [P, SEQ], F32)) for i in range(8)]
        BM, BO = (0, 1, 6, 7), (4, 6, 7, 5)
        BA, BB = (0, 1, 2, 3), (4, 5, 6, 7)

        raw_in = [sig(f"raw_in{i}", 16 * BLOCKS // RAW) for i in range(RAW)]
        hi_done = sig("hi_done", BLOCKS)
        lo_done = sig("lo_done", BLOCKS)
        used = sig("used", BLOCKS, SPLIT)
        x_in = [ctx.enter_context(nc.semaphore(f"x_in{i}")) for i in range(KD // 2)]
        const_in = ctx.enter_context(nc.semaphore("const_in"))
        gain_in = [ctx.enter_context(nc.semaphore(f"gain_in{i}")) for i in range(2)]
        const_done = ctx.enter_context(nc.semaphore("const_done"))
        trig_dve = ctx.enter_context(nc.semaphore("trig_dve"))
        trig_act = ctx.enter_context(nc.semaphore("trig_act"))
        out_done = ctx.enter_context(nc.semaphore("out_done"))
        stored = ctx.enter_context(nc.semaphore("stored"))
        par_in = sig("par_in", 16)
        ln_in = sig("ln_in", 16)
        mem_in = sig("mem_in", 16)
        x_ready = sig("x_ready", 32, 8)
        sq_done = sig("sq_done", TILE0[-1])
        add_done = sig("add_done", ADD0[-1])
        ssq_done = sig("ssq_done", len(WIDE))
        nv_done = sig("nv_done", len(WIDE))
        ln_done = sig("ln_done", len(WIDE))
        r0_done = sig("r0_done", len(WIDE))
        y_done = sig("y_done", Y0[-1])
        nhi_done = sig("nhi_done", TILE0[-1])
        nlo_done = sig("nlo_done", TILE0[-1])
        ssq_tok = sig("ssq_tok", len(TOK))
        s_v = sig("s_v", 5)
        s_ln = sig("s_ln", 5)
        s_r0 = sig("s_r0", 5)
        lat_done = sig("lat_done", 2)
        kpe_ready = sig("kpe_ready", 1)
        kpe_hi = sig("kpe_hi", 2)
        u_done = sig("u_done", 4)
        vg_done = sig("vg_done", 4)
        vn_done = sig("vn_done", 4)
        svh_done = sig("svh_done", 4)
        svl_done = sig("svl_done", 4)
        v_mm = sig("v_mm", TT - 1)
        mq_mm = sig("mq_mm", 6)
        wv_mm = sig("wv_mm", TT - 1)
        vh_done = sig("vh_done", 4)
        vl_done = sig("vl_done", 4)
        qp_mm = sig("qp_mm", HEADS)
        kp_mm = sig("kp_mm", HEADS // 2)
        qh_done = sig("qh_done", HEADS)
        pe_copied = sig("pe_copied", 2 * HEADS)
        ql_done = sig("ql_done", HEADS)
        roped = sig("roped", HEADS)
        kh_done = sig("kh_done", HEADS)
        kl_done = sig("kl_done", HEADS)
        peh_done = sig("peh_done", HEADS)
        pel_done = sig("pel_done", HEADS)
        pool_step = sig("pool_step", 2 * HEADS)
        mrecip_done = sig("mrecip_done", MEM_HEADS * TT)
        score_mm = sig("score_mm", HEADS * TT)
        nmax_done = sig("nmax_done", HEADS * TT)
        exp_done = sig("exp_done", HEADS * TT)
        turned = sig("turned", HEADS * TT)
        pth_done = sig("pth_done", HEADS * TT)
        ptl_done = sig("ptl_done", HEADS * TT)
        pv_mm = sig("pv_mm", HEADS)
        rsum_done = sig("rsum_done", HEADS)
        hrec_done = sig("hrec_done", HEADS)
        spread = sig("spread", HEADS)
        o_done = sig("o_done", HEADS)
        mix_mm = sig("mix_mm", SG_HEADS // 2 - 1)
        gated = sig("gated", SG_HEADS)
        sg_normed = sig("sg_normed", 4)
        sg_turned = sig("sg_turned", 4)
        sgh_done = sig("sgh_done", 4)
        sgl_done = sig("sgl_done", 4)
        kmh_done = sig("kmh_done", 8)
        kml_done = sig("kml_done", 8)
        vmh_done = sig("vmh_done", 4)
        vml_done = sig("vml_done", 4)
        qmh_done = sig("qmh_done", 8)
        qml_done = sig("qml_done", 8)
        mscore_mm = sig("mscore_mm", MEM_HEADS * TT)
        mnmax_done = sig("mnmax_done", MEM_HEADS * TT)
        mexp_done = sig("mexp_done", MEM_HEADS * TT)
        mprob_done = sig("mprob_done", MEM_HEADS * TT)
        mturned = sig("mturned", MEM_HEADS * TT)
        pmh_done = sig("pmh_done", MEM_HEADS * TT)
        pml_done = sig("pml_done", MEM_HEADS * TT)
        mpv_mm = sig("mpv_mm", MEM_HEADS * 2)
        omh_done = sig("omh_done", 8)
        oml_done = sig("oml_done", 8)
        tap1 = sig("tap1", 2 * FT)
        taps = sig("taps", 4 * FT)
        scaled = sig("scaled", 2 * FT, 8)
        silu_done = sig("silu_done", FT)
        prod_done = sig("prod_done", FT)
        fh_done = sig("fh_done", FT)
        fl_done = sig("fl_done", FT)
        dve_passed = ctx.enter_context(nc.semaphore("dve_passed"))
        pe_passed = ctx.enter_context(nc.semaphore("pe_passed"))
        N_STEP = 114
        dve_step = sig("dve_step", N_STEP)

        def q_bank(h):
            return (4, 6)[h] if h < 2 else 4

        def k_bank(h):
            return (5, 7)[h] if h < 2 else 4

        block = ctx.enter_context(nc.Block())

        @block.sync
        def _(sp):
            for n in range(RAW):
                sp.dma_start(x[:, 2 * n:2 * n + 2, :], xT_d[:, 2 * n:2 * n + 2, :]).then_inc(x_in[n], 16)
                if n < 2:
                    sp.dma_start(raw[:, n, :], blocks_d[n]).then_inc(raw_in[n].sem, 16)
            for n in range(2, RAW):
                sp.dma_start(raw[:, n, :], blocks_d[n]).then_inc(raw_in[n].sem, 16)
            with sp.Fori(0, DEPTH * BLOCKS // RAW - 1) as i:
                for r in range(RAW):
                    sp.wait_ge(lo_done.sem, i * RAW + (r + 1))
                    sp.dma_start(raw[:, r, :],
                                 blocks_d[bass.ds(i * RAW + (r + RAW), 1), :, :].rearrange("a p n -> (a p) n"))\
                        .then_inc(raw_in[r].sem, 16)
            for t in range(KD):
                sp.wait_ge(out_done, t + 1)
                sp.dma_start(out_d[:, t, :], conv[:, t, :]).then_inc(stored, 16)
            sp.wait_ge(stored, 16 * KD)

        @block.gpsimd
        def _(gp):
            gp.memset(ones[:, :], 1.0).then_inc(const_done, 1)
            gp.memset(ident[:, :], 0.0).then_inc(const_done, 1)
            gp.wait_ge(const_done, 2)
            gp.affine_select(out=ident[:, :], in_=ident[:, :], compare_op=ALU.not_equal, fill=1.0, base=0,
                             pattern=[[-1, P]], channel_multiplier=1).then_inc(const_done, 1)

            def layer(l):
                def need(s, n):
                    gp.wait_ge(s.sem, s.at(l, n))

                steps = [0]

                def link(ins):
                    steps[0] += 1
                    ins.then_inc(pool_step.sem, 1)
                    need(pool_step, steps[0])

                def low(b, i=0, step=0):
                    gp.wait_ge(hi_done.sem, l * BLOCKS + i * step + (b + 1))
                    gp.tensor_tensor(w_lo[:, b % SPLIT, :], raw[:, b % RAW, :], w_hi[:, b % SPLIT, :].bitcast(F32),
                                     ALU.subtract).then_inc(lo_done.sem, 1)

                def lows(b0, n):
                    with gp.Fori(0, n // SPLIT) as i:
                        for r in range(SPLIT):
                            low(b0 + r, i, SPLIT)
                    for r in range(n // SPLIT * SPLIT, n):
                        low(b0 + r)

                def rotate(h):
                    need(pe_copied, 2 * h + 2)
                    link(gp.tensor_tensor(rot[64:96, 1, :], rot[64:96, 1, :], trig[64:96, 1, :], ALU.mult))
                    link(gp.tensor_tensor(rot[64:96, 2, :], rot[64:96, 0, :], trig[64:96, 0, :], ALU.mult))
                    gp.tensor_tensor(rot[64:96, 2, :], rot[64:96, 2, :], rot[64:96, 1, :], ALU.add)\
                        .then_inc(roped.sem, 1)

                def rotated_low(h):
                    need(peh_done, h + 1)
                    gp.tensor_tensor(q_lo[64:96, h % 2, :], rot[64:96, 2, :], q_hi[64:96, h % 2, :].bitcast(F32),
                                     ALU.subtract).then_inc(pel_done.sem, 1)

                def gate_low(t):
                    need(svh_done, t + 1)
                    gp.tensor_tensor(sv_lo[:, t, :], vt[:, t, :], sv_hi[:, t, :].bitcast(F32), ALU.subtract)\
                        .then_inc(svl_done.sem, 1)

                lows(0, B_V + AHEAD)
                need(lo_done, B_V + AHEAD)
                for h in range(2):
                    rotate(h)
                    rotated_low(h)
                need(pel_done, 2)
                for b in range(B_V + AHEAD, B_V + 7):
                    low(b)
                for h in range(HEADS):
                    if h % 2 == 1:
                        low(B_V + 7 + h // 2)
                    if h + 2 < HEADS:
                        need(lo_done, B_V + 7 + (h + 1) // 2)
                        rotate(h + 2)
                        if h in (2, 3):
                            need(roped, h + 3)
                            gate_low(2 * h - 4)
                            gate_low(2 * h - 3)
                            need(svl_done, 2 * h - 2)
                        rotated_low(h + 2)
                        need(pel_done, h + 3)
                lows(B_OUT + 3, BLOCKS - (B_OUT + 3))

            with gp.Fori(0, DEPTH) as l:
                layer(l)

        @block.scalar
        def _(act):
            act.sem_inc(used.sem, SPLIT)
            for n in range(DEPTH):
                act.dma_start(mix_g[:, KD * n:KD * n + KD], par_d[n, :, G_MIX:G_MIX + KD]).then_inc(gain_in[n > 0], 16)
                if n == 0:
                    act.dma_start(work[64:128, 2, :].bitcast(I32), pos_d.to_broadcast([2 * ROPE, SEQ]))\
                        .then_inc(const_in, 16)
                    act.dma_start(freq[:, :], freq_d).then_inc(const_in, 16)
            act.dma_start(mix_g[:, KD * DEPTH:KD * DEPTH + KD], fin_d).then_inc(gain_in[1], 16)

            def hi_and_square(l, m, t, x_tiles, later=0):
                act.wait_ge(x_ready.sem, x_ready.at(l, x_tiles))
                g = mix_g[:, bass.ds(l * KD + (later * KD + t), 1)] if m == MIX \
                    else par[:, GAIN[m] + t:GAIN[m] + t + 1]
                act.activation(h_hi[:, t, :], x[:, t, :], ACT.Copy, scale=g).then_inc(nhi_done.sem, 1)
                if t == 1 and m > 0:
                    act.wait_ge(nlo_done.sem, nlo_done.at(l, TILE0[m]))
                if t >= 3:
                    act.wait_ge(add_done.sem, add_done.at(l, ADD0[m] + t - 2, later))
                act.activation(acc if t == 0 else sq[:, (t - 1) % 2, :], x[:, t, :], ACT.Square)\
                    .then_inc(sq_done.sem, 1)

            act.wait_ge(gain_in[0], 16)
            for t in range(EARLY):
                hi_and_square(0, MIX, t, t + 1 - 8)
            act.wait_ge(trig_dve, 1)
            act.activation(trig[64:96, 1, :], work[64:96, 0, :], ACT.Sin).then_inc(trig_act, 1)
            act.activation(trig[64:96, 0, :], work[96:128, 0, :], ACT.Sin).then_inc(trig_act, 1)
            act.wait_ge(gain_in[1], 16 * DEPTH)

            def layer(l):
                def need(s, n):
                    act.wait_ge(s.sem, s.at(l, n))

                def split(b, i=0, step=0):
                    r = b % RAW
                    act.wait_ge(raw_in[r].sem,
                                l * (16 * BLOCKS // RAW) + i * (16 * step // RAW) + 16 * (b // RAW + 1))
                    act.wait_ge(used.sem,
                                l * BLOCKS + i * step + (b + 1))
                    act.activation(w_hi[:, b % SPLIT, :], raw[:, r, :], ACT.Copy).then_inc(hi_done.sem, 1)

                def ahead(b, i=0, step=0):
                    if b + AHEAD < BLOCKS:
                        split(b + AHEAD, i, step)

                def block_used(b):
                    need(used, b + 1)

                def squares(m, src, ready, acc_t=acc):
                    n = NORM_COLS[m]
                    for t in range(NORM_TILES[m]):
                        ready(t)
                        if t == 1 and m > 0:
                            need(nlo_done, TILE0[m])
                        if t >= 3:
                            need(add_done, ADD0[m] + t - 2)
                        dst = acc_t if t == 0 else sq[:, (t - 1) % 2, :]
                        act.activation(dst[:, 0:n], src(t), ACT.Square).then_inc(sq_done.sem, 1)

                def root(m, v=nv):
                    n = NORM_COLS[m]
                    act.preload_act_table_set("natural_log_exp_and_others")
                    need(nv_done, WIDE[m] + 1)
                    act.activation(r0[:, 0:n], v[:, 0:n], ACT.Ln).then_inc(ln_done.sem, 1)
                    need(ln_done, WIDE[m] + 1)
                    act.activation(r0[:, 0:n], r0[:, 0:n], ACT.Exp, scale=-0.5).then_inc(r0_done.sem, 1)

                def his(m, dst, blocks={}):
                    n = NORM_COLS[m]
                    for t in range(NORM_TILES[m]):
                        if t in blocks:
                            ahead(blocks[t])
                        need(y_done, Y0[m] + t + 1)
                        act.activation(dst(t), sq[:, t % 2, 0:n], ACT.Copy,
                                       scale=par[:, GAIN[m] + t:GAIN[m] + t + 1]).then_inc(nhi_done.sem, 1)

                def small_root(i):
                    act.preload_act_table_set("natural_log_exp_and_others")
                    need(s_v, i + 1)
                    act.activation(sm_r, sm_v, ACT.Ln).then_inc(s_ln.sem, 1)
                    need(s_ln, i + 1)
                    act.activation(sm_r, sm_r, ACT.Exp, scale=-0.5).then_inc(s_r0.sem, 1)

                act.dma_start(par[:, :], par_d[bass.ds(l, 1), :, :].rearrange("a p n -> (a p) n"))\
                    .then_inc(par_in.sem, 16)
                for b in range(AHEAD):
                    split(b)
                for t in range(EARLY, KD):
                    hi_and_square(l, MIX, t, t + 1 - 8)
                for b in range(B_LAT, B_LAT + 4):
                    ahead(b)
                root(MIX)
                small_root(0)
                need(par_in, 16)
                block_used(B_LAT + 3)
                for j in range(2):
                    act.activation(cq_hi[:, j, :], ps[4 + j][:, :], ACT.Copy, scale=par[:, G_Q + j:G_Q + j + 1])\
                        .then_inc(nhi_done.sem, 1)
                    act.activation((acc, sq[:, 0, :])[j], ps[4 + j][:, :], ACT.Square).then_inc(sq_done.sem, 1)
                squares(NKV, lambda t: lat_kv, lambda t: need(lat_done, 1), acc_t=sq[:, 1, :])
                ahead(B_U)
                need(kpe_ready, 1)
                for p in range(2):
                    act.activation(k_hi[64:96, p, :], rot[64:96, 2, :], ACT.Copy).then_inc(kpe_hi.sem, 1)
                ahead(B_U + 1)
                small_root(1)
                root(NKV, nv_kv)
                his(NKV, lambda t: ckv_hi[:, t, :])
                ahead(B_U + 2)
                need(nlo_done, TILE0[NKV] + 1)
                act.dma_start(ln_gb.rearrange("p a n -> p (a n)"),
                              ln_d[bass.ds(l, 1), :].to_broadcast([P, 2 * SG])).then_inc(ln_in.sem, 16)
                ahead(B_U + 3)
                ahead(B_WV)
                for t in range(TT):
                    if t < TT - 1:
                        need(wv_mm, t + 1)
                    else:
                        block_used(B_WV)
                    act.activation(v_hi[:, t, :], ps[BB[t]][:, :], ACT.Copy).then_inc(vh_done.sem, 1)
                for t in range(TT):
                    act.activation(u[:, t, :], ps[BA[t]][:, :], ACT.Gelu_apprx_tanh, scale=rs_tok[:, t:t + 1])\
                        .then_inc(u_done.sem, 1)
                ahead(B_HEAD[0])

                def q_part(h):
                    need(qp_mm, h + 1)
                    act.activation(q_hi[0:64, h % 2, :], ps[q_bank(h)][0:64, :], ACT.Copy).then_inc(qh_done.sem, 1)
                    if h > 0:
                        need(pel_done, h)
                    for k in range(2):
                        act.activation(rot[64:96, k, :], ps[q_bank(h)][64 + 32 * k:96 + 32 * k, :], ACT.Copy)\
                            .then_inc(pe_copied.sem, 1)

                def k_part(h):
                    if h % 2 == 0:
                        need(kp_mm, h // 2 + 1)
                    else:
                        block_used(B_HEAD[h // 2])
                    act.activation(k_hi[0:64, h % 2, :], ps[k_bank(h)][0:64, :], ACT.Copy).then_inc(kh_done.sem, 1)

                def rotated(h):
                    need(roped, h + 1)
                    act.activation(q_hi[64:96, h % 2, :], rot[64:96, 2, :], ACT.Copy).then_inc(peh_done.sem, 1)

                def exps(i):
                    need(nmax_done, i + 1)
                    if i >= 3:
                        need(turned, i - 2)
                    act.activation(e[:, i % 3, :], ps[6 + i % 2][:, :], ACT.Exp, bias=nmx[:, i % 4:i % 4 + 1],
                                   scale=qs[:, i % TT:i % TT + 1], accum_out=hsum[:, i % 8:i % 8 + 1]).then_inc(exp_done.sem, 1)

                def turned_hi(i):
                    need(turned, i + 1)
                    h, t = divmod(i, TT)
                    if t == 0 and h >= 2:
                        need(pv_mm, h - 1)
                    act.activation(pt_hi[h % 2][:, :, P * t:P * t + P],
                                   ps[i % 2][:, :].rearrange("p (k q) -> p k q", k=TT), ACT.Copy)\
                        .then_inc(pth_done.sem, 1)

                def copy_sums(h):
                    need(spread, h + 1)
                    if h > 0:
                        need(o_done, h)
                    act.activation(rsum, ps[3][0:64, :], ACT.Copy).then_inc(rsum_done.sem, 1)

                def square_output(t):
                    need(o_done, 2 * t + 2)
                    if t == 0:
                        need(svl_done, 4)
                    if t == 3:
                        need(add_done, ADD0[MLA] + 1)
                    act.activation(acc_o if t == 0 else sq_o[:, (t - 1) % 2, :], o_mla[:, t, :], ACT.Square)\
                        .then_inc(sq_done.sem, 1)

                def gate_turned(f):
                    need(sg_turned, f + 1)
                    act.activation(h_hi[:, 4 + f, :], ps[2][:, :], ACT.Copy,
                                   scale=par[:, G_SG + f:G_SG + f + 1]).then_inc(sgh_done.sem, 1)

                for h in range(2):
                    q_part(h)
                    k_part(h)
                    if h == 1:
                        ahead(B_V)
                    rotated(h)
                act.preload_act_table_set("natural_log_exp_and_others")
                exps(0)
                exps(1)
                for b in range(B_V + 1, B_V + 4):
                    ahead(b)
                for t in range(TT):
                    if t < TT - 1:
                        need(v_mm, t + 1)
                    else:
                        block_used(B_V + 3)
                    act.activation(vt[:, t, :], ps[BA[t]][:, :], ACT.Gelu_apprx_tanh, scale=rs_tok[:, t:t + 1])\
                        .then_inc(vg_done.sem, 1)
                act.preload_act_table_set("natural_log_exp_and_others")
                for i in range(HEADS * TT):
                    h, t = divmod(i, TT)
                    if i + 2 < HEADS * TT:
                        exps(i + 2)
                    turned_hi(i)
                    if t == 0:
                        if 1 <= h and h + 1 < HEADS:
                            rotated(h + 1)
                        if h == 0:
                            ahead(B_HEAD[1])
                    if t == 1:
                        if h + 2 < HEADS:
                            q_part(h + 2)
                    if (h, t) in SQUARE_STEPS:
                        square_output(SQUARE_STEPS.index((h, t)))
                    if t == 2 and h >= 1:
                        copy_sums(h - 1)
                    if t == 2 and h in (2, 4, 6):
                        ahead(B_V + 4 + h // 2)
                    if (h, t) == (7, 0):
                        ahead(B_OUT)
                    if t == 3:
                        if h + 2 < HEADS:
                            k_part(h + 2)
                    if (h, t) == STAT_STEPS[-1]:
                        small_root(2)
                    if (h, t) == GATED_STEPS[-1]:
                        small_root(3)
                    if (h, t) == (7, 2):
                        gate_turned(0)
                    if (h, t) in SPLIT_STEPS:
                        g = SPLIT_STEPS.index((h, t))
                        need(vn_done, g + 1)
                        act.activation(sv_hi[:, g, :], vt[:, g, :], ACT.Copy).then_inc(svh_done.sem, 1)
                gate_turned(1)
                copy_sums(HEADS - 1)
                gate_turned(2)
                square_output(3)
                gate_turned(3)
                act.dma_start(memT, memT_d).then_inc(mem_in.sem, 16)
                root(MLA)
                his(MLA, lambda t: h_hi[:, t, :], {2: B_OUT + 1})
                ahead(B_OUT + 2)
                squares(MTOK, lambda t: memT[:, t, :], lambda t: need(mem_in, 16) if t == 0 else None)
                ahead(B_OUT + 3)
                ahead(B_OUT + 4)
                root(MTOK)
                his(MTOK, lambda t: mt_hi[:, t, :], {2: B_OUT + 5, 5: B_OUT + 6})
                ahead(B_OUT + 7)
                def keys(g):
                    block_used(B_MK + 4 * g + 3)
                    for j in range(4):
                        act.activation(km_hi[:, 4 * g + j, :], ps[(BB, BA)[g][j]][:, 0:N_MEM], ACT.Copy)\
                            .then_inc(kmh_done.sem, 1)

                def values(g):
                    block_used(B_MV + 4 * g + 3)
                    for j in range(MT):
                        act.activation(vm_hi[:, 2 * j + g, :], ps[4 + 2 * g + j][:, :], ACT.Copy)\
                            .then_inc(vmh_done.sem, 1)

                def queries(g):
                    for j in range(4):
                        if j < 3:
                            need(mq_mm, 3 * g + j + 1)
                        else:
                            block_used(B_MQ + 4 * g + 3)
                        act.activation(qm_hi[:, 4 * g + j, :], ps[(BA, BB)[g][j]][:, :], ACT.Copy)\
                            .then_inc(qmh_done.sem, 1)

                for g in range(2):
                    for t in range(4 * g, 4 * g + 4):
                        ahead(B_MK + t)
                        hi_and_square(l, MEM, t, max(t + 1, 5))
                    keys(g)
                for b in range(B_MV, B_MV + 4):
                    ahead(b)
                values(0)
                ahead(B_MV + 4)
                small_root(4)
                for b in range(B_MV + 5, B_MV + 8):
                    ahead(b)
                values(1)
                for g in range(2):
                    for b in range(B_MQ + 4 * g, B_MQ + 4 * g + 4):
                        ahead(b)
                    queries(g)

                def mexps(i):
                    need(mnmax_done, i + 1)
                    if i >= 4:
                        need(mturned, i - 3)
                    act.activation(em[:, i % 4, :], ps[BM[i % 4]][:, 0:N_MEM], ACT.Exp, bias=nmx[:, i % 4:i % 4 + 1],
                                   scale=ms[:, i % TT:i % TT + 1], accum_out=sums[:, i % 4:i % 4 + 1])\
                        .then_inc(mexp_done.sem, 1)

                def mprobs(i):
                    need(mrecip_done, i + 1)
                    act.activation(em[:, i % 4, :], em[:, i % 4, :], ACT.Copy, scale=rin[:, i % 4:i % 4 + 1])\
                        .then_inc(mprob_done.sem, 1)

                def mturned_hi(i):
                    need(mturned, i + 1)
                    h, t = divmod(i, TT)
                    if t == 0 and h >= 2:
                        need(mpv_mm, 2 * h - 2)
                    act.activation(pm_hi[h % 2][:, :, P * t:P * t + P],
                                   ps[2 + i % 2][:, 0:MT * P].rearrange("p (k q) -> p k q", k=MT), ACT.Copy)\
                        .then_inc(pmh_done.sem, 1)

                def outputs(h):
                    for j in range(2):
                        need(mpv_mm, 2 * h + j + 1)
                        act.activation(qm_hi[:, 2 * h + j, :], ps[4 + j][:, :], ACT.Copy)\
                            .then_inc(omh_done.sem, 1)

                act.preload_act_table_set("natural_log_exp_and_others")
                for i in range(3):
                    mexps(i)
                mprobs(0)
                for i in range(MEM_HEADS * TT):
                    h, t = divmod(i, TT)
                    if i + 1 < MEM_HEADS * TT:
                        mprobs(i + 1)
                    if i + 3 < MEM_HEADS * TT:
                        mexps(i + 3)
                    mturned_hi(i)
                    if t == 2 and h >= 1:
                        outputs(h - 1)
                outputs(MEM_HEADS - 1)
                for b in range(B_MO, B_MO + 5):
                    ahead(b)
                for t in range(4):
                    hi_and_square(l, FFN, t, 8 + t + 1)
                for b in range(B_MO + 5, B_MO + 8):
                    ahead(b)
                for t in range(4, KD):
                    hi_and_square(l, FFN, t, 8 + t + 1)

                def up_group(half, r, i, step):
                    g = sum(GROUPS[:half]) + r
                    for b in range(B_UP[half] + 4 * r, B_UP[half] + 4 * r + 4):
                        ahead(b, i, 4 * step)
                        if g == 0 and b == B_UP[0] and not step:
                            root(FFN)
                    bank = 4 * (r % 2)
                    for j in range(2):
                        for s in range(2):
                            act.wait_ge(scaled.sem, l * (2 * FT) + i * (4 * step) + (4 * g + 2 * j + s + 1 + scaled.start))
                            c = s * FT + 2 * g + j
                            cb = par[:, bass.ds(i * (2 * step) + (C_B + c), 1)] if step else par[:, C_B + c:C_B + c + 1]
                            cw = par[:, bass.ds(i * (2 * step) + (C_W1 + c), 1)] if step else par[:, C_W1 + c:C_W1 + c + 1]
                            act.activation(conv[:, bank + 2 * j + s, :], lin[:, 2 * j + s, :], ACT.Identity,
                                           bias=cb, scale=cw).then_inc(tap1.sem, 1)
                    for j in range(2):
                        act.wait_ge(taps.sem, l * (4 * FT) + i * (8 * step) + (8 * g + 4 * j + 2 + taps.start))
                        cg = conv[:, bank + 2 * j, :]
                        act.activation(cg, cg, ACT.Silu).then_inc(silu_done.sem, 1)
                    for j in range(2):
                        act.wait_ge(prod_done.sem, l * FT + i * (2 * step) + (2 * g + j + 1))
                        dst = hid_hi[:, bass.ds(i * (2 * step) + (2 * r + j), 1), :] if step \
                            else hid_hi[:, 2 * r + j:2 * r + j + 1, :]
                        act.activation(dst, conv[:, bank + 2 * j:bank + 2 * j + 1, :], ACT.Copy).then_inc(fh_done.sem, 1)

                for half in range(2):
                    peeled = 0
                    if half == 0:
                        up_group(0, 0, 0, 0)
                        up_group(0, 1, 0, 0)
                        peeled = 2
                    with act.Fori(0, (GROUPS[half] - peeled) // 2) as i:
                        for r in range(peeled, peeled + 2):
                            up_group(half, r, i, 2)
                    if GROUPS[half] % 2:
                        up_group(half, GROUPS[half] - 1, 0, 0)
                    for b in range(B_DN[half], B_DN[half] + 2 * GROUPS[half]):
                        ahead(b)
                        if half == 1 and b == B_DN[1] + GROUPS[1]:
                            for t in range(EARLY):
                                hi_and_square(l, MIX, t, 24 + t + 1, later=1)

            with act.Fori(0, DEPTH) as l:
                layer(l)

            for t in range(EARLY, KD):
                act.wait_ge(x_ready.sem, x_ready.at(DEPTH, t + 1 - 8))
                if t >= 3:
                    act.wait_ge(add_done.sem, add_done.at(DEPTH, t - 2))
                act.activation(sq[:, (t - 1) % 2, :], x[:, t, :], ACT.Square).then_inc(sq_done.sem, 1)
            act.preload_act_table_set("natural_log_exp_and_others")
            act.wait_ge(nv_done.sem, nv_done.at(DEPTH, 1))
            act.activation(r0, nv, ACT.Ln).then_inc(ln_done.sem, 1)
            act.wait_ge(ln_done.sem, ln_done.at(DEPTH, 1))
            act.activation(r0, r0, ACT.Exp, scale=-0.5).then_inc(r0_done.sem, 1)

        @block.vector
        def _(dve):
            pos_i = work[64:128, 2, :].bitcast(I32)
            pos, ang, kt, red = work[64:128, 3, :], work[64:128, 4, :], work[64:128, 5, :], work[64:128, 0, :]
            steps = [0]

            def prep(ins):
                steps[0] += 1
                ins.then_inc(const_done, 1)
                dve.wait_ge(const_done, 3 + steps[0])

            def first_tiles(n):
                dve.wait_ge(x_in[n], 16)
                dve.sem_inc(x_ready.sem, 2)

            dve.wait_ge(const_in, 32)
            dve.wait_ge(const_done, 3)
            first_tiles(0)
            prep(dve.tensor_copy(pos, pos_i))
            prep(dve.tensor_scalar(ang, pos, freq[64:128, 0:1], None, ALU.mult))
            prep(dve.tensor_scalar(kt, ang, float(1 / TWO_PI), freq[64:128, 2:3], ALU.mult, ALU.add))
            prep(dve.tensor_scalar(kt, kt, ROUND, None, ALU.add))
            prep(dve.tensor_scalar(kt, kt, ROUND, None, ALU.subtract))
            prep(dve.scalar_tensor_tensor(out=red, in0=kt, scalar=-PI_A, in1=ang, op0=ALU.mult, op1=ALU.add))
            prep(dve.scalar_tensor_tensor(out=red, in0=kt, scalar=-PI_B, in1=red, op0=ALU.mult, op1=ALU.add))
            prep(dve.scalar_tensor_tensor(out=red, in0=kt, scalar=-PI_C, in1=red, op0=ALU.mult, op1=ALU.add))
            prep(dve.tensor_scalar(red, red, freq[64:128, 3:4], None, ALU.add))
            prep(dve.tensor_scalar(red, red, -PI_IN, PI_IN, ALU.max, ALU.min))
            dve.sem_inc(trig_dve, 1)
            for n in range(1, KD // 2):
                first_tiles(n)
            dve.wait_ge(gain_in[0], 16)
            dve.wait_ge(gain_in[1], 16 * DEPTH)
            dve.sem_inc(scaled.sem, scaled.start)

            def low_and_add(l, m, t, later=0):
                dve.wait_ge(nhi_done.sem, nhi_done.at(l, TILE0[m] + t + 1, later))
                g = mix_g[:, bass.ds(l * KD + (later * KD + t), 1)] if m == MIX \
                    else par[:, GAIN[m] + t:GAIN[m] + t + 1]
                dve.scalar_tensor_tensor(out=h_lo[:, t, :], in0=x[:, t, :], scalar=g, in1=h_hi[:, t, :].bitcast(F32),
                                         op0=ALU.mult, op1=ALU.subtract).then_inc(nlo_done.sem, 1)
                if t >= 1:
                    dve.wait_ge(sq_done.sem, sq_done.at(l, TILE0[m] + t + 1, later))
                    if t >= 2:
                        dve.wait_ge(add_done.sem, add_done.at(l, ADD0[m] + t - 1, later))
                    dve.tensor_tensor(acc, acc, sq[:, (t - 1) % 2, :], ALU.add).then_inc(add_done.sem, 1)

            for t in range(EARLY):
                low_and_add(0, MIX, t)
            dve.wait_ge(trig_act, 2)
            prep(dve.tensor_scalar(trig[64:96, 1, :], trig[64:96, 1, :], freq[64:96, 1:2], None, ALU.mult))

            def adds(l, m, first=1):
                n = NORM_COLS[m]
                for t in range(first, NORM_TILES[m]):
                    dve.wait_ge(sq_done.sem, sq_done.at(l, TILE0[m] + t + 1))
                    if t >= 2:
                        dve.wait_ge(add_done.sem, add_done.at(l, ADD0[m] + t - 1))
                    dve.tensor_tensor(acc[:, 0:n], acc[:, 0:n], sq[:, (t - 1) % 2, 0:n], ALU.add)\
                        .then_inc(add_done.sem, 1)

            def layer_tools(l):
                count = [0]

                def need(s, n):
                    dve.wait_ge(s.sem, s.at(l, n))

                def link(ins):
                    count[0] += 1
                    ins.then_inc(dve_step.sem, 1)
                    dve.wait_ge(dve_step.sem, dve_step.at(l, count[0]))

                def mean_square(m, bank, v=nv):
                    n = NORM_COLS[m]
                    need(ssq_done, WIDE[m] + 1)
                    dve.tensor_scalar(v[:, 0:n], ps[bank][:, 0:n], 1.0 / NORM_DIM[m], EPS, ALU.mult, ALU.add)\
                        .then_inc(nv_done.sem, 1)

                def newton(m, nv=nv):
                    n = NORM_COLS[m]
                    a, v, r = rs[:, 0:n], nv[:, 0:n], r0[:, 0:n]
                    need(r0_done, WIDE[m] + 1)
                    link(dve.tensor_tensor(a, r, r, ALU.mult))
                    link(dve.scalar_tensor_tensor(out=a, in0=a, scalar=-0.5, in1=v, op0=ALU.mult, op1=ALU.mult))
                    link(dve.scalar_tensor_tensor(out=a, in0=a, scalar=1.5, in1=r, op0=ALU.add, op1=ALU.mult))

                def apply(m, src, hi, lo):
                    n = NORM_COLS[m]

                    def y(t):
                        if t >= 2:
                            need(nlo_done, TILE0[m] + t - 1)
                        dve.tensor_tensor(sq[:, t % 2, 0:n], src(t), rs[:, 0:n], ALU.mult).then_inc(y_done.sem, 1)

                    y(0)
                    for t in range(NORM_TILES[m]):
                        if t + 1 < NORM_TILES[m]:
                            y(t + 1)
                        need(nhi_done, TILE0[m] + t + 1)
                        dve.scalar_tensor_tensor(out=lo(t), in0=sq[:, t % 2, 0:n],
                                                 scalar=par[:, GAIN[m] + t:GAIN[m] + t + 1], in1=hi(t).bitcast(F32),
                                                 op0=ALU.mult, op1=ALU.subtract).then_inc(nlo_done.sem, 1)

                def small_root(i, out=sm_t):
                    need(s_r0, i + 1)
                    link(dve.tensor_tensor(sm_t, sm_r, sm_r, ALU.mult))
                    link(dve.scalar_tensor_tensor(out=sm_t, in0=sm_t, scalar=-0.5, in1=sm_v, op0=ALU.mult, op1=ALU.mult))
                    link(dve.scalar_tensor_tensor(out=out, in0=sm_t, scalar=1.5, in1=sm_r, op0=ALU.add, op1=ALU.mult))

                return need, link, mean_square, newton, apply, small_root, count

            half_turn = [(i + 16) % 32 for i in range(32)]

            def layer(l):
                need, link, mean_square, newton, apply, small_root, count = layer_tools(l)

                def token_sums(m):
                    need(ssq_tok, TOK[m] + 1)

                for t in range(EARLY, KD):
                    low_and_add(l, MIX, t)
                mean_square(MIX, 0)
                token_sums(MIX)
                dve.tensor_scalar(sm_v, ps[1][:, 0:TT], 1.0 / D, EPS, ALU.mult, ALU.add).then_inc(s_v.sem, 1)
                newton(MIX)
                small_root(0, rs_tok)
                need(used, B_LAT + 4)
                dve.tensor_tensor(lat_kv, ps[6][:, :], rs, ALU.mult).then_inc(lat_done.sem, 1)
                dve.tensor_tensor(key, ps[7][64:96, :], rs[64:96, :], ALU.mult).then_inc(lat_done.sem, 1)
                for j in range(2):
                    need(nhi_done, TILE0[NQ] + j + 1)
                    need(sq_done, TILE0[NQ] + j + 1)
                    dve.scalar_tensor_tensor(out=cq_lo[:, j, :], in0=ps[4 + j][:, :], scalar=par[:, G_Q + j:G_Q + j + 1],
                                             in1=cq_hi[:, j, :].bitcast(F32), op0=ALU.mult, op1=ALU.subtract)\
                        .then_inc(nlo_done.sem, 1)
                adds(l, NQ)
                need(lat_done, 2)
                dve.sem_inc(dve_passed, 1)
                link(dve.stream_shuffle(rot[64:96, 1, :], key, half_turn))
                link(dve.tensor_tensor(rot[64:96, 1, :], rot[64:96, 1, :], trig[64:96, 1, :], ALU.mult))
                link(dve.tensor_tensor(rot[64:96, 2, :], key, trig[64:96, 0, :], ALU.mult))
                dve.tensor_tensor(rot[64:96, 2, :], rot[64:96, 2, :], rot[64:96, 1, :], ALU.add)\
                    .then_inc(kpe_ready.sem, 1)
                link(dve.tensor_tensor(qs, rs_tok, rs_tok, ALU.mult))
                token_sums(NQ)
                link(dve.scalar_tensor_tensor(out=sm_v, in0=ps[4][:, 0:TT], scalar=1.0 / Q_LORA, in1=qs,
                                              op0=ALU.mult, op1=ALU.mult))
                dve.tensor_scalar(sm_v, sm_v, EPS, None, ALU.add).then_inc(s_v.sem, 1)
                mean_square(NKV, 5, nv_kv)
                for p in range(2):
                    need(kpe_hi, p + 1)
                    link(dve.tensor_tensor(k_lo[64:96, p, :], rot[64:96, 2, :], k_hi[64:96, p, :].bitcast(F32),
                                           ALU.subtract))
                small_root(1)
                link(dve.scalar_tensor_tensor(out=qs, in0=sm_t, scalar=SCALE, in1=rs_tok, op0=ALU.mult, op1=ALU.mult))
                link(dve.tensor_scalar(nqs, qs, -1.0, None, ALU.mult))
                newton(NKV, nv_kv)
                apply(NKV, lambda t: lat_kv, lambda t: ckv_hi[:, t, :], lambda t: ckv_lo[:, t, :])
                for t in range(TT):
                    need(vh_done, t + 1)
                    dve.tensor_tensor(v_lo[:, t, :],
                                      ps[BB[t]][:, :], v_hi[:, t, :].bitcast(F32), ALU.subtract)\
                        .then_inc(vl_done.sem, 1)

                def q_part(h):
                    need(qh_done, h + 1)
                    need(pe_copied, 2 * h + 2)
                    dve.tensor_tensor(q_lo[0:64, h % 2, :], ps[q_bank(h)][0:64, :], q_hi[0:64, h % 2, :].bitcast(F32),
                                      ALU.subtract).then_inc(ql_done.sem, 1)

                def k_part(h):
                    need(kh_done, h + 1)
                    dve.tensor_tensor(k_lo[0:64, h % 2, :], ps[k_bank(h)][0:64, :], k_hi[0:64, h % 2, :].bitcast(F32),
                                      ALU.subtract).then_inc(kl_done.sem, 1)

                def maximum(i, mm, done, scores, minus_scale):
                    c = slice(i % 4, i % 4 + 1)
                    need(mm, i + 1)
                    link(dve.reduce_max(mx[:, c], scores, AXX))
                    dve.tensor_scalar(nmx[:, c], mx[:, c], minus_scale[:, i % TT:i % TT + 1], None, ALU.mult)\
                        .then_inc(done.sem, 1)

                def recip(i):
                    c = slice(i % 4, i % 4 + 1)
                    need(mexp_done, i + 1)
                    dve.reciprocal(rin[:, c], sums[:, c]).then_inc(mrecip_done.sem, 1)

                def amax(i):
                    maximum(i, score_mm, nmax_done, ps[6 + i % 2][:, :], nqs)

                def recip_sums(h):
                    need(exp_done, TT * h + TT)
                    c = slice(4 * (h % 2), 4 * (h % 2) + 4)
                    dve.reciprocal(hrec[:, c], hsum[:, c]).then_inc(hrec_done.sem, 1)

                def attended(h):
                    need(rsum_done, h + 1)
                    need(pv_mm, h + 1)
                    dve.tensor_tensor(o_mla[64 * (h % 2):64 * (h % 2) + 64, h // 2, :], ps[5][0:64, :], rsum, ALU.mult)\
                        .then_inc(o_done.sem, 1)

                def add_square(t):
                    need(sq_done, TILE0[MLA] + t + 1)
                    if t >= 2:
                        need(add_done, ADD0[MLA] + t - 1)
                    dve.tensor_tensor(acc_o, acc_o, sq_o[:, (t - 1) % 2, :], ALU.add).then_inc(add_done.sem, 1)

                def turned_lo(i):
                    need(pth_done, i + 1)
                    h, t = divmod(i, TT)
                    c = slice(P * t, P * t + P)
                    dve.tensor_tensor(pt_lo[h % 2][:, :, c], ps[i % 2][:, :].rearrange("p (k q) -> p k q", k=TT),
                                      pt_hi[h % 2][:, :, c].bitcast(F32), ALU.subtract).then_inc(ptl_done.sem, 1)

                def statistics(src, t):
                    link(dve.bn_stats(bn[:, t, :], src[:, t, :]))
                    dve.sem_inc(dve_passed, 1)
                    link(dve.bn_aggr(mv[:, t, :], bn[:, t, :]))

                def gated_heads(n):
                    for s in range(2 * n, 2 * n + 2):
                        if n < SG_HEADS // 2 - 1:
                            need(mix_mm, n + 1)
                        else:
                            need(used, B_WS + 1)
                        us = u[:, :, SG_HD * s:SG_HD * s + SG_HD]
                        dve.scalar_tensor_tensor(out=us, in0=ps[2][:, (s % 2) * 256:(s % 2) * 256 + 256]
                                                 .rearrange("p (c d) -> p c d", c=TT),
                                                 scalar=par[:, C_BS + s:C_BS + s + 1], in1=us,
                                                 op0=ALU.add, op1=ALU.mult).then_inc(gated.sem, 1)

                def gate_turned(f):
                    need(sgh_done, f + 1)
                    dve.scalar_tensor_tensor(out=h_lo[:, 4 + f, :], in0=ps[2][:, :],
                                             scalar=par[:, G_SG + f:G_SG + f + 1], in1=h_hi[:, 4 + f, :].bitcast(F32),
                                             op0=ALU.mult, op1=ALU.subtract).then_inc(sgl_done.sem, 1)

                for h in range(2):
                    q_part(h)
                    k_part(h)
                amax(0)
                amax(1)
                for i in range(HEADS * TT):
                    h, t = divmod(i, TT)
                    if i + 2 < HEADS * TT:
                        amax(i + 2)
                    if t == 0 and 1 <= h and h + 1 < HEADS:
                        k_part(h + 1)
                    if t == 0 and h >= 1:
                        recip_sums(h - 1)
                    if t == 2 and h + 2 < HEADS:
                        q_part(h + 2)
                    if t == 3 and h >= 1:
                        attended(h - 1)
                    if (h, t) in ADD_STEPS:
                        add_square(ADD_STEPS.index((h, t)) + 1)
                    if (h, t) in STAT_STEPS:
                        c = STAT_STEPS.index((h, t))
                        need(vg_done, c + 1)
                        statistics(vt, c)
                        if c == TT - 1:
                            dve.tensor_scalar(sm_v, mv[:, :, 1], EPS, None, ALU.add).then_inc(s_v.sem, 1)
                    if (h, t) == NORM_STEPS[0]:
                        small_root(2)
                    if (h, t) in NORM_STEPS:
                        g = NORM_STEPS.index((h, t))
                        if g == 0:
                            need(ln_in, 16)
                        link(dve.tensor_scalar(vt[:, g, :], vt[:, g, :], mv[:, g, 0:1], sm_t[:, g:g + 1],
                                               ALU.subtract, ALU.mult))
                        link(dve.tensor_tensor(vt[:, g, :], vt[:, g, :], ln_gb[:, 0, :], ALU.mult))
                        dve.tensor_tensor(vt[:, g, :], vt[:, g, :], ln_gb[:, 1, :], ALU.add).then_inc(vn_done.sem, 1)
                    if (h, t) in MIX_STEPS:
                        gated_heads(MIX_STEPS.index((h, t)))
                    if (h, t) in GATED_STEPS:
                        if (h, t) == GATED_STEPS[0]:
                            need(gated, SG_HEADS)
                        statistics(u, GATED_STEPS.index((h, t)))
                    if (h, t) == GATED_STEPS[-1]:
                        link(dve.tensor_tensor(sm_t, mv[:, :, 0], mv[:, :, 0], ALU.mult))
                        dve.scalar_tensor_tensor(out=sm_v, in0=sm_t, scalar=EPS, in1=mv[:, :, 1], op0=ALU.add,
                                                 op1=ALU.add).then_inc(s_v.sem, 1)
                    if (h, t) == (7, 0):
                        small_root(3)
                        for c in range(TT):
                            dve.tensor_scalar(u[:, c, :], u[:, c, :], sm_t[:, c:c + 1], None, ALU.mult)\
                                .then_inc(sg_normed.sem, 1)
                    if (h, t) == (7, 2):
                        gate_turned(0)
                    turned_lo(i)
                recip_sums(HEADS - 1)
                gate_turned(1)
                gate_turned(2)
                attended(HEADS - 1)
                add_square(3)
                gate_turned(3)
                mean_square(MLA, 0)
                newton(MLA)
                apply(MLA, lambda t: o_mla[:, t, :], lambda t: h_hi[:, t, :], lambda t: h_lo[:, t, :])
                adds(l, MTOK)
                need(used, B_OUT + 4)

                def residual(b_last, banks, t0):
                    need(used, b_last + 1)
                    for j in range(4):
                        dve.tensor_tensor(x[:, t0 + j, :], x[:, t0 + j, :], ps[banks[j]][:, :], ALU.add)\
                            .then_inc(x_ready.sem, 1)

                residual(B_OUT + 3, BO, 0)
                mean_square(MTOK, 4)
                newton(MTOK)
                apply(MTOK, lambda t: memT[:, t, :], lambda t: mt_hi[:, t, :], lambda t: mt_lo[:, t, :])
                residual(B_OUT + 7, BA, 4)
                def values_lo(g):
                    for j in range(MT):
                        need(vmh_done, MT * g + j + 1)
                        dve.tensor_tensor(vm_lo[:, 2 * j + g, :], ps[4 + 2 * g + j][:, :],
                                          vm_hi[:, 2 * j + g, :].bitcast(F32), ALU.subtract).then_inc(vml_done.sem, 1)

                for g in range(2):
                    for t in range(4 * g, 4 * g + 4):
                        low_and_add(l, MEM, t)
                    for j in range(4):
                        need(kmh_done, 4 * g + j + 1)
                        dve.tensor_tensor(km_lo[:, 4 * g + j, :], ps[(BB, BA)[g][j]][:, 0:N_MEM],
                                          km_hi[:, 4 * g + j, :].bitcast(F32), ALU.subtract).then_inc(kml_done.sem, 1)
                values_lo(0)
                token_sums(MEM)
                dve.tensor_scalar(sm_v, ps[0][:, 0:TT], 1.0 / D, EPS, ALU.mult, ALU.add).then_inc(s_v.sem, 1)
                small_root(4)
                link(dve.tensor_scalar(ms, sm_t, MEM_SCALE, None, ALU.mult))
                link(dve.tensor_scalar(nms, sm_t, -MEM_SCALE, None, ALU.mult))
                values_lo(1)
                for g in range(2):
                    for j in range(4):
                        need(qmh_done, 4 * g + j + 1)
                        dve.tensor_tensor(qm_lo[:, 4 * g + j, :], ps[(BA, BB)[g][j]][:, :],
                                          qm_hi[:, 4 * g + j, :].bitcast(F32), ALU.subtract).then_inc(qml_done.sem, 1)

                def mmax(i):
                    maximum(i, mscore_mm, mnmax_done, ps[BM[i % 4]][:, 0:N_MEM], nms)

                def mturned_lo(i):
                    need(pmh_done, i + 1)
                    h, t = divmod(i, TT)
                    c = slice(P * t, P * t + P)
                    dve.tensor_tensor(pm_lo[h % 2][:, :, c], ps[2 + i % 2][:, 0:MT * P].rearrange("p (k q) -> p k q", k=MT),
                                      pm_hi[h % 2][:, :, c].bitcast(F32), ALU.subtract).then_inc(pml_done.sem, 1)

                def outputs(h):
                    for j in range(2):
                        need(omh_done, 2 * h + j + 1)
                        dve.tensor_tensor(qm_lo[:, 2 * h + j, :], ps[4 + j][:, :],
                                          qm_hi[:, 2 * h + j, :].bitcast(F32), ALU.subtract).then_inc(oml_done.sem, 1)

                for i in range(3):
                    mmax(i)
                recip(0)
                recip(1)
                for i in range(MEM_HEADS * TT):
                    h, t = divmod(i, TT)
                    if i + 3 < MEM_HEADS * TT:
                        mmax(i + 3)
                    if i + 2 < MEM_HEADS * TT:
                        recip(i + 2)
                    if t == 3 and h >= 1:
                        outputs(h - 1)
                    mturned_lo(i)
                outputs(MEM_HEADS - 1)
                for g in range(2):
                    residual(B_MO + 4 * g + 3, (BA, BB)[g], 4 * g)
                    for t in range(4 * g, 4 * g + 4):
                        low_and_add(l, FFN, t)
                mean_square(FFN, 4)
                newton(FFN)

                def up_group(half, r, i, step):
                    g = sum(GROUPS[:half]) + r
                    bank = 4 * (r % 2)

                    def col(base):
                        return par[:, bass.ds(i * (2 * step) + base, 1)] if step else par[:, base:base + 1]

                    def scale(j, s):
                        dve.tensor_tensor(lin[:, 2 * j + s, :], ps[bank + 2 * s + j][:, :], rs, ALU.mult)\
                            .then_inc(scaled.sem, 1)

                    def outer(j, s):
                        n = 4 * g + 2 * j + s
                        dve.wait_ge(tap1.sem, l * (2 * FT) + i * (4 * step) + (n + 1))
                        c, a = conv[:, bank + 2 * j + s, :], lin[:, 2 * j + s, :]
                        at = s * FT + 2 * g + j
                        dve.scalar_tensor_tensor(out=c[:, 1:SEQ], in0=a[:, 0:SEQ - 1], scalar=col(C_W0 + at),
                                                 in1=c[:, 1:SEQ], op0=ALU.mult, op1=ALU.add).then_inc(taps.sem, 1)
                        dve.wait_ge(taps.sem, l * (4 * FT) + i * (8 * step) + (2 * n + 1 + taps.start))
                        dve.scalar_tensor_tensor(out=c[:, 0:SEQ - 1], in0=a[:, 1:SEQ], scalar=col(C_W2 + at),
                                                 in1=c[:, 0:SEQ - 1], op0=ALU.mult, op1=ALU.add).then_inc(taps.sem, 1)

                    def product(j):
                        n = 2 * g + j
                        dve.wait_ge(silu_done.sem, l * FT + i * (2 * step) + (n + 1))
                        dve.wait_ge(taps.sem, l * (4 * FT) + i * (8 * step) + (4 * n + 4 + taps.start))
                        c = conv[:, bank + 2 * j, :]
                        dve.tensor_tensor(c, c, conv[:, bank + 2 * j + 1, :], ALU.mult).then_inc(prod_done.sem, 1)

                    def low(j):
                        dve.wait_ge(fh_done.sem, l * FT + i * (2 * step) + (2 * g + j + 1))
                        at = bass.ds(i * (2 * step) + (2 * r + j), 1) if step else slice(2 * r + j, 2 * r + j + 1)
                        dve.tensor_tensor(hid_lo[:, at, :], conv[:, bank + 2 * j:bank + 2 * j + 1, :],
                                          hid_hi[:, at, :].bitcast(F32), ALU.subtract).then_inc(fl_done.sem, 1)

                    dve.wait_ge(used.sem, l * BLOCKS + i * (4 * step) + (B_UP[half] + 4 * r + 4 + SPLIT))
                    if g:
                        dve.wait_ge(taps.sem, l * (4 * FT) + i * (8 * step) + 8 * g)
                    for j in range(2):
                        for s in range(2):
                            scale(j, s)
                    outer(0, 0)
                    outer(0, 1)
                    outer(1, 0)
                    product(0)
                    outer(1, 1)
                    product(1)
                    low(0)
                    low(1)

                dve.sem_inc(dve_passed, 1)
                for half in range(2):
                    with dve.Fori(0, GROUPS[half] // 2) as i:
                        for r in range(2):
                            up_group(half, r, i, 2)
                    if GROUPS[half] % 2:
                        up_group(half, GROUPS[half] - 1, 0, 0)
                    for hf in range(2):
                        residual(B_DN[half] + GROUPS[half] * (hf + 1) - 1, ((BA, BB), (BB, BA))[half][hf], 4 * hf)
                        if half == 1 and hf == 0:
                            for t in range(EARLY):
                                low_and_add(l, MIX, t, later=1)
                assert count[0] == N_STEP, count[0]

            with dve.Fori(0, DEPTH) as l:
                layer(l)

            need, link, mean_square, newton, apply, small_root, count = layer_tools(DEPTH)
            adds(DEPTH, MIX, EARLY)
            mean_square(MIX, 4)
            newton(MIX)
            for t in range(KD):
                dve.scalar_tensor_tensor(out=conv[:, t, :], in0=x[:, t, :], scalar=mix_g[:, DEPTH * KD + t:DEPTH * KD + t + 1],
                                         in1=rs, op0=ALU.mult, op1=ALU.mult).then_inc(out_done, 1)

        @block.tensor
        def _(pe):
            pe.wait_ge(const_done, 3)

            def layer(l):
                def need(s, n):
                    pe.wait_ge(s.sem, s.at(l, n))

                def block_ready(b, i=0, step=0):
                    pe.wait_ge(lo_done.sem, l * BLOCKS + i * step + (b + 1))

                def product3(out, a_hi, a_lo, b_hi, b_lo, first, last):
                    pe.matmul(out, a_hi, b_hi, start=first, stop=False)
                    pe.matmul(out, a_hi, b_lo, start=False, stop=False)
                    return pe.matmul(out, a_lo, b_hi, start=False, stop=last)

                def sum_squares(m, bank, acc_t=acc):
                    n = NORM_COLS[m]
                    if NORM_TILES[m] > 1:
                        need(add_done, ADD0[m + 1])
                    else:
                        need(sq_done, TILE0[m] + 1)
                    pe.matmul(ps[bank][:, 0:n], ones[:, :], acc_t[:, 0:n], start=True, stop=True)\
                        .then_inc(ssq_done.sem, 1)

                def token_sums(m, bank):
                    need(add_done, ADD0[m + 1])
                    for t in range(TT):
                        last = pe.matmul(ps[bank][:, t:t + 1], acc[:, P * t:P * t + P], ones[:, 0:1], start=True, stop=True)
                    last.then_inc(ssq_tok.sem, 1)

                def halves(b, width):
                    s = b % SPLIT
                    return (w_hi[:, s, :].rearrange("p (k c) -> p k c", c=width),
                            w_lo[:, s, :].rearrange("p (k c) -> p k c", c=width))

                def turns(n, final):
                    return [(jk, j) for j in range(n) for jk in range(2)] if final \
                        else [(jk, j) for jk in range(2) for j in range(n)]

                def project(b0, banks, x_hi, x_lo, ready, n=SEQ, cols=None, blocks=4, i=0, step=0,
                            between=None, norm_after=None, order=None, tile_mm=None,
                            bank_free=lambda j: None):
                    order = order or list(range(blocks))
                    for n_kp, kp in enumerate(order):
                        block_ready(b0 + n_kp, i, step)
                        wh, wl = halves(b0 + n_kp, 512)
                        if between and n_kp == (blocks - 1 if norm_after is None else norm_after):
                            between()
                        final = n_kp == blocks - 1
                        for jk, j in turns(len(banks), final):
                            k = 2 * kp + jk
                            if j == 0:
                                ready(k)
                            if n_kp == 0 and jk == 0:
                                bank_free(j)
                            c = cols[j] if cols else slice(P * j, P * j + P)
                            last = product3(ps[banks[j]][0:c.stop - c.start, 0:n], wh[:, jk, c], wl[:, jk, c],
                                            x_hi[:, k, 0:n], x_lo[:, k, 0:n],
                                            n_kp == 0 and jk == 0, final and jk == 1)
                            if tile_mm and final and jk == 1 and j < len(banks) - 1:
                                last.then_inc(tile_mm.sem, 1)
                        last.then_inc(used.sem, 1)

                def project_tokens(b0, banks, x_hi, x_lo, ready, between=None, tile_mm=None):
                    for kp in range(4):
                        if between and kp == 2:
                            between()
                        block_ready(b0 + kp)
                        wh, wl = halves(b0 + kp, 512)
                        for jk, j in turns(len(banks), kp == 3):
                            k = 2 * kp + jk
                            if j == 0:
                                ready(k)
                            c = slice(P * j, P * j + P)
                            last = product3(ps[banks[j]][:, :], x_hi[:, k, c], x_lo[:, k, c],
                                            wh[:, jk, :], wl[:, jk, :], k == 0, k == 7)
                            if tile_mm and k == 7 and j < len(banks) - 1:
                                last.then_inc(tile_mm.sem, 1)
                        last.then_inc(used.sem, 1)

                def normed(m):
                    return lambda k: need(nlo_done, TILE0[m] + k + 1)

                def latent_sums():
                    need(lat_done, 2)
                    need(nlo_done, TILE0[NQ] + 2)
                    token_sums(NQ, 4)
                    sum_squares(NKV, 5, acc_t=sq[:, 1, :])

                def mixers_norm():
                    need(x_ready, 0)
                    sum_squares(MIX, 0)
                    token_sums(MIX, 1)

                project(B_LAT, BB, h_hi, h_lo, normed(MIX),
                        cols=[slice(0, 128), slice(128, 256), slice(256, 384), slice(320, 416)],
                        between=mixers_norm)
                need(s_v, 1)
                project_tokens(B_U, BA, h_hi, h_lo, lambda k: None, between=latent_sums)
                block_ready(B_WV)
                wh, wl = halves(B_WV, 512)
                need(nlo_done, TILE0[NKV] + 1)
                for t in range(TT):
                    c = slice(P * t, P * t + P)
                    last = product3(ps[BB[t]][:, :], ckv_hi[:, 0, c], ckv_lo[:, 0, c], wh[:, 0, :], wl[:, 0, :],
                                    True, True)
                    if t < TT - 1:
                        last.then_inc(wv_mm.sem, 1)
                last.then_inc(used.sem, 1)

                def q_proj(h):
                    b = B_HEAD[h // 2]
                    if h % 2 == 0:
                        block_ready(b)
                    wh, wl = halves(b, BLK)
                    if h >= 2:
                        need(kl_done, h)
                    else:
                        need(vl_done, 2 * h + 1)
                    for k in range(2):
                        c = slice((2 * k + h % 2) * P, (2 * k + h % 2) * P + P)
                        last = product3(ps[q_bank(h)][:, :], wh[:, 0, c], wl[:, 0, c], cq_hi[:, k, :], cq_lo[:, k, :],
                                        k == 0, k == 1)
                    last.then_inc(qp_mm.sem, 1)

                def k_proj(h):
                    b = B_HEAD[h // 2]
                    wh, wl = halves(b, BLK)
                    c = slice(4 * P + (h % 2) * NOPE, 4 * P + (h % 2) * NOPE + NOPE)
                    if h >= 2:
                        need(ql_done, h + 1)
                    else:
                        need(vl_done, 2 * h + 2)
                    product3(ps[k_bank(h)][0:NOPE, :], wh[:, 0, c], wl[:, 0, c], ckv_hi[:, 0, :], ckv_lo[:, 0, :],
                             True, True).then_inc((used if h % 2 else kp_mm).sem, 1)

                def scores(i):
                    h, t = divmod(i, TT)
                    if t == 0:
                        need(kl_done, h + 1)
                        need(pel_done, h + 1)
                    if i == 0:
                        need(kl_done, 2)
                    if i >= 2:
                        need(exp_done, i - 1)
                    c = slice(P * t, P * t + P)
                    product3(ps[6 + i % 2][:, :], q_hi[0:QK, h % 2, c], q_lo[0:QK, h % 2, c],
                             k_hi[0:QK, h % 2, :], k_lo[0:QK, h % 2, :], True, True).then_inc(score_mm.sem, 1)

                def turn(i):
                    need(exp_done, i + 1)
                    if i >= 2:
                        need(ptl_done, i - 1)
                    for k in range(TT):
                        last = pe.transpose(ps[i % 2][:, P * k:P * k + P], e[:, i % 3, P * k:P * k + P], ident[:, :])
                    last.then_inc(turned.sem, 1)

                def attend(h):
                    need(ptl_done, TT * h + TT)
                    if h > 0:
                        need(o_done, h)
                    c = slice(VD * h, VD * h + VD)
                    for k in range(TT):
                        last = product3(ps[5][0:VD, :], v_hi[:, k, c], v_lo[:, k, c],
                                        pt_hi[h % 2][:, k, :], pt_lo[h % 2][:, k, :], k == 0, k == TT - 1)
                    last.then_inc(pv_mm.sem, 1)

                def spread_sums(h):
                    need(hrec_done, h + 1)
                    if h > 0:
                        need(o_done, h)
                    for t in range(TT):
                        c = 4 * (h % 2) + t
                        last = pe.transpose(ps[3][:, P * t:P * t + P], hrec[:, c:c + 1].to_broadcast([P, P]), ident[:, :])
                    last.then_inc(spread.sem, 1)

                def mix(n):
                    if n == 0:
                        block_ready(B_WS)
                        need(svl_done, 4)
                    else:
                        need(gated, 2 * n)
                    wh, wl = halves(B_WS, P)
                    for s in range(2 * n, 2 * n + 2):
                        c = slice(SG_HD * s, SG_HD * s + SG_HD)
                        out = ps[2][:, (s % 2) * 256:(s % 2) * 256 + 256].rearrange("p (c d) -> p c d", c=TT)
                        last = product3(out, wh[:, s, :], wl[:, s, :], sv_hi[:, :, c], sv_lo[:, :, c], True, True)
                    last.then_inc((mix_mm if n < SG_HEADS // 2 - 1 else used).sem, 1)

                def turn_gated(f):
                    if f == 0:
                        need(sg_normed, 4)
                    else:
                        need(sgl_done, f)
                    for t in range(TT):
                        last = pe.transpose(ps[2][:, P * t:P * t + P], u[:, t, P * f:P * f + P], ident[:, :])
                    last.then_inc(sg_turned.sem, 1)

                for h in range(2):
                    q_proj(h)
                    k_proj(h)

                def first_scores():
                    scores(0)
                    scores(1)

                need(u_done, 4)
                project_tokens(B_V, BA, h_hi, h_lo, lambda k: None, between=first_scores, tile_mm=v_mm)
                need(vg_done, 4)
                for i in range(HEADS * TT):
                    h, t = divmod(i, TT)
                    if i + 2 < HEADS * TT:
                        scores(i + 2)
                    turn(i)
                    if (h, t) in MIX_STEPS:
                        mix(MIX_STEPS.index((h, t)))
                    if t == 1 and h + 2 < HEADS:
                        q_proj(h + 2)
                    if t == 1 and h >= 1:
                        spread_sums(h - 1)
                    if t == 2 and h >= 1:
                        attend(h - 1)
                    if t == 3 and h + 2 < HEADS:
                        k_proj(h + 2)
                    if h == HEADS - 1 and t % 2:
                        turn_gated(t // 2)
                attend(HEADS - 1)
                spread_sums(HEADS - 1)
                turn_gated(2)

                def mixed(k):
                    if k == 5:
                        turn_gated(3)
                    if k < 4:
                        need(nlo_done, TILE0[MLA] + k + 1)
                    else:
                        need(sgl_done, k - 3)

                project(B_OUT, BO, h_hi, h_lo, mixed, order=[2, 3, 0, 1], norm_after=1,
                        bank_free=lambda j: need(o_done, HEADS) if j == 3 else None,
                        between=lambda: sum_squares(MLA, 0, acc_t=acc_o))

                def tokens_norm():
                    need(x_ready, 4)
                    sum_squares(MTOK, 4)

                project(B_OUT + 4, BA, h_hi, h_lo, lambda k: None, order=[2, 3, 0, 1], norm_after=1,
                        between=tokens_norm)
                project(B_MK, BB, mt_hi, mt_lo, normed(MTOK), n=N_MEM)
                need(x_ready, 8)
                project(B_MK + 4, BA, mt_hi, mt_lo, lambda k: None, n=N_MEM)
                need(kml_done, 4)
                project_tokens(B_MV, (4, 5), mt_hi, mt_lo, lambda k: None)
                need(kml_done, 8)
                token_sums(MEM, 0)
                project_tokens(B_MV + 4, (6, 7), mt_hi, mt_lo, lambda k: None)
                need(s_v, 5)
                project(B_MQ, BA, h_hi, h_lo, normed(MEM), tile_mm=mq_mm)
                need(vml_done, 4)
                project(B_MQ + 4, BB, h_hi, h_lo, lambda k: None, tile_mm=mq_mm)

                def mscores(i):
                    h, t = divmod(i, TT)
                    if i >= 4:
                        need(mexp_done, i - 3)
                    c = slice(P * t, P * t + P)
                    for k in range(2):
                        f = 2 * h + k
                        last = product3(ps[BM[i % 4]][:, 0:N_MEM], qm_hi[:, f, c], qm_lo[:, f, c],
                                        km_hi[:, f, :], km_lo[:, f, :], k == 0, k == 1)
                    last.then_inc(mscore_mm.sem, 1)

                def mturn(i):
                    need(mprob_done, i + 1)
                    if i >= 2:
                        need(pml_done, i - 1)
                    for k in range(MT):
                        last = pe.transpose(ps[2 + i % 2][:, P * k:P * k + P], em[:, i % 4, P * k:P * k + P], ident[:, :])
                    last.then_inc(mturned.sem, 1)

                def mattend(h):
                    need(pml_done, TT * h + TT)
                    if h >= 1:
                        need(oml_done, 2 * h)
                    for j in range(2):
                        f = 2 * h + j
                        c = slice((f % 4) * P, (f % 4) * P + P)
                        for k in range(MT):
                            at = 2 * k + f // 4
                            last = product3(ps[4 + j][:, :], vm_hi[:, at, c], vm_lo[:, at, c],
                                            pm_hi[h % 2][:, k, :], pm_lo[h % 2][:, k, :], k == 0, k == MT - 1)
                        last.then_inc(mpv_mm.sem, 1)

                need(qml_done, 8)
                for i in range(3):
                    mscores(i)
                for i in range(MEM_HEADS * TT):
                    h, t = divmod(i, TT)
                    if i + 3 < MEM_HEADS * TT:
                        mscores(i + 3)
                    mturn(i)
                    if t == 1 and h >= 1:
                        mattend(h - 1)
                mattend(MEM_HEADS - 1)
                project(B_MO, BA, qm_hi, qm_lo, lambda k: need(oml_done, k + 1))
                project(B_MO + 4, BB, qm_hi, qm_lo, lambda k: None)

                def ffn_norm():
                    need(x_ready, 16)
                    sum_squares(FFN, 4)

                need(x_ready, 12)

                def up_group(half, r, i, step, **first):
                    g = sum(GROUPS[:half]) + r
                    bank = 4 * (r % 2)
                    if half == 1:
                        need(x_ready, (20, 24)[r % 2])
                    pe.wait_ge(scaled.sem, l * (2 * FT) + i * (4 * step) + (4 * (g - 1) + scaled.start))
                    project(B_UP[half] + 4 * r, tuple(range(bank, bank + 4)), h_hi, h_lo,
                            normed(FFN) if first else lambda k: None, i=i, step=4 * step, **first)

                for half in range(2):
                    peeled = 0
                    if half == 0:
                        up_group(0, 0, 0, 0, between=ffn_norm)
                        need(nv_done, WIDE[FFN] + 1)
                        up_group(0, 1, 0, 0)
                        peeled = 2
                    else:
                        pe.sem_inc(pe_passed, 1)
                    with pe.Fori(0, (GROUPS[half] - peeled) // 2) as i:
                        for r in range(peeled, peeled + 2):
                            up_group(half, r, i, 2)
                    if GROUPS[half] % 2:
                        up_group(half, GROUPS[half] - 1, 0, 0)
                    g0 = sum(GROUPS[:half])
                    for hf in range(2):
                        need(scaled, 4 * (g0 + GROUPS[half] - 1 + hf))
                        project(B_DN[half] + GROUPS[half] * hf, ((BA, BB), (BB, BA))[half][hf], hid_hi, hid_lo,
                                (lambda k: need(fl_done, 2 * g0 + k + 1)) if hf == 0 else (lambda k: None),
                                blocks=GROUPS[half])

            with pe.Fori(0, DEPTH) as l:
                layer(l)
            pe.wait_ge(add_done.sem, add_done.at(DEPTH, KD - 1))
            pe.matmul(ps[4][:, :], ones[:, :], acc, start=True, stop=True).then_inc(ssq_done.sem, 1)


def _pack(w, c0, width):
    k = w.shape[0] // (2 * P)
    return w[:, c0:c0 + width].reshape(k, 2, P, width).transpose(0, 2, 1, 3).reshape(k, P, 2 * width)


def _weight_blocks(w_in, w_uq, w_ukv, w_s, w_out, w_mkv, w_mq, w_mo, w_up, w_down):
    out = np.zeros((BLOCKS, P, BLK), np.float32)
    c3 = Q_LORA + KV_LORA + ROPE
    for k in range(2):
        out[B_LAT:B_LAT + 4, :, 512 * k:512 * k + c3] = \
            w_in[:, 0:c3].reshape(4, 2, P, c3)[:, k]
    out[B_U:B_U + 4] = _pack(w_in, c3, SG)
    out[B_V:B_V + 4] = _pack(w_in, c3 + SG, SG)
    ukv = w_ukv.reshape(KV_LORA, HEADS, NOPE + VD)
    out[B_WV, :, 0:HEADS * VD] = ukv[:, :, NOPE:].reshape(KV_LORA, HEADS * VD)
    uq = w_uq.reshape(2, P, HEADS, QK)
    half = ROPE // 2
    for p in range(HEADS // 2):
        for k in range(2):
            for i in range(2):
                c = (2 * k + i) * P
                out[B_HEAD[p], :, c:c + QK] = uq[k, :, 2 * p + i]
                out[B_HEAD[p], :, c + QK:c + QK + half] = uq[k, :, 2 * p + i, NOPE + half:]
                out[B_HEAD[p], :, c + QK + half:c + P] = uq[k, :, 2 * p + i, NOPE:NOPE + half]
        out[B_HEAD[p], :, 4 * P:4 * P + 2 * NOPE] = ukv[:, 2 * p:2 * p + 2, 0:NOPE].reshape(P, 2 * NOPE)
    out[B_WS] = w_s.transpose(2, 0, 1).reshape(P, SG_HEADS * P)
    for base, w, c in ((B_MK, w_mkv, 0), (B_MV, w_mkv, D), (B_MQ, w_mq, 0), (B_MO, w_mo, 0)):
        for g in range(2):
            out[base + 4 * g:base + 4 * g + 4] = _pack(w, c + 512 * g, 512)
    for g in range(2):
        out[B_OUT + 4 * g:B_OUT + 4 * g + 4] = _pack(w_out, 512 * g, 512)[[2, 3, 0, 1]]
    g = 0
    for half in range(2):
        for r in range(GROUPS[half]):
            cols = np.concatenate([w_up[:, 256 * g:256 * g + 256], w_up[:, D_FF + 256 * g:D_FF + 256 * g + 256]], 1)
            out[B_UP[half] + 4 * r:B_UP[half] + 4 * r + 4] = _pack(cols, 0, 512)
            g += 1
        rows = w_down[256 * sum(GROUPS[:half]):256 * sum(GROUPS[:half + 1])]
        for hf in range(2):
            n = GROUPS[half]
            out[B_DN[half] + n * hf:B_DN[half] + n * (hf + 1)] = _pack(rows, 512 * hf, 512)
    return out


def _columns(v):
    return v.reshape(-1, P).T


def kernel(**inputs):
    import concourse.bacc as bacc
    from concourse.bass_utils import run_bass_kernel_spmd

    a = {k: np.asarray(v) for k, v in inputs.items()}
    blocks = np.concatenate([
        _weight_blocks(*(a[n][l] for n in ("w_in", "w_uq", "w_ukv", "sg_w_s", "w_out", "w_mkv", "w_mq", "w_mo",
                                           "w_up", "w_down"))) for l in range(DEPTH)])
    par = np.stack([np.concatenate(
        [_columns(a[n][l]) for n in ("norm_mix_g", "q_norm_g", "kv_norm_g", "out_norm_mla_g", "out_norm_sg_g",
                                     "mem_norm_g", "norm_mem_g", "norm_ffn_g")]
        + [a["sg_b_s"][l].T] + [_columns(a["conv_w"][l, k]) for k in range(3)] + [_columns(a["conv_b"][l])], 1)
        for l in range(DEPTH)])
    half = ROPE // 2
    inv = np.float32(10000.0) ** (-np.arange(half, dtype=np.float32) / np.float32(half))
    freq = np.zeros((P, 4), np.float32)
    freq[64:, 0] = np.tile(inv, 4)
    freq[64:80, 1], freq[80:96, 1] = -1.0, 1.0
    freq[96:, 2], freq[96:, 3] = 0.25, np.pi / 2
    arrays = {
        "blocks": blocks,
        "xT": np.ascontiguousarray(a["x"][0].T.reshape(KD, P, SEQ).transpose(1, 0, 2)),
        "memT": np.ascontiguousarray(a["mem"][0].T.reshape(KD, P, N_MEM).transpose(1, 0, 2)),
        "pos": np.ascontiguousarray(a["positions"]),
        "par": np.ascontiguousarray(par),
        "ln": np.ascontiguousarray(np.concatenate([a["sg_ln_g"], a["sg_ln_b"]], 1)),
        "fin": np.ascontiguousarray(_columns(a["final_norm_g"])),
        "freq": freq,
    }
    nc = bacc.Bacc("TRN2", target_bir_lowering=False, num_devices=1)
    args = [nc.dram_tensor(f"{n}_d", v.shape, mybir.dt.from_np(v.dtype), kind="ExternalInput").ap()
            for n, v in arrays.items()]
    out = nc.dram_tensor("outT_d", (P, KD, SEQ), F32, kind="ExternalOutput").ap()
    encoder_program(nc, *args, out)
    r = run_bass_kernel_spmd(nc, [{f"{n}_d": v for n, v in arrays.items()}], core_ids=[0])
    outT = r.results[0]["outT_d"]
    return np.ascontiguousarray(outT.transpose(1, 0, 2).reshape(D, SEQ).T)[None]
```
